# Optimizing a Trainium2 kernel written in Bass

```python
import math
import jax, jax.numpy as jnp
from jax import lax
import numpy as np

D_MODEL = 1024
BATCH = 1
SEQ = 1024
DEPTH = 2

PLE_DIM = 256
N_HEADS_DIFF = 4
DIFF_HEAD_DIM = 128
DIFF_HALF = DIFF_HEAD_DIM // 2
N_HEADS_FOX = 4
FOX_HEAD_DIM = 128
DIFF_W = N_HEADS_DIFF * DIFF_HEAD_DIM
FOX_W = N_HEADS_FOX * FOX_HEAD_DIM
MIX_W_EVEN = DIFF_W + FOX_W
EVEN_IN = 3 * DIFF_W + 3 * FOX_W + N_HEADS_FOX
Q_BLOCK = 128
GLA_HEADS = 4
GLA_DK = (D_MODEL // 2) // GLA_HEADS
GLA_DV = D_MODEL // GLA_HEADS
GLA_LOWRANK = 16
GLA_GATE_NORM = 16.0
GLA_CHUNK = 64
MIX_W_ODD = GLA_HEADS * GLA_DV
ODD_IN = 2 * GLA_HEADS * GLA_DK + 2 * GLA_HEADS * GLA_DV + GLA_LOWRANK
D_FF = 4 * D_MODEL
EPS = 1e-6
N_EVEN = (DEPTH + 1) // 2
N_ODD = DEPTH // 2

kernel_name = "hybrid_diff_fox_gla_trunk"

def rmsnorm(x, g):
    xf = x.astype(jnp.float32)
    y = xf * lax.rsqrt(jnp.mean(xf * xf, axis=-1, keepdims=True) + EPS)
    return (y * g.astype(jnp.float32)).astype(x.dtype)

def split_heads(t, n_heads):
    b, s, _ = t.shape
    return t.reshape(b, s, n_heads, -1).transpose(0, 2, 1, 3)

def merge_heads(t):
    b, h, s, d = t.shape
    return t.transpose(0, 2, 1, 3).reshape(b, s, h * d)

def split_cols(t, sizes):
    idx = [int(v) for v in np.cumsum(sizes)[:-1]]
    return jnp.split(t, idx, axis=-1)

def diff_attention(q, k, v, lam):
    b, h, s, _ = q.shape
    scale = DIFF_HALF ** -0.5
    q1, q2 = q[..., :DIFF_HALF] * scale, q[..., DIFF_HALF:] * scale
    k1, k2 = k[..., :DIFF_HALF], k[..., DIFF_HALF:]
    kpos = jnp.arange(s)

    def block(start):
        qb1 = lax.dynamic_slice_in_dim(q1, start, Q_BLOCK, axis=2)
        qb2 = lax.dynamic_slice_in_dim(q2, start, Q_BLOCK, axis=2)
        qpos = start + jnp.arange(Q_BLOCK)
        mask = kpos[None, :] <= qpos[:, None]
        s1 = jnp.einsum('bhqd,bhkd->bhqk', qb1, k1).astype(jnp.float32)
        s2 = jnp.einsum('bhqd,bhkd->bhqk', qb2, k2).astype(jnp.float32)
        a1 = jax.nn.softmax(jnp.where(mask, s1, -jnp.inf), axis=-1)
        a2 = jax.nn.softmax(jnp.where(mask, s2, -jnp.inf), axis=-1)
        w = (a1 - lam * a2).astype(v.dtype)
        return jnp.einsum('bhqk,bhkd->bhqd', w, v)

    out = lax.map(block, jnp.arange(s // Q_BLOCK) * Q_BLOCK)
    return out.transpose(1, 2, 0, 3, 4).reshape(b, h, s, -1)

def forgetting_attention(q, k, v, log_f):
    b, h, s, d = q.shape
    scale = d ** -0.5
    c = jnp.cumsum(log_f, axis=-1)
    kpos = jnp.arange(s)

    def block(start):
        qb = lax.dynamic_slice_in_dim(q, start, Q_BLOCK, axis=2)
        cb = lax.dynamic_slice_in_dim(c, start, Q_BLOCK, axis=2)
        qpos = start + jnp.arange(Q_BLOCK)
        mask = kpos[None, :] <= qpos[:, None]
        sc = jnp.einsum('bhqd,bhkd->bhqk', qb, k).astype(jnp.float32) * scale
        sc = sc + cb[..., :, None] - c[..., None, :]
        a = jax.nn.softmax(jnp.where(mask, sc, -jnp.inf), axis=-1)
        return jnp.einsum('bhqk,bhkd->bhqd', a.astype(v.dtype), v)

    out = lax.map(block, jnp.arange(s // Q_BLOCK) * Q_BLOCK)
    return out.transpose(1, 2, 0, 3, 4).reshape(b, h, s, d)

def gla_chunked(q, k, v, gk):
    b, h, s, dk = q.shape
    dv = v.shape[-1]
    L = GLA_CHUNK
    n = s // L

    def chunks(t):
        return t.reshape(b, h, n, L, t.shape[-1]).transpose(2, 0, 1, 3, 4)

    causal = jnp.arange(L)[:, None] >= jnp.arange(L)[None, :]

    def step(state, inp):
        qc, kc, vc, gc = inp
        bcum = jnp.cumsum(gc, axis=-2)
        o_inter = jnp.einsum('bhld,bhde->bhle', qc * jnp.exp(bcum), state)
        rel = bcum[:, :, :, None, :] - bcum[:, :, None, :, :]
        decay = jnp.exp(jnp.where(causal[:, :, None], rel, -jnp.inf))
        scores = jnp.einsum('bhid,bhjd,bhijd->bhij', qc, kc, decay)
        o_intra = jnp.einsum('bhij,bhjd->bhid', scores, vc)
        b_last = bcum[:, :, -1:, :]
        state = (jnp.exp(b_last[:, :, 0, :])[..., None] * state
                 + jnp.einsum('bhld,bhle->bhde', kc * jnp.exp(b_last - bcum), vc))
        return state, o_inter + o_intra

    s0 = jnp.zeros((b, h, dk, dv), jnp.float32)
    _, o = lax.scan(step, s0, (chunks(q), chunks(k), chunks(v), chunks(gk)))
    return o.transpose(1, 2, 0, 3, 4).reshape(b, h, s, dv)

def even_mixer(hn, w_in, b_f, lam_q1, lam_k1, lam_q2, lam_k2, g_sub, w_o, layer_idx):
    proj = hn @ w_in
    qa, ka, va, qb, kb, vb, fl = split_cols(
        proj, [DIFF_W, DIFF_W, DIFF_W, FOX_W, FOX_W, FOX_W, N_HEADS_FOX])
    lam_init = 0.8 - 0.6 * math.exp(-0.3 * layer_idx)
    f32 = jnp.float32
    lam = (jnp.exp(jnp.sum(lam_q1.astype(f32) * lam_k1.astype(f32)))
           - jnp.exp(jnp.sum(lam_q2.astype(f32) * lam_k2.astype(f32))) + lam_init)
    oa = diff_attention(split_heads(qa, N_HEADS_DIFF), split_heads(ka, N_HEADS_DIFF),
                        split_heads(va, N_HEADS_DIFF), lam)
    oa = rmsnorm(oa, g_sub) * (1.0 - lam_init)
    log_f = jax.nn.log_sigmoid((fl + b_f).astype(f32)).transpose(0, 2, 1)
    ob = forgetting_attention(split_heads(qb, N_HEADS_FOX), split_heads(kb, N_HEADS_FOX),
                              split_heads(vb, N_HEADS_FOX), log_f)
    o = jnp.concatenate([merge_heads(oa), merge_heads(ob).astype(oa.dtype)], axis=-1)
    return o @ w_o

def odd_mixer(hn, w_in, w_gk, b_gk, g_onorm, w_o):
    proj = hn @ w_in
    q, k, v, g, gl = split_cols(
        proj, [GLA_HEADS * GLA_DK, GLA_HEADS * GLA_DK, GLA_HEADS * GLA_DV,
               GLA_HEADS * GLA_DV, GLA_LOWRANK])
    f32 = jnp.float32
    gk = jax.nn.log_sigmoid((gl @ w_gk + b_gk).astype(f32)) / GLA_GATE_NORM
    o = gla_chunked(split_heads(q.astype(f32), GLA_HEADS) * (GLA_DK ** -0.5),
                    split_heads(k.astype(f32), GLA_HEADS),
                    split_heads(v.astype(f32), GLA_HEADS),
                    split_heads(gk, GLA_HEADS))
    o = rmsnorm(o, g_onorm).astype(hn.dtype)
    o = merge_heads(o) * jax.nn.silu(g)
    return o @ w_o

def mlp_sq_relu(hn, w_up, w_down):
    return jnp.square(jax.nn.relu(hn @ w_up)) @ w_down

def setup_inputs(seed: int = 0) -> dict:
    key = jax.random.key(seed)
    ks = jax.random.split(key, 32)

    def nrm(k, shape, scale):
        return jax.random.normal(k, shape, jnp.float32) * scale

    def gain(k, shape):
        return 1.0 + 0.02 * jax.random.normal(k, shape, jnp.float32)

    return {
        "x": nrm(ks[0], (BATCH, SEQ, D_MODEL), 1.0),
        "p": nrm(ks[1], (DEPTH, BATCH, SEQ, PLE_DIM), 1.0),
        "norm_mix": gain(ks[2], (DEPTH, D_MODEL)),
        "norm_mlp": gain(ks[3], (DEPTH, D_MODEL)),
        "norm_ple": gain(ks[4], (DEPTH, D_MODEL)),
        "norm_final": gain(ks[5], (D_MODEL,)),
        "even_w_in": nrm(ks[6], (N_EVEN, D_MODEL, EVEN_IN), D_MODEL ** -0.5),
        "even_b_f": jax.random.uniform(ks[7], (N_EVEN, N_HEADS_FOX), jnp.float32, 1.0, 4.0),
        "lam_q1": nrm(ks[8], (N_EVEN, DIFF_HALF), 0.1),
        "lam_k1": nrm(ks[9], (N_EVEN, DIFF_HALF), 0.1),
        "lam_q2": nrm(ks[10], (N_EVEN, DIFF_HALF), 0.1),
        "lam_k2": nrm(ks[11], (N_EVEN, DIFF_HALF), 0.1),
        "diff_subln": gain(ks[12], (N_EVEN, DIFF_HEAD_DIM)),
        "even_w_o": nrm(ks[13], (N_EVEN, MIX_W_EVEN, D_MODEL), MIX_W_EVEN ** -0.5),
        "odd_w_in": nrm(ks[14], (N_ODD, D_MODEL, ODD_IN), D_MODEL ** -0.5),
        "odd_w_gk": nrm(ks[15], (N_ODD, GLA_LOWRANK, GLA_HEADS * GLA_DK), GLA_LOWRANK ** -0.5),
        "odd_b_gk": nrm(ks[16], (N_ODD, GLA_HEADS * GLA_DK), 0.1),
        "gla_onorm": gain(ks[17], (N_ODD, GLA_DV)),
        "odd_w_o": nrm(ks[18], (N_ODD, MIX_W_ODD, D_MODEL), MIX_W_ODD ** -0.5),
        "w_up": nrm(ks[19], (DEPTH, D_MODEL, D_FF), D_MODEL ** -0.5),
        "w_down": nrm(ks[20], (DEPTH, D_FF, D_MODEL), D_FF ** -0.5),
        "w_ple_gate": nrm(ks[21], (DEPTH, D_MODEL, D_MODEL), D_MODEL ** -0.5),
        "w_ple_proj": nrm(ks[22], (DEPTH, PLE_DIM, D_MODEL), PLE_DIM ** -0.5),
    }

def reference(x, p, norm_mix, norm_mlp, norm_ple, norm_final,
              even_w_in, even_b_f, lam_q1, lam_k1, lam_q2, lam_k2, diff_subln, even_w_o,
              odd_w_in, odd_w_gk, odd_b_gk, gla_onorm, odd_w_o,
              w_up, w_down, w_ple_gate, w_ple_proj):
    h = x
    for i in range(DEPTH):
        j = i // 2
        hn = rmsnorm(h, norm_mix[i])
        if i % 2 == 0:
            h = h + even_mixer(hn, even_w_in[j], even_b_f[j], lam_q1[j], lam_k1[j],
                               lam_q2[j], lam_k2[j], diff_subln[j], even_w_o[j], i)
        else:
            h = h + odd_mixer(hn, odd_w_in[j], odd_w_gk[j], odd_b_gk[j],
                              gla_onorm[j], odd_w_o[j])
        h = h + mlp_sq_relu(rmsnorm(h, norm_mlp[i]), w_up[i], w_down[i])
        gate = jax.nn.sigmoid(rmsnorm(h, norm_ple[i]) @ w_ple_gate[i])
        h = h + gate * (p[i] @ w_ple_proj[i])
    return rmsnorm(h, norm_final)


_drawn_inputs = setup_inputs


def setup_inputs(seed=0):
    import zlib

    import numpy as np

    out = dict(_drawn_inputs(seed))
    spreads = {}
    factors = {'norm_ple': 49.634,
     'norm_final': 7.282,
     'lam_k1': 8.0,
     'lam_q2': 8.0,
     'diff_subln': 5.114,
     'odd_b_gk': 3.101,
     'gla_onorm': 30.901,
     'norm_mlp': 2.786}
    for name, (base, spread) in spreads.items():
        noise = np.random.default_rng([zlib.crc32(name.encode()), seed]).standard_normal(out[name].shape)
        drawn = base * np.exp(spread * noise) if base else spread * noise
        out[name] = __import__('jax').numpy.asarray(drawn.astype(out[name].dtype))
    for name, factor in factors.items():
        out[name] = (out[name] * factor).astype(out[name].dtype)
    return out
```

```python
from contextlib import ExitStack

import concourse.bass as bass
from concourse import mybir
from concourse.alu_op_type import AluOpType as ALU

F32 = mybir.dt.float32
F32R = mybir.dt.float32r
I32 = mybir.dt.int32
ACT = mybir.ActivationFunctionType
AX = mybir.AxisListType.X
ds = bass.ds

P = 128
D = 1024
SEQ = 1024
KT = D // P
HALF = SEQ // 2
NQT = SEQ // P
FF = 4 * D
CHUNKS = FF // D
PLE = 256
HEADS = 8
DIFF_HEADS = 4
GLA_HEADS = 4
DK = 128
DV = 256
LOWRANK = 16
LEVELS = 7
EPS = 1e-6
SIG_MIX1 = 2 * KT
SIG_GATE1 = SIG_MIX1 + 4 * GLA_HEADS
LAM_INIT = 0.8 - 0.6 * 1.0
MASKED = -1.0e30

PANELS_MIX = 1 + 3 * HEADS
PANELS_MLP = 2 * KT * CHUNKS
PANELS_LAYER = PANELS_MIX + KT + PANELS_MLP + 4 + KT
PANELS = 2 * PANELS_LAYER
UNITS = 2 * KT
GROUPS = [1 if i < 4 else 2 for i in range(NQT)]
GROUPS_HEAD = sum(GROUPS)


class Idx:

    def __init__(self, c, terms=()):
        self.c, self.terms = c, tuple(terms)

    def __add__(self, n):
        if isinstance(n, Idx):
            return Idx(self.c + n.c, self.terms + n.terms)
        return Idx(self.c + n, self.terms)

    def times(self, m):
        return Idx(self.c * m, [(k * m, r) for k, r in self.terms])

    def half(self):
        return Idx(self.c // 2, [(k // 2, r) for k, r in self.terms])

    @property
    def parity(self):
        assert all(k % 2 == 0 for k, _ in self.terms)
        return self.c % 2

    def at(self, add=0):
        v = self.c + add
        for k, r in self.terms:
            v = r * k + v
        return v

    def cols(self, n, scale=None, add=0):
        s = self.times(n if scale is None else scale)
        return ds(s.at(add), n)


class Chain:

    def __init__(self, eng, sem):
        self.eng, self.sem, self.base, self.n = eng, sem, Idx(0), 0

    def link(self, ins):
        self.n += 1
        ins.then_inc(self.sem, 1)
        self.eng.wait_ge(self.sem, self.base.at(self.n))

    def enter(self, reg, steps):
        self.saved = (self.base, self.n)
        self.base, self.n = self.base + Idx(self.n, [(steps, reg)]), 0

    def leave(self, iterations, steps):
        assert self.n == steps, (self.n, steps)
        base, n = self.saved
        self.base, self.n = base, n + iterations * steps


def plan_layer(layer):
    p0 = layer * PANELS_LAYER
    x0 = layer * 128
    s = dict(mix=p0, heads=p0 + 1, wo=p0 + PANELS_MIX)
    s["mlp"] = s["wo"] + KT
    s["ple"] = s["mlp"] + PANELS_MLP
    s["gate"] = s["ple"] + 4
    s["x_mix"] = x0
    s["x_o"] = x0 + 16
    s["x_mlp"] = x0 + 32
    s["x_hid"] = x0 + 48
    s["x_ple"] = x0 + 48 + 16 * CHUNKS
    s["norm"] = 3 * layer
    assert s["x_ple"] + 16 == x0 + 128 and s["heads"] % 2 == s["wo"] % 2
    return s


PLAN = [plan_layer(0), plan_layer(1)]


def build_trunk(nc, x_t, p_t, panels, gains, b_f, lam_vec, g_sub, w_gk, b_gk, g_on, out_t):
    h_dram = nc.dram_tensor("h_spill", [KT, P, SEQ], F32, kind="Internal").ap()
    ctx = ExitStack()
    with ctx:
        def overlay(*groups):
            made = {}
            for group in groups[1:]:
                with ExitStack() as inner:
                    for name, shape, dt in group:
                        made[name] = inner.enter_context(nc.sbuf_tensor(name, shape, dt))
            for name, shape, dt in groups[0]:
                made[name] = ctx.enter_context(nc.sbuf_tensor(name, shape, dt))
            return made

        def sb(name, shape, dt=F32):
            return ctx.enter_context(nc.sbuf_tensor(name, shape, dt))

        def sem(name):
            return ctx.enter_context(nc.semaphore(name))

        m = overlay(
            [("a_hi", [P, KT, SEQ], F32R), ("a_lo", [P, KT, SEQ], F32R)],
            [("p_raw", [P, 2, SEQ], F32), ("p_skip", [P, 6, SEQ], F32), ("pp", [P, KT, SEQ], F32)],
        )
        a_hi, a_lo, p_raw, pp = m["a_hi"], m["a_lo"], m["p_raw"], m["pp"]
        m = overlay(
            [("b_hi", [P, KT, SEQ], F32R), ("b_lo", [P, KT, SEQ], F32R)],
            [("o_raw", [P, KT, SEQ], F32),
             ("pt_hi", [P, NQT, 256], F32R), ("pt_lo", [P, NQT, 256], F32R),
             ("v_t", [P, SEQ], F32), ("c_row", [P, SEQ], F32),
             ("cm_hi", [P, SEQ], F32R), ("cm_lo", [P, SEQ], F32R)],
            [("o_raw1", [P, KT, SEQ], F32),
             ("dec", [P, SEQ], F32), ("lev", [P, SEQ], F32), ("att", [P, SEQ], F32),
             ("q_dec", [P, SEQ], F32), ("k_dec", [P, SEQ], F32), ("k_tok", [P, SEQ], F32),
             ("gl_t", [P, SEQ], F32), ("resets", [P, SEQ], F32)],
        )
        b_hi, b_lo, o_raw, pt_hi, pt_lo = m["b_hi"], m["b_lo"], m["o_raw"], m["pt_hi"], m["pt_lo"]
        v_t, c_row, cm_hi, cm_lo = m["v_t"], m["c_row"], m["cm_hi"], m["cm_lo"]
        o_raw1, dec, lev, att = m["o_raw1"], m["dec"], m["lev"], m["att"]
        q_dec, k_dec, k_tok, gl_t, resets = m["q_dec"], m["k_dec"], m["k_tok"], m["gl_t"], m["resets"]
        m = overlay(
            [("h", [P, KT, SEQ], F32)],
            [("q_hi", [P, SEQ], F32R), ("q_lo", [P, SEQ], F32R), ("k_hi", [P, SEQ], F32R),
             ("k_lo", [P, SEQ], F32R), ("v_hi", [P, NQT, P], F32R), ("v_lo", [P, NQT, P], F32R),
             ("prob", [P, 2, SEQ], F32)],
            [("q_t", [P, SEQ], F32), ("k_t", [P, SEQ], F32), ("vg_t", [P, 2, SEQ], F32),
             ("v_tok", [P, NQT, DV], F32), ("b_cum", [P, SEQ], F32), ("lmask", [P, 8, P], F32)],
        )
        h, prob = m["h"], m["prob"]
        q_hi, q_lo, k_hi, k_lo, v_hi, v_lo = (m[n] for n in ("q_hi", "q_lo", "k_hi", "k_lo", "v_hi", "v_lo"))
        q_t, k_t, vg_t, v_tok, b_cum, lmask = (m[n] for n in ("q_t", "k_t", "vg_t", "v_tok", "b_cum", "lmask"))

        wraw = sb("wraw", [P, 2, KT, P])
        whi = sb("whi", [P, 2, KT, P], F32R)
        wlo = sb("wlo", [P, 2, KT, P], F32R)
        rstd = sb("rstd", [P, SEQ])
        sumsq = sb("sumsq", [P, 2, HALF])
        zt = sb("zt", [P, 2, HALF])
        zs = sb("zs", [P, 2, HALF])
        ones = sb("ones", [P, P])
        ident = sb("ident", [P, P])
        ident_r = sb("ident_r", [P, P], F32R)
        mask_f = zt[:, 0, 0:P]
        mask_r = sb("mask_r", [P, P], F32R)
        negones_r = sb("negones_r", [DIFF_HEADS, P], F32R)
        gcol = sb("gcol", [P, 7 * KT])
        colc = sb("colc", [P, 64])
        state = sb("state", [P, 2, DV])
        wgk_all = sb("wgk_all", [LOWRANK, GLA_HEADS * DK])
        wgk_h = zs[0:LOWRANK, 0, 0:DK]
        lam_in = zs[:, 1, 0:256]

        QS = 0
        ONE = 8
        GSUB, BF, BGK, GON = 9, 10, 11, 15
        LAM1, LAM2, NEGLAM = 17, 18, 19
        NEG, L, RL = 20, 24, 28
        C2 = 32
        EB = 40
        MARK = 50

        gemm_ps = ctx.enter_context(nc.psum_tensor("gemm_ps", [P, 2, HALF], F32))
        s_ps = ctx.enter_context(nc.psum_tensor("s_ps", [P, 2, SEQ], F32))
        to_ps = ctx.enter_context(nc.psum_tensor("to_ps", [P, SEQ], F32))

        w_loaded = [sem("w_loaded0"), sem("w_loaded1")]
        w_hi_ready, w_lo_ready = sem("w_hi_ready"), sem("w_lo_ready")
        unit_ready, unit_free = sem("unit_ready"), sem("unit_free")
        x_hi_ready, x_lo_ready = sem("x_hi_ready"), sem("x_lo_ready")
        sq_ready, sq_added = sem("sq_ready"), sem("sq_added")
        norm_sum, norm_ms, norm_root = sem("norm_sum"), sem("norm_ms"), sem("norm_root")
        x_loaded, const_loaded, const_ready = sem("x_loaded"), sem("const_loaded"), sem("const_ready")
        gp_const, lam_exp, ph_ready = sem("gp_const"), sem("lam_exp"), sem("ph_ready")
        v_step, a_step, g_step = sem("v_step"), sem("a_step"), sem("g_step")
        qk_hi_ready, qk_lo_ready = sem("qk_hi_ready"), sem("qk_lo_ready")
        vt_ready, v_hi_ready, v_lo_ready = sem("vt_ready"), sem("v_hi_ready"), sem("v_lo_ready")
        scores_ready, negmax_ready, exp_ready, w_ready = (sem("scores_ready"), sem("negmax_ready"),
                                                          sem("exp_ready"), sem("weights_ready"))
        tr_ready, tr_hi, tr_lo = sem("tr_ready"), sem("tr_hi"), sem("tr_lo")
        pv_ready, o_evacuated = sem("pv_ready"), sem("o_evacuated")
        sub_sq, sub_sum, sub_ms, sub_root, sub_done = (sem("sub_sq"), sem("sub_sum"), sem("sub_ms"),
                                                       sem("sub_root"), sem("sub_done"))
        fl_ready, fl_log = sem("fl_ready"), sem("fl_log")
        cm_hi_ready, cm_lo_ready = sem("cm_hi_ready"), sem("cm_lo_ready")
        h_loaded = [sem("h_loaded0"), sem("h_loaded1")]
        h_spilled, p_loaded, out_stored = sem("h_spilled"), sem("p_loaded"), sem("out_stored")
        p_hi_ready, p_lo_ready = sem("p_hi_ready"), sem("p_lo_ready")
        sig_ready, h_ready, final_ready, o_gated = sem("sig_ready"), sem("h_ready"), sem("final_ready"), sem("o_gated")
        gk_w, gk_sum, gk_in, gk_log = sem("gk_w"), sem("gk_sum"), sem("gk_in"), sem("gk_log")
        vtok_sum, vtok_ready = sem("vtok_sum"), sem("vtok_ready")
        dec_in, dec_exp, lev_ready, lev_sum, lev_done = (sem("dec_in"), sem("dec_exp"), sem("lev_ready"),
                                                         sem("lev_sum"), sem("lev_done"))
        ktok_in, ktok_sum, ktok_ready = sem("ktok_in"), sem("ktok_sum"), sem("ktok_ready")
        gla_o, gla_o_free, st_sum, st_ready = sem("gla_o"), sem("gla_o_free"), sem("st_sum"), sem("st_ready")
        on_sq, on_sum, on_ms, on_root = sem("on_sq"), sem("on_sum"), sem("on_ms"), sem("on_root")

        block = ctx.enter_context(nc.Block())

        def state_c(c):
            return state[:, c % 2]

        def half_cols(half):
            return slice(half * HALF, (half + 1) * HALF)

        @block.sync
        def _(sp):
            def load_panel(p):
                if not (isinstance(p.at(), int) and p.at() < 2):
                    sp.wait_ge(w_lo_ready, p.at(-1))
                sp.dma_start(wraw[:, p.parity].rearrange("p k m -> p (k m)"),
                             panels[p.cols(1)].rearrange("a p n -> p (a n)")).then_inc(w_loaded[p.parity], 16)

            def load_panels(first, count):
                if count % 2:
                    load_panel(Idx(first))
                    first, count = first + 1, count - 1
                with sp.Fori(0, count // 2) as i:
                    for s in range(2):
                        load_panel(Idx(first + s, [(2, i)]))

            for layer, st in enumerate(PLAN):
                if layer == 0:
                    load_panel(Idx(0))
                    load_panel(Idx(1))
                    load_panels(2, PANELS_MIX - 2)
                else:
                    load_panels(st["mix"], PANELS_MIX)
                def wo_and_residual(o, first):
                    for s in range(2):
                        load_panel(o + (st["wo"] + s))
                    if first:
                        sp.wait_ge(x_lo_ready, st["x_o"] + 16)
                        if layer == 1:
                            sp.wait_ge(h_spilled, 16 * KT)
                    src = x_t if layer == 0 else h_dram
                    for s in range(2):
                        if not (first and layer == 0):
                            sp.wait_ge(h_loaded[s], (o.half() + 4 * layer).times(16).at())
                        sp.dma_start(h[:, (o + s).cols(1)].rearrange("p a n -> p (a n)"),
                                     src[(o + s).cols(1)].rearrange("a p n -> p (a n)")).then_inc(h_loaded[s], 16)

                wo_and_residual(Idx(0), True)
                with sp.Fori(1, KT // 2) as i:
                    wo_and_residual(Idx(0, [(2, i)]), False)
                load_panels(st["mlp"], PANELS_MLP + 4 + KT)
            for o in range(KT):
                sp.wait_ge(final_ready, o + 1)
                sp.dma_start(out_t[o], h[:, o]).then_inc(out_stored, 16)
            sp.wait_ge(out_stored, 16 * KT)

        @block.tensor
        def _(pe):
            def product(out, hi_w, lo_w, hi_x, lo_x, start, stop):
                nc.tensor.matmul(out, hi_w, hi_x, start=start, stop=False, skip_group_check=True)
                nc.tensor.matmul(out, hi_w, lo_x, start=False, stop=False, skip_group_check=True)
                return nc.tensor.matmul(out, lo_w, hi_x, start=False, stop=stop, skip_group_check=True)

            def norm_sums(n):
                pe.wait_ge(sq_added, 16 * (n + 1))
                for half in range(2):
                    nc.tensor.matmul(s_ps[:, 0, half_cols(half)], ones[:], sumsq[:, half], start=True,
                                     stop=True).then_inc(norm_sum, 1)

            def panel(p, hi, lo, x_base=None, norm=None):
                s = p.parity
                pe.wait_ge(w_lo_ready, p.at(1))
                for half in range(2):
                    u = p.times(2) + half
                    if not (isinstance(u.at(), int) and u.at() < 2):
                        pe.wait_ge(unit_free, u.at(-1))
                    for k in range(KT):
                        if x_base is not None:
                            pe.wait_ge(x_lo_ready, x_base.at(2 * k + half + 1))
                        last = product(gemm_ps[:, half], whi[:, s, k], wlo[:, s, k],
                                       hi[:, k, half_cols(half)], lo[:, k, half_cols(half)], k == 0, k == KT - 1)
                    last.then_inc(unit_ready, 1)
                    if norm is not None and half == 0:
                        norm_sums(norm)

            def stage(p, count, hi, lo, x_base=None, norm=None):
                if x_base is not None:
                    for s in range(2):
                        panel(p + s, hi, lo, x_base if s == 0 else None, norm if s == 0 else None)
                    p, count = p + 2, count - 2
                with pe.Fori(0, count // 2) as i:
                    for s in range(2):
                        panel(p + Idx(s, [(2, i)]), hi, lo)

            def attention(hd, diff):
                maps = 2 if diff else 1
                pe.wait_ge(unit_free, hd.times(6).at(2 * 1 + 6))
                for t in range(NQT):
                    last = nc.tensor.transpose(to_ps[:, t * P:(t + 1) * P], v_t[:, t * P:(t + 1) * P], ident[:])
                last.then_inc(vt_ready, 1)

                def scores(i):
                    keys = (i + 1) * P
                    for mp in range(maps):
                        r = slice(64 * mp, 64 * mp + 64) if diff else slice(0, P)
                        for c0 in range(0, keys, HALF):
                            c1 = min(keys, c0 + HALF)
                            out = s_ps[:, mp, c0:c1]
                            last = product(out, q_hi[r, i * P:(i + 1) * P], q_lo[r, i * P:(i + 1) * P],
                                           k_hi[r, c0:c1], k_lo[r, c0:c1], True, False)
                            if not diff:
                                for cm in (cm_hi, cm_lo):
                                    last = nc.tensor.matmul(out, negones_r[:], cm[0:DIFF_HEADS, c0:c1], start=False,
                                                            stop=False, skip_group_check=True)
                            if c1 == keys:
                                last = nc.tensor.matmul(s_ps[:, mp, i * P:keys], ident_r[:], mask_r[:], start=False,
                                                        stop=True, skip_group_check=True)
                    last.then_inc(scores_ready, 1)

                def transposes(i, done):
                    pe.wait_ge(w_ready, hd.times(NQT).at(i + 1))
                    for g in range(GROUPS[i]):
                        if i == 0:
                            pe.wait_ge(v_lo_ready, hd.at(1))
                        else:
                            pe.wait_ge(tr_lo, hd.times(GROUPS_HEAD).at(done + g))
                        for j in range(4 * g, min(4 * g + 4, i + 1)):
                            last = nc.tensor.transpose(to_ps[:, (j - 4 * g) * P:(j - 4 * g + 1) * P],
                                                       prob[:, 0, j * P:(j + 1) * P], ident[:])
                        last.then_inc(tr_ready, 1)

                def values(c):
                    pe.wait_ge(tr_lo, hd.times(GROUPS_HEAD).at(sum(GROUPS[:2 * c + 2])))
                    pe.wait_ge(o_evacuated, hd.times(4).at(c + 1))
                    for j in range(2 * c + 2):
                        q0 = P if j == 2 * c + 1 else 0
                        last = product(to_ps[:, HALF + q0:HALF + 256], v_hi[:, j], v_lo[:, j],
                                       pt_hi[:, j, q0:256], pt_lo[:, j, q0:256], j == 0, j == 2 * c + 1)
                    last.then_inc(pv_ready, 1)

                pe.wait_ge(qk_lo_ready, hd.times(4).at(4))
                if diff:
                    pe.wait_ge(sub_done, hd.at(1))
                else:
                    pe.wait_ge(sub_done, DIFF_HEADS + 1)
                    pe.wait_ge(cm_lo_ready, hd.at(1 - DIFF_HEADS))
                scores(0)
                for i in range(NQT):
                    if i + 1 < NQT:
                        pe.wait_ge(exp_ready, hd.times(NQT).at(i + 1))
                        scores(i + 1)
                    if i >= 2 and i % 2 == 0:
                        values(i // 2 - 1)
                    transposes(i, sum(GROUPS[:i]))
                values(3)
                if diff:
                    pe.wait_ge(sub_sq, hd.at(1))
                    for half in range(2):
                        last = nc.tensor.matmul(s_ps[:, 0, half_cols(half)], ones[:], prob[:, 0, half_cols(half)],
                                                start=True, stop=True)
                    last.then_inc(sub_sum, 1)

            def gla_head(hd):
                p = hd.times(6) + PLAN[1]["heads"]
                for j in range(4):
                    panel(p + j, a_hi, a_lo)
                pe.wait_ge(gk_w, hd.at(1))
                for half in range(2):
                    last = nc.tensor.matmul(to_ps[:, half_cols(half)], wgk_h, gl_t[0:LOWRANK, half_cols(half)],
                                            start=True, stop=True)
                last.then_inc(gk_sum, 1)
                pe.wait_ge(unit_free, p.times(2).at(8))
                for t in range(2):
                    for c in range(NQT):
                        last = nc.tensor.transpose(s_ps[:, t, c * P:(c + 1) * P], vg_t[:, t, c * P:(c + 1) * P], ident[:])
                last.then_inc(vtok_sum, 1)
                pe.wait_ge(vtok_ready, hd.at(1))
                for lv in range(LEVELS + 1):
                    n = hd.times(LEVELS + 1)
                    if lv < LEVELS:
                        pe.wait_ge(lev_ready, hd.times(LEVELS).at(lv + 1))
                    if lv >= 2:
                        pe.wait_ge(lev_done, n.at(lv - 1))
                    for c in range(NQT):
                        cs = slice(c * P, (c + 1) * P)
                        kk, qq = (lev, lev) if lv < LEVELS else (k_t, q_t)
                        last = nc.tensor.matmul(s_ps[:, lv % 2, cs], kk[:, cs], qq[:, cs], start=True, stop=True)
                    last.then_inc(lev_sum, 1)
                pe.wait_ge(ktok_in, hd.at(1))
                for c in range(NQT):
                    cs = slice(c * P, (c + 1) * P)
                    last = nc.tensor.transpose(to_ps[:, cs], k_dec[:, cs], ident[:])
                last.then_inc(ktok_sum, 1)
                pe.wait_ge(ktok_ready, hd.at(1))
                pe.wait_ge(lev_done, hd.times(LEVELS + 1).at(LEVELS + 1))
                for c in range(NQT):
                    cs = slice(c * P, (c + 1) * P)
                    if c >= 1:
                        pe.wait_ge(st_ready, hd.times(NQT - 1).at(c))
                    if c < NQT - 1:
                        nc.tensor.matmul(to_ps[:, 0:DV], k_tok[:, cs], v_tok[:, c], start=True,
                                         stop=True).then_inc(st_sum, 1)
                    if c >= 2:
                        pe.wait_ge(gla_o_free, hd.times(NQT).at(c - 1))
                    for t in range(2):
                        out = s_ps[:, c % 2, t * P:(t + 1) * P]
                        last = nc.tensor.matmul(out, v_tok[:, c, t * P:(t + 1) * P], att[:, cs], start=True,
                                                stop=(c == 0))
                        if c >= 1:
                            last = nc.tensor.matmul(out, state_c(c - 1)[:, t * P:(t + 1) * P], q_dec[:, cs],
                                                    start=False, stop=True)
                    last.then_inc(gla_o, 1)
                pe.wait_ge(on_sq, hd.at(1))
                for half in range(2):
                    for t, sq in enumerate((dec, lev)):
                        last = nc.tensor.matmul(s_ps[:, 0, half_cols(half)], ones[:], sq[:, half_cols(half)],
                                                start=(t == 0), stop=(t == 1))
                last.then_inc(on_sum, 1)
                for j in range(4, 6):
                    panel(p + j, a_hi, a_lo)

            def rest_of_layer(layer):
                st = PLAN[layer]
                stage(Idx(st["wo"]), KT, a_hi, a_lo, Idx(st["x_o"]))

                def ff_chunk(c, first):
                    p = c.times(2 * KT) + st["mlp"]
                    if first:
                        stage(p, KT, b_hi, b_lo, Idx(st["x_mlp"]), st["norm"] + 1)
                    else:
                        stage(p, KT, b_hi, b_lo)
                    stage(p + KT, KT, a_hi, a_lo, c.times(16) + st["x_hid"])

                ff_chunk(Idx(0), True)
                with pe.Fori(1, CHUNKS) as c:
                    ff_chunk(Idx(0, [(1, c)]), False)
                for j in range(4):
                    p = st["ple"] + j
                    s = p % 2
                    pe.wait_ge(w_lo_ready, p + 1)
                    if j == 0:
                        pe.wait_ge(p_lo_ready, layer + 1)
                    half = j // 2
                    wh = whi[:, s].rearrange("p k m -> p (k m)")
                    wl = wlo[:, s].rearrange("p k m -> p (k m)")
                    for e in range(2):
                        pe.wait_ge(unit_free, 2 * p + e - 1)
                        for b in range(2):
                            for k in range(2):
                                o = k * HALF + (2 * e + b) * P
                                last = product(s_ps[:, e, half_cols(b)], wh[:, o:o + P], wl[:, o:o + P],
                                               a_hi[:, 4 + k, half_cols(half)], a_hi[:, 6 + k, half_cols(half)],
                                               k == 0, k == 1)
                        last.then_inc(unit_ready, 1)
                stage(Idx(st["gate"]), KT, b_hi, b_lo, Idx(st["x_ple"]), st["norm"] + 2)

            st = PLAN[0]
            pe.wait_ge(const_ready, 1)
            pe.wait_ge(gp_const, 1)
            panel(Idx(st["mix"]), a_hi, a_lo, Idx(st["x_mix"]), st["norm"])
            pe.wait_ge(ph_ready, 1)
            for first, diff in ((0, True), (DIFF_HEADS, False)):
                with pe.Fori(0, DIFF_HEADS // 2) as i:
                    for e in range(2):
                        hd = Idx(first + e, [(2, i)])
                        for j in range(3):
                            panel(hd.times(3) + (st["heads"] + j), a_hi, a_lo)
                        attention(hd, diff)
            rest_of_layer(0)
            st = PLAN[1]
            panel(Idx(st["mix"]), a_hi, a_lo, Idx(st["x_mix"]), st["norm"])
            with pe.Fori(0, GLA_HEADS) as i:
                gla_head(Idx(0, [(1, i)]))
            rest_of_layer(1)
            norm_sums(6)

        @block.gpsimd
        def _(gp):
            steps = Chain(gp, g_step)
            gp.dma_start(gcol[:], gains).then_inc(const_loaded, 16)
            gp.dma_start(colc[:, GSUB:GSUB + 1], g_sub).then_inc(const_loaded, 16)
            gp.dma_start(colc[0:DIFF_HEADS, BF:BF + 1], b_f).then_inc(const_loaded, 16)
            gp.dma_start(colc[:, BGK:BGK + GLA_HEADS], b_gk).then_inc(const_loaded, 16)
            gp.dma_start(colc[:, GON:GON + 2], g_on).then_inc(const_loaded, 16)
            gp.dma_start(wgk_all[:], w_gk).then_inc(const_loaded, 16)
            gp.dma_start(lam_in, lam_vec.rearrange("a n -> (a n)").partition_broadcast(P)).then_inc(const_loaded, 16)
            steps.link(nc.gpsimd.memset(ident[:], 0.0))
            steps.link(nc.gpsimd.affine_select(out=ident[:], in_=ident[:], compare_op=ALU.not_equal, fill=1.0,
                                               base=0, pattern=[[-1, P]], channel_multiplier=1))
            steps.link(nc.gpsimd.memset(mask_f, 0.0))
            nc.gpsimd.affine_select(out=mask_f, in_=mask_f, compare_op=ALU.is_ge, fill=MASKED,
                                    base=0, pattern=[[-1, P]], channel_multiplier=1).then_inc(gp_const, 1)

            def add_squares(n, o, half):
                a = o.times(2) + (16 * n + half)
                gp.wait_ge(sq_ready, a.at(1))
                return a

            def tile_squares(n, o, first):
                for half in range(2):
                    a = add_squares(n, o, half)
                    if first:
                        if n >= 1:
                            gp.wait_ge(norm_sum, 2 * n)
                        nc.gpsimd.tensor_copy(sumsq[:, half], zs[:, half]).then_inc(sq_added, 1)
                    else:
                        gp.wait_ge(sq_added, a.at(-1))
                        nc.gpsimd.tensor_tensor(sumsq[:, half], sumsq[:, half], zs[:, half],
                                                ALU.add).then_inc(sq_added, 1)

            def all_squares(n, after=None):
                tile_squares(n, Idx(0), True)
                if after:
                    after(Idx(0))
                with gp.Fori(1, KT) as o:
                    tile_squares(n, Idx(0, [(1, o)]), False)
                    if after:
                        after(Idx(0, [(1, o)]))

            all_squares(0)
            for layer, st in enumerate(PLAN):
                if layer == 1:
                    gp.wait_ge(h_spilled, 16 * KT)
                    gp.wait_ge(x_lo_ready, st["x_mix"] + 16)
                    for lv in range(LEVELS):
                        half_block = 64 >> lv
                        v = lmask[:, lv].rearrange("p (b n) -> p b n", n=2 * half_block)
                        nb = P // (2 * half_block)
                        steps.link(nc.gpsimd.memset(v, 1.0))
                        steps.link(nc.gpsimd.memset(v[:, :, 0:half_block], 0.0))
                        steps.link(nc.gpsimd.affine_select(out=v, in_=v, compare_op=ALU.is_ge, fill=0.0, base=0,
                                                           pattern=[[-2 * half_block, nb], [0, 2 * half_block]],
                                                           channel_multiplier=1))
                        steps.link(nc.gpsimd.affine_select(out=v, in_=v, compare_op=ALU.is_ge, fill=0.0,
                                                           base=half_block - 1,
                                                           pattern=[[2 * half_block, nb], [0, 2 * half_block]],
                                                           channel_multiplier=-1))
                    nc.gpsimd.tensor_copy(lmask[:, LEVELS], ident[:]).then_inc(gp_const, 1)
                all_squares(st["norm"] + 1)
                all_squares(st["norm"] + 2)
                gp.wait_ge(unit_ready, 2 * st["ple"])
                gp.dma_start(p_raw[:], p_t[layer].rearrange("k p n -> p k n")).then_inc(p_loaded, 16)

                def spill(o):
                    gp.wait_ge(h_ready, o.times(2).at(2))
                    gp.dma_start(h_dram[o.cols(1)].rearrange("a p n -> p (a n)"),
                                 h[:, o.cols(1)].rearrange("p a n -> p (a n)")).then_inc(h_spilled, 16)

                all_squares(st["norm"] + 3, spill if layer == 0 else None)

        @block.scalar
        def _(act):
            steps = Chain(act, a_step)
            A = nc.scalar.activation

            def w_hi(p):
                if p.at() is not None and isinstance(p.at(), int) and p.at() >= PANELS:
                    return
                act.wait_ge(w_loaded[p.parity], p.half().times(16).at(16))
                if not (isinstance(p.at(), int) and p.at() < 2):
                    act.wait_ge(unit_ready, p.times(2).at(-2))
                A(whi[:, p.parity], wraw[:, p.parity], ACT.Copy).then_inc(w_hi_ready, 1)

            def finish(n, o, half, next_hi):
                a = o.times(2) + (16 * n + half)
                src = h[:, o.cols(1), half_cols(half)].rearrange("p a n -> p (a n)")
                if not (isinstance(a.at(), int) and a.at() < 2):
                    act.wait_ge(sq_added, a.at(-1))
                A(zs[:, half], src, ACT.Square).then_inc(sq_ready, 1)
                if next_hi is not None:
                    A(next_hi[:, o.cols(1), half_cols(half)].rearrange("p a n -> p (a n)"), src, ACT.Copy,
                      scale=gcol[:, o.cols(1, add=KT * n)]).then_inc(x_hi_ready, 1)

            def norm_root_of(n):
                act.wait_ge(norm_ms, n + 1)
                A(rstd[:], rstd[:], ACT.Sqrt).then_inc(norm_root, 1)

            def split_head(hd):
                u = hd.times(6) + 2 * PLAN[0]["heads"]
                for j, dst in enumerate((q_hi, k_hi)):
                    w_hi(hd.times(3) + (PLAN[0]["heads"] + j + 1))
                    for half in range(2):
                        act.wait_ge(unit_free, u.at(2 * j + half + 1))
                        A(dst[:, half_cols(half)], zt[:, half], ACT.Copy).then_inc(qk_hi_ready, 1)
                w_hi(hd.times(3) + (PLAN[0]["heads"] + 3))

            def attention(hd, diff):
                maps = 2 if diff else 1
                split_head(hd)
                if not diff:
                    A(cm_hi[0:DIFF_HEADS], c_row[0:DIFF_HEADS], ACT.Copy,
                      scale=ident[0:DIFF_HEADS, hd.cols(1, add=-DIFF_HEADS)]).then_inc(cm_hi_ready, 1)
                act.wait_ge(vt_ready, hd.at(1))
                A(v_hi[:].rearrange("p a n -> p (a n)"), to_ps[:], ACT.Copy).then_inc(v_hi_ready, 1)

                def exps(i):
                    n = (i + 1) * P
                    act.wait_ge(negmax_ready, hd.times(NQT).at(i + 1))
                    for mp in range(maps):
                        c = 2 * (i % 2) + mp
                        last = A(prob[:, mp, 0:n], s_ps[:, mp, 0:n], ACT.Exp, bias=colc[:, NEG + c:NEG + c + 1],
                                 accum_out=colc[:, L + c:L + c + 1])
                    last.then_inc(exp_ready, 1)

                exps(0)
                done = 0
                for i in range(NQT):
                    if i % 2 == 0 and i >= 2:
                        act.wait_ge(pv_ready, hd.times(4).at(i // 2))
                    for g in range(GROUPS[i]):
                        n = min(4, i + 1 - 4 * g)
                        act.wait_ge(tr_ready, hd.times(GROUPS_HEAD).at(done + 1))
                        A(pt_hi[:, 4 * g:4 * g + n, (i % 2) * P:(i % 2 + 1) * P],
                          to_ps[:, 0:n * P].rearrange("p (j q) -> p j q", q=P), ACT.Copy).then_inc(tr_hi, 1)
                        done += 1
                    if i + 1 < NQT:
                        exps(i + 1)
                if diff:
                    act.wait_ge(o_evacuated, hd.times(4).at(5))
                    A(prob[:, 0], o_raw[:, hd.cols(1)].rearrange("p a n -> p (a n)"), ACT.Square).then_inc(sub_sq, 1)
                    act.wait_ge(sub_ms, hd.at(1))
                    A(prob[:, 1], prob[:, 1], ACT.Sqrt).then_inc(sub_root, 1)

            def log_sigmoid_part(x, t):
                steps.link(A(t, x, ACT.Abs))
                steps.link(A(t, t, ACT.Exp, scale=-1.0))
                return A(t, t, ACT.Ln, bias=colc[0:x.shape[0], ONE:ONE + 1])

            def gla_head(hd):
                p = hd.times(6) + PLAN[1]["heads"]
                for j in range(4):
                    w_hi(p + (j + 1))
                act.wait_ge(gk_in, hd.at(1))
                log_sigmoid_part(b_cum[:], dec[:]).then_inc(gk_log, 1)
                act.wait_ge(vtok_sum, hd.at(1))
                for t in range(2):
                    last = A(v_tok[:, :, t * P:(t + 1) * P], s_ps[:, t].rearrange("p (c n) -> p c n", n=P), ACT.Copy)
                last.then_inc(vtok_ready, 1)
                for e in range(LEVELS + 2):
                    act.wait_ge(dec_in, hd.times(LEVELS + 2).at(e + 1))
                    if e == LEVELS:
                        A(dec[:], b_cum[:], ACT.Exp)
                        A(colc[:, EB:EB + NQT], b_cum[:, P - 1:SEQ:P], ACT.Exp).then_inc(dec_exp, 1)
                    else:
                        A(dec[:], dec[:], ACT.Exp).then_inc(dec_exp, 1)
                act.wait_ge(ktok_sum, hd.at(1))
                A(k_tok[:], to_ps[:], ACT.Copy).then_inc(ktok_ready, 1)
                act.wait_ge(gla_o_free, hd.times(NQT).at(NQT))
                for t, dst in enumerate((dec, lev)):
                    last = A(dst[:], o_raw1[:, (hd.times(2) + t).cols(1)].rearrange("p a n -> p (a n)"), ACT.Square)
                last.then_inc(on_sq, 1)
                act.wait_ge(on_ms, hd.at(1))
                A(dec[:], dec[:], ACT.Sqrt).then_inc(on_root, 1)
                for j in range(4, 6):
                    w_hi(p + (j + 1))
                    for half in range(2):
                        act.wait_ge(unit_free, (p + j).times(2).at(half + 1))
                        A(zs[:, half], zt[:, half], ACT.Sigmoid).then_inc(sig_ready, 1)

            def pairs(count, body):
                with act.Fori(0, count // 2) as i:
                    for s in range(2):
                        body(Idx(s, [(2, i)]))

            def rest_of_layer(layer):
                st = PLAN[layer]
                src = o_raw if layer == 0 else o_raw1
                act.wait_ge(unit_ready, 2 * st["wo"])

                def split_o(o):
                    for half in range(2):
                        A(a_hi[:, o.cols(1), half_cols(half)].rearrange("p a n -> p (a n)"),
                          src[:, o.cols(1), half_cols(half)].rearrange("p a n -> p (a n)"),
                          ACT.Copy).then_inc(x_hi_ready, 1)

                if layer == 0:
                    act.wait_ge(o_evacuated, 4 * HEADS + 1)
                else:
                    act.wait_ge(o_gated, 1)
                pairs(KT, split_o)

                def wo(o):
                    w_hi(o + (st["wo"] + 1))
                    for half in range(2):
                        act.wait_ge(unit_free, (o + st["wo"]).times(2).at(half + 1))
                        finish(st["norm"] + 1, o, half, b_hi)

                pairs(KT, wo)
                norm_root_of(st["norm"] + 1)

                def ff_chunk(c, last_chunk):
                    p = c.times(2 * KT) + st["mlp"]

                    def up(o):
                        w_hi(p + (o + 1))
                        for half in range(2):
                            act.wait_ge(unit_free, (p + o).times(2).at(half + 1))
                            A(zs[:, half], zt[:, half], ACT.Square)
                            A(a_hi[:, o.cols(1), half_cols(half)].rearrange("p a n -> p (a n)"), zt[:, half],
                              ACT.Square).then_inc(x_hi_ready, 1)

                    def down(o):
                        w_hi(p + (o + KT + 1))
                        if last_chunk:
                            for half in range(2):
                                act.wait_ge(unit_free, (p + (o + KT)).times(2).at(half + 1))
                                finish(st["norm"] + 2, o, half, b_hi)

                    pairs(KT, up)
                    pairs(KT, down)

                with act.Fori(0, CHUNKS - 1) as c:
                    ff_chunk(Idx(0, [(1, c)]), False)
                ff_chunk(Idx(CHUNKS - 1), True)
                act.wait_ge(p_loaded, 16 * (layer + 1))
                A(a_hi[:, 4:6], p_raw[:], ACT.Copy).then_inc(p_hi_ready, 1)
                for j in range(4):
                    w_hi(Idx(st["ple"] + j + 1))
                norm_root_of(st["norm"] + 2)

                def gate(o):
                    n = st["norm"] + 3
                    w_hi(o + (st["gate"] + 1))
                    for half in range(2):
                        g = o.times(2) + half
                        act.wait_ge(unit_free, (o + st["gate"]).times(2).at(half + 1))
                        act.wait_ge(sq_added, (g + 16 * n).at(-1))
                        A(zs[:, half], zt[:, half], ACT.Sigmoid).then_inc(sig_ready, 1)
                        act.wait_ge(h_ready, g.at(16 * layer + 1))
                        finish(n, o, half, a_hi if layer == 0 else None)

                if layer == 0:
                    pairs(KT, gate)
                else:
                    with act.Fori(0, KT // 2 - 1) as i:
                        for s in range(2):
                            gate(Idx(s, [(2, i)]))
                    for o in (KT - 2, KT - 1):
                        gate(Idx(o))
                norm_root_of(st["norm"] + 3)

            for o in range(KT):
                act.dma_start(h[:, o], x_t[o]).then_inc(x_loaded, 16)
            act.wait_ge(const_loaded, 16 * 7)
            act.wait_ge(x_loaded, 16 * KT)
            act.wait_ge(gp_const, 1)
            A(ident_r[:], ident[:], ACT.Copy)
            A(mask_r[:], mask_f, ACT.Copy)
            act.wait_ge(const_ready, 2)
            A(negones_r[:], ones[0:DIFF_HEADS], ACT.Copy, scale=-1.0).then_inc(ph_ready, 1)
            A(colc[:, LAM1:LAM1 + 2], colc[:, LAM1:LAM1 + 2], ACT.Exp).then_inc(lam_exp, 1)
            w_hi(Idx(0))
            for o in range(KT):
                for half in range(2):
                    finish(0, Idx(o), half, a_hi)
            w_hi(Idx(1))
            norm_root_of(0)
            act.wait_ge(fl_ready, 1)
            log_sigmoid_part(prob[0:DIFF_HEADS, 0], prob[0:DIFF_HEADS, 1]).then_inc(fl_log, 1)
            for first, diff in ((0, True), (DIFF_HEADS, False)):
                with act.Fori(0, DIFF_HEADS // 2) as i:
                    for e in range(2):
                        attention(Idx(first + e, [(2, i)]), diff)
            rest_of_layer(0)
            w_hi(Idx(PLAN[1]["heads"]))
            with act.Fori(0, GLA_HEADS) as i:
                steps.enter(i, 2)
                gla_head(Idx(0, [(1, i)]))
                steps.leave(GLA_HEADS, 2)
            rest_of_layer(1)

        @block.vector
        def _(dve):
            steps = Chain(dve, v_step)
            V = nc.vector

            def w_lo(p):
                if isinstance(p.at(), int) and p.at() >= PANELS:
                    return
                dve.wait_ge(w_hi_ready, p.at(1))
                V.tensor_tensor(wlo[:, p.parity], wraw[:, p.parity], whi[:, p.parity],
                                ALU.subtract).then_inc(w_lo_ready, 1)

            def tile_of(t, o, half):
                return t[:, o.cols(1), half_cols(half)].rearrange("p a n -> p (a n)")

            def split_lo(n, o, half, x, hi, lo):
                dve.wait_ge(x_hi_ready, x.at(1))
                V.scalar_tensor_tensor(tile_of(lo, o, half), tile_of(h, o, half), gcol[:, o.cols(1, add=KT * n)],
                                       tile_of(hi, o, half), ALU.mult, ALU.subtract).then_inc(x_lo_ready, 1)

            def norm_scale(n):
                dve.wait_ge(norm_sum, 2 * n + 2)
                V.tensor_scalar(rstd[:], s_ps[:, 0], 1.0 / D, EPS, ALU.mult, ALU.add).then_inc(norm_ms, 1)
                dve.wait_ge(norm_root, n + 1)
                steps.link(V.reciprocal(rstd[:], rstd[:]))

            def bank(half, rows=P):
                return gemm_ps[0:rows, half]

            def project(hd):
                p = hd.times(3) + PLAN[0]["heads"]
                for j, (hi, lo) in enumerate(((q_hi, q_lo), (k_hi, k_lo), (None, None))):
                    w_lo(p + (j + 1))
                    for half in range(2):
                        u = (p + j).times(2) + half
                        dve.wait_ge(unit_ready, u.at(1))
                        if j == 0:
                            V.scalar_tensor_tensor(zt[:, half], bank(half), colc[:, hd.cols(1, add=QS)],
                                                   rstd[:, half_cols(half)], ALU.mult, ALU.mult).then_inc(unit_free, 1)
                        elif j == 1:
                            V.tensor_tensor(zt[:, half], bank(half), rstd[:, half_cols(half)],
                                            ALU.mult).then_inc(unit_free, 1)
                        else:
                            V.tensor_tensor(v_t[:, half_cols(half)], bank(half), rstd[:, half_cols(half)],
                                            ALU.mult).then_inc(unit_free, 1)
                            continue
                        dve.wait_ge(qk_hi_ready, hd.times(4).at(2 * j + half + 1))
                        V.tensor_tensor(lo[:, half_cols(half)], zt[:, half], hi[:, half_cols(half)],
                                        ALU.subtract).then_inc(qk_lo_ready, 1)

            def attention(hd, diff):
                maps = 2 if diff else 1
                project(hd)
                if not diff:
                    dve.wait_ge(cm_hi_ready, hd.at(1 - DIFF_HEADS))
                    V.scalar_tensor_tensor(cm_lo[0:DIFF_HEADS], c_row[0:DIFF_HEADS],
                                           ident[0:DIFF_HEADS, hd.cols(1, add=-DIFF_HEADS)],
                                           cm_hi[0:DIFF_HEADS], ALU.mult, ALU.subtract).then_inc(cm_lo_ready, 1)
                dve.wait_ge(v_hi_ready, hd.at(1))
                V.tensor_tensor(v_lo[:].rearrange("p a n -> p (a n)"), to_ps[:], v_hi[:].rearrange("p a n -> p (a n)"),
                                ALU.subtract).then_inc(v_lo_ready, 1)

                def negmax(i):
                    n = (i + 1) * P
                    dve.wait_ge(scores_ready, hd.times(NQT).at(i + 1))
                    c = NEG + 2 * (i % 2)
                    V.tensor_reduce(colc[:, c:c + maps], s_ps[:, 0:maps, 0:n], AX, ALU.max,
                                    negate=True).then_inc(negmax_ready, 1)

                def weights(i):
                    n = (i + 1) * P
                    c = 2 * (i % 2)
                    dve.wait_ge(exp_ready, hd.times(NQT).at(i + 1))
                    steps.link(V.reciprocal(colc[:, RL + c:RL + c + maps], colc[:, L + c:L + c + maps]))
                    if diff:
                        steps.link(V.tensor_tensor(colc[:, C2:C2 + 1], colc[:, RL + c + 1:RL + c + 2],
                                                   colc[:, NEGLAM:NEGLAM + 1], ALU.mult))
                        steps.link(V.tensor_scalar(prob[:, 1, 0:n], prob[:, 1, 0:n], colc[:, C2:C2 + 1], None, ALU.mult))
                        V.scalar_tensor_tensor(prob[:, 0, 0:n], prob[:, 0, 0:n], colc[:, RL + c:RL + c + 1],
                                               prob[:, 1, 0:n], ALU.mult, ALU.add).then_inc(w_ready, 1)
                    else:
                        V.tensor_scalar(prob[:, 0, 0:n], prob[:, 0, 0:n], colc[:, RL + c:RL + c + 1], None,
                                        ALU.mult).then_inc(w_ready, 1)

                def evacuate(c):
                    dve.wait_ge(pv_ready, hd.times(4).at(c + 1))
                    V.tensor_copy(o_raw[:, hd.cols(1), c * 256:(c + 1) * 256].rearrange("p a n -> p (a n)"),
                                  to_ps[:, HALF:HALF + 256]).then_inc(o_evacuated, 1)

                negmax(0)
                done = 0
                for i in range(NQT):
                    weights(i)
                    if i + 1 < NQT:
                        negmax(i + 1)
                    if i % 2 == 0 and i >= 2:
                        evacuate(i // 2 - 1)
                    for g in range(GROUPS[i]):
                        n = min(4, i + 1 - 4 * g)
                        done += 1
                        dve.wait_ge(tr_hi, hd.times(GROUPS_HEAD).at(done))
                        q = slice((i % 2) * P, (i % 2 + 1) * P)
                        V.tensor_tensor(pt_lo[:, 4 * g:4 * g + n, q],
                                        to_ps[:, 0:n * P].rearrange("p (j q) -> p j q", q=P),
                                        pt_hi[:, 4 * g:4 * g + n, q], ALU.subtract).then_inc(tr_lo, 1)
                evacuate(3)
                if diff:
                    dve.wait_ge(sub_sum, hd.at(1))
                    V.tensor_scalar(prob[:, 1], s_ps[:, 0], 1.0 / P, EPS, ALU.mult, ALU.add).then_inc(sub_ms, 1)
                    dve.wait_ge(sub_root, hd.at(1))
                    steps.link(V.reciprocal(prob[:, 1], prob[:, 1]))
                    o = o_raw[:, hd.cols(1)].rearrange("p a n -> p (a n)")
                    V.scalar_tensor_tensor(o, o, colc[:, GSUB:GSUB + 1], prob[:, 1], ALU.mult,
                                           ALU.mult).then_inc(sub_done, 1)

            def log_sigmoid(x, t, scale):
                steps.link(V.scalar_tensor_tensor(t, x, 0.0, t, ALU.min, ALU.subtract))
                if scale != 1.0:
                    steps.link(V.tensor_scalar(t, t, scale, None, ALU.mult))

            def gla_head(hd):
                st = PLAN[1]
                p = hd.times(6) + st["heads"]
                V.tensor_copy(wgk_h, wgk_all[:, hd.cols(DK)]).then_inc(gk_w, 1)
                for j, dst in enumerate((q_t[:], k_t[:], vg_t[:, 0], vg_t[:, 1])):
                    w_lo(p + (j + 1))
                    for half in range(2):
                        dve.wait_ge(unit_ready, (p + j).times(2).at(half + 1))
                        if j == 0:
                            V.scalar_tensor_tensor(dst[:, half_cols(half)], bank(half), DK ** -0.5,
                                                   rstd[:, half_cols(half)], ALU.mult, ALU.mult).then_inc(unit_free, 1)
                        else:
                            V.tensor_tensor(dst[:, half_cols(half)], bank(half), rstd[:, half_cols(half)],
                                            ALU.mult).then_inc(unit_free, 1)
                dve.wait_ge(gk_sum, hd.at(1))
                V.tensor_scalar(b_cum[:], to_ps[:], colc[:, hd.cols(1, add=BGK)], None, ALU.add).then_inc(gk_in, 1)
                dve.wait_ge(gk_log, hd.at(1))
                log_sigmoid(b_cum[:], dec[:], 1.0 / 16.0)
                steps.link(V.tensor_tensor_scan(b_cum[:], resets[:], dec[:], 0.0, ALU.mult, ALU.add))

                def decays(lv):
                    hb = 64 >> lv
                    b = b_cum[:].rearrange("p (b n) -> p b n", n=2 * hb)
                    d = dec[:].rearrange("p (b n) -> p b n", n=2 * hb)
                    ref = b[:, :, hb - 1:hb].to_broadcast([P, SEQ // (2 * hb), hb])
                    V.tensor_tensor(d[:, :, 0:hb], ref, b[:, :, 0:hb], ALU.subtract)
                    V.tensor_tensor(d[:, :, hb:2 * hb], b[:, :, hb:2 * hb], ref, ALU.subtract).then_inc(dec_in, 1)

                def level(lv):
                    hb = 64 >> lv
                    dve.wait_ge(dec_exp, hd.times(LEVELS + 2).at(lv + 1))
                    if lv >= 1:
                        dve.wait_ge(lev_sum, hd.times(LEVELS + 1).at(lv))
                    d, t, kk, qq = (a[:].rearrange("p (b n) -> p b n", n=2 * hb) for a in (dec, lev, k_t, q_t))
                    V.tensor_tensor(t[:, :, 0:hb], d[:, :, 0:hb], kk[:, :, 0:hb], ALU.mult)
                    V.tensor_tensor(t[:, :, hb:2 * hb], d[:, :, hb:2 * hb], qq[:, :, hb:2 * hb],
                                    ALU.mult).then_inc(lev_ready, 1)
                    dve.wait_ge(lev_ready, hd.times(LEVELS).at(lv + 1))

                def place(lv):
                    dve.wait_ge(lev_sum, hd.times(LEVELS + 1).at(lv + 1))
                    if lv >= 1:
                        dve.wait_ge(lev_done, hd.times(LEVELS + 1).at(lv))
                    V.memset(colc[:, MARK + 2 + lv:MARK + 3 + lv], 0.0)
                    mask = lmask[:, lv:lv + 1].bitcast(I32).to_broadcast([P, NQT, P])
                    V.copy_predicated(att[:].rearrange("p (c n) -> p c n", n=P), mask,
                                      s_ps[:, lv % 2].rearrange("p (c n) -> p c n", n=P)).then_inc(lev_done, 1)

                decays(0)
                for lv in range(LEVELS):
                    level(lv)
                    if lv + 1 < LEVELS:
                        decays(lv + 1)
                    else:
                        V.memset(colc[:, MARK + 1:MARK + 2], 0.0).then_inc(dec_in, 1)
                    if lv >= 1:
                        place(lv - 1)
                place(LEVELS - 1)
                dve.wait_ge(dec_exp, hd.times(LEVELS + 2).at(LEVELS + 1))
                steps.link(V.tensor_tensor(q_dec[:], q_t[:], dec[:], ALU.mult))
                b = b_cum[:].rearrange("p (c n) -> p c n", n=P)
                V.tensor_tensor(dec[:].rearrange("p (c n) -> p c n", n=P),
                                b[:, :, P - 1:P].to_broadcast([P, NQT, P]), b, ALU.subtract).then_inc(dec_in, 1)
                dve.wait_ge(dec_exp, hd.times(LEVELS + 2).at(LEVELS + 2))
                V.tensor_tensor(k_dec[:], k_t[:], dec[:], ALU.mult).then_inc(ktok_in, 1)
                place(LEVELS)
                for c in range(NQT):
                    if c < NQT - 1:
                        dve.wait_ge(st_sum, hd.times(NQT - 1).at(c + 1))
                        if c == 0:
                            V.tensor_copy(state_c(0), to_ps[:, 0:DV]).then_inc(st_ready, 1)
                        else:
                            V.scalar_tensor_tensor(state_c(c), state_c(c - 1), colc[:, EB + c:EB + c + 1],
                                                   to_ps[:, 0:DV], ALU.mult, ALU.add).then_inc(st_ready, 1)
                        dve.wait_ge(st_ready, hd.times(NQT - 1).at(c + 1))
                    dve.wait_ge(gla_o, hd.times(NQT).at(c + 1))
                    V.tensor_copy(o_raw1[:, hd.times(2).cols(2, scale=1), c * P:(c + 1) * P],
                                  s_ps[:, c % 2, 0:DV].rearrange("p (t n) -> p t n", n=P)).then_inc(gla_o_free, 1)
                dve.wait_ge(on_sum, hd.at(1))
                V.tensor_scalar(dec[:], s_ps[:, 0], 1.0 / DV, EPS, ALU.mult, ALU.add).then_inc(on_ms, 1)
                dve.wait_ge(on_root, hd.at(1))
                steps.link(V.reciprocal(dec[:], dec[:]))
                for t in range(2):
                    j = 4 + t
                    w_lo(p + (j + 1))
                    for half in range(2):
                        dve.wait_ge(unit_ready, (p + j).times(2).at(half + 1))
                        V.tensor_tensor(zt[:, half], bank(half), rstd[:, half_cols(half)],
                                        ALU.mult).then_inc(unit_free, 1)
                        o = tile_of(o_raw1, hd.times(2) + t, half)
                        steps.link(V.tensor_tensor(o, o, dec[:, half_cols(half)], ALU.mult))
                        dve.wait_ge(sig_ready, hd.times(4).at(SIG_MIX1 + 2 * t + half + 1))
                        steps.link(V.tensor_tensor(zt[:, half], zt[:, half], zs[:, half], ALU.mult))
                        steps.link(V.scalar_tensor_tensor(o, o, colc[:, GON + t:GON + t + 1], zt[:, half],
                                                          ALU.mult, ALU.mult))

            def pairs(count, body, links=0):
                with dve.Fori(0, count // 2) as i:
                    steps.enter(i, links)
                    for s in range(2):
                        body(Idx(s, [(2, i)]))
                    steps.leave(count // 2, links)

            def rest_of_layer(layer):
                st = PLAN[layer]
                src = o_raw if layer == 0 else o_raw1
                if layer == 1:
                    V.memset(colc[:, MARK:MARK + 1], 0.0).then_inc(o_gated, 1)

                def split_o(o):
                    for half in range(2):
                        dve.wait_ge(x_hi_ready, o.times(2).at(st["x_o"] + half + 1))
                        V.tensor_tensor(tile_of(a_lo, o, half), tile_of(src, o, half), tile_of(a_hi, o, half),
                                        ALU.subtract).then_inc(x_lo_ready, 1)

                pairs(KT, split_o)

                def wo(o):
                    w_lo(o + (st["wo"] + 1))
                    for half in range(2):
                        u = (o + st["wo"]).times(2) + half
                        if half == 0:
                            dve.wait_ge(h_loaded[o.parity], (o.half() + 4 * layer).times(16).at(16))
                        dve.wait_ge(unit_ready, u.at(1))
                        V.tensor_tensor(tile_of(h, o, half), bank(half), tile_of(h, o, half),
                                        ALU.add).then_inc(unit_free, 1)
                        split_lo(st["norm"] + 1, o, half, o.times(2) + (st["x_mlp"] + half), b_hi, b_lo)

                pairs(KT, wo)
                norm_scale(st["norm"] + 1)

                def ff_chunk(c, last_chunk):
                    p = c.times(2 * KT) + st["mlp"]
                    x = c.times(16) + st["x_hid"]

                    def up(o):
                        w_lo(p + (o + 1))
                        for half in range(2):
                            dve.wait_ge(unit_ready, (p + o).times(2).at(half + 1))
                            V.scalar_tensor_tensor(zt[:, half], bank(half), 0.0, rstd[:, half_cols(half)], ALU.max,
                                                   ALU.mult).then_inc(unit_free, 1)
                            dve.wait_ge(x_hi_ready, (x + o.times(2)).at(half + 1))
                            V.tensor_tensor(tile_of(a_lo, o, half), zs[:, half], tile_of(a_hi, o, half),
                                            ALU.subtract).then_inc(x_lo_ready, 1)

                    def down(o):
                        w_lo(p + (o + KT + 1))
                        for half in range(2):
                            dve.wait_ge(unit_ready, (p + (o + KT)).times(2).at(half + 1))
                            V.tensor_tensor(tile_of(h, o, half), bank(half), tile_of(h, o, half),
                                            ALU.add).then_inc(unit_free, 1)
                            if last_chunk:
                                split_lo(st["norm"] + 2, o, half, o.times(2) + (st["x_ple"] + half), b_hi, b_lo)

                    pairs(KT, up)
                    pairs(KT, down)

                with dve.Fori(0, CHUNKS - 1) as c:
                    ff_chunk(Idx(0, [(1, c)]), False)
                ff_chunk(Idx(CHUNKS - 1), True)
                dve.wait_ge(p_hi_ready, layer + 1)
                V.tensor_tensor(a_hi[:, 6:8], p_raw[:], a_hi[:, 4:6], ALU.subtract).then_inc(p_lo_ready, 1)
                for j in range(4):
                    w_lo(Idx(st["ple"] + j + 1))
                    for e in range(2):
                        o = 4 * (j % 2) + 2 * e
                        dve.wait_ge(unit_ready, 2 * (st["ple"] + j) + e + 1)
                        V.tensor_copy(pp[:, o:o + 2, half_cols(j // 2)],
                                      s_ps[:, e].rearrange("p (a n) -> p a n", n=HALF)).then_inc(unit_free, 1)
                norm_scale(st["norm"] + 2)

                def gate(o):
                    n = st["norm"] + 3
                    w_lo(o + (st["gate"] + 1))
                    for half in range(2):
                        g = o.times(2) + half
                        dve.wait_ge(unit_ready, (o + st["gate"]).times(2).at(half + 1))
                        V.tensor_tensor(zt[:, half], bank(half), rstd[:, half_cols(half)],
                                        ALU.mult).then_inc(unit_free, 1)
                        dve.wait_ge(sig_ready, g.at((0 if layer == 0 else SIG_GATE1) + 1))
                        steps.link(V.tensor_tensor(zt[:, half], zs[:, half], tile_of(pp, o, half), ALU.mult))
                        V.tensor_tensor(tile_of(h, o, half), tile_of(h, o, half), zt[:, half],
                                        ALU.add).then_inc(h_ready, 1)
                        if layer == 0:
                            split_lo(n, o, half, g + PLAN[1]["x_mix"], a_hi, a_lo)

                if layer == 0:
                    pairs(KT, gate, 4)
                else:
                    with dve.Fori(0, KT // 2 - 1) as i:
                        steps.enter(i, 4)
                        for s in range(2):
                            gate(Idx(s, [(2, i)]))
                        steps.leave(KT // 2 - 1, 4)
                    for o in (KT - 2, KT - 1):
                        gate(Idx(o))

            V.memset(ones[:], 1.0).then_inc(const_ready, 1)
            V.memset(colc[:, QS:QS + DIFF_HEADS], 64 ** -0.5).then_inc(o_evacuated, 1)
            V.memset(colc[:, QS + DIFF_HEADS:QS + HEADS], 128 ** -0.5).then_inc(sub_done, 1)
            steps.link(V.memset(colc[:, ONE:ONE + 1], 1.0))
            dve.wait_ge(const_loaded, 16 * 7)
            for t in range(2):
                steps.link(V.tensor_tensor(zt[:, 1, t * 64:(t + 1) * 64], lam_in[:, 2 * t * 64:(2 * t + 1) * 64],
                                           lam_in[:, (2 * t + 1) * 64:(2 * t + 2) * 64], ALU.mult))
            V.tensor_reduce(colc[:, LAM1:LAM1 + 2], zt[:, 1, 0:128].rearrange("p (t n) -> p t n", t=2), AX,
                            ALU.add).then_inc(const_ready, 1)
            w_lo(Idx(0))
            for o in range(KT):
                for half in range(2):
                    split_lo(0, Idx(o), half, Idx(2 * o + half), a_hi, a_lo)
            dve.wait_ge(lam_exp, 1)
            steps.link(V.tensor_tensor(colc[:, NEGLAM:NEGLAM + 1], colc[:, LAM2:LAM2 + 1], colc[:, LAM1:LAM1 + 1],
                                       ALU.subtract))
            steps.link(V.tensor_scalar(colc[:, NEGLAM:NEGLAM + 1], colc[:, NEGLAM:NEGLAM + 1], LAM_INIT, None,
                                       ALU.subtract))
            steps.link(V.tensor_scalar(colc[:, GSUB:GSUB + 1], colc[:, GSUB:GSUB + 1], 1.0 - LAM_INIT, None, ALU.mult))
            w_lo(Idx(1))
            norm_scale(0)
            F = DIFF_HEADS
            for half in range(2):
                dve.wait_ge(unit_ready, half + 1)
                V.tensor_tensor(prob[0:F, 0, half_cols(half)], bank(half, F), rstd[0:F, half_cols(half)],
                                ALU.mult).then_inc(unit_free, 1)
            dve.wait_ge(unit_free, 2)
            V.tensor_scalar(prob[0:F, 0], prob[0:F, 0], colc[0:F, BF:BF + 1], None, ALU.add).then_inc(fl_ready, 1)
            V.memset(c_row[:], 0.0)
            steps.link(V.memset(v_t[:], 1.0))
            dve.wait_ge(fl_log, 1)
            log_sigmoid(prob[0:F, 0], prob[0:F, 1], 1.0)
            steps.link(V.tensor_tensor_scan(c_row[0:F], v_t[0:F], prob[0:F, 1], 0.0, ALU.mult, ALU.add))
            for first, diff in ((0, True), (DIFF_HEADS, False)):
                links = 2 * (3 * NQT + 1) if diff else 2 * NQT
                with dve.Fori(0, DIFF_HEADS // 2) as i:
                    steps.enter(i, links)
                    for e in range(2):
                        attention(Idx(first + e, [(2, i)]), diff)
                    steps.leave(DIFF_HEADS // 2, links)
            rest_of_layer(0)
            st = PLAN[1]
            dve.wait_ge(gp_const, 2)
            V.memset(att[:], 0.0)
            steps.link(V.memset(resets[:], 1.0))
            steps.link(V.memset(resets[:, 0:SEQ:P], 0.0))
            norm_scale(st["norm"])
            w_lo(Idx(st["heads"]))
            for half in range(2):
                dve.wait_ge(unit_ready, 2 * st["mix"] + half + 1)
                V.tensor_tensor(gl_t[0:LOWRANK, half_cols(half)], bank(half, LOWRANK), rstd[0:LOWRANK, half_cols(half)],
                                ALU.mult).then_inc(unit_free, 1)
            with dve.Fori(0, GLA_HEADS) as i:
                links = 2 + 1 + 1 + 1 + 4 * 3
                steps.enter(i, links)
                gla_head(Idx(0, [(1, i)]))
                steps.leave(GLA_HEADS, links)
            rest_of_layer(1)
            norm_scale(6)
            for o in range(KT):
                V.scalar_tensor_tensor(h[:, o], h[:, o], gcol[:, 6 * KT + o:6 * KT + o + 1], rstd[:], ALU.mult,
                                       ALU.mult).then_inc(final_ready, 1)


def kernel(**inputs):
    import numpy as np
    import concourse.bacc as bacc
    from concourse.bass_utils import run_bass_kernel_spmd

    a = {k: np.asarray(v) for k, v in inputs.items()}

    def panel(w):
        k, n = w.shape
        return w.reshape(k // P, P, n // P, P).transpose(2, 1, 0, 3).reshape(n // P, P, -1)

    def padded(w):
        return np.concatenate([w, np.zeros((w.shape[0], P - w.shape[1]), w.dtype)], axis=1)

    def layer_tail(w_o, i):
        up, down = a["w_up"][i], a["w_down"][i]
        parts = [panel(w_o)]
        for c in range(CHUNKS):
            parts += [panel(up[:, c * D:(c + 1) * D]), panel(down[c * D:(c + 1) * D])]
        proj = a["w_ple_proj"][i].reshape(2, P, 2, HALF).transpose(2, 1, 0, 3).reshape(2, P, -1)
        return parts + [proj, proj, panel(a["w_ple_gate"][i])]

    even, odd = a["even_w_in"][0], a["odd_w_in"][0]
    W = DIFF_HEADS * P
    cols = lambda w, c: panel(w[:, c:c + P])
    stream = [panel(padded(even[:, 6 * W:]))]
    for hd in range(HEADS):
        base = (hd // DIFF_HEADS) * 3 * W + (hd % DIFF_HEADS) * P
        stream += [cols(even, base), cols(even, base + W), cols(even, base + 2 * W)]
    stream += layer_tail(a["even_w_o"][0], 0)
    stream += [panel(padded(odd[:, 6 * W:]))]
    for hd in range(GLA_HEADS):
        v, g = 2 * W + hd * DV, 4 * W + hd * DV
        stream += [cols(odd, hd * DK), cols(odd, W + hd * DK), cols(odd, v), cols(odd, v + P), cols(odd, g),
                   cols(odd, g + P)]
    stream += layer_tail(a["odd_w_o"][0], 1)
    gains = [g for i in range(2) for g in (a["norm_mix"][i], a["norm_mlp"][i], a["norm_ple"][i])]
    arrays = {
        "x_t": a["x"][0].T.reshape(KT, P, SEQ),
        "p_t": a["p"][:, 0].transpose(0, 2, 1).reshape(2, 2, P, SEQ),
        "panels": np.concatenate(stream),
        "gains": np.stack(gains + [a["norm_final"]]).reshape(7 * KT, P).T,
        "b_f": a["even_b_f"].reshape(DIFF_HEADS, 1),
        "lam_vec": np.concatenate([a["lam_q1"], a["lam_k1"], a["lam_q2"], a["lam_k2"]]),
        "g_sub": a["diff_subln"].reshape(P, 1),
        "w_gk": a["odd_w_gk"][0],
        "b_gk": a["odd_b_gk"].reshape(GLA_HEADS, DK).T,
        "g_on": a["gla_onorm"].reshape(2, P).T,
    }
    arrays = {k: np.ascontiguousarray(v) for k, v in arrays.items()}
    assert arrays["panels"].shape == (PANELS, P, D)
    nc = bacc.Bacc("TRN2", target_bir_lowering=False, num_devices=1)
    args = [nc.dram_tensor(k, v.shape, mybir.dt.from_np(v.dtype), kind="ExternalInput").ap()
            for k, v in arrays.items()]
    args.append(nc.dram_tensor("out_t", [KT, P, SEQ], F32, kind="ExternalOutput").ap())
    build_trunk(nc, *args)
    r = run_bass_kernel_spmd(nc, [arrays], core_ids=[0])
    got = r.results[0]["out_t"]
    return np.ascontiguousarray(got.reshape(D, SEQ).T).reshape(1, SEQ, D)
```

```python
from contextlib import ExitStack

import concourse.bass as bass
from concourse import mybir
from concourse.alu_op_type import AluOpType as ALU

F32 = mybir.dt.float32
F32R = mybir.dt.float32r
I32 = mybir.dt.int32
ACT = mybir.ActivationFunctionType
AX = mybir.AxisListType.X
ds = bass.ds

P = 128
D = 1024
SEQ = 1024
KT = D // P
HALF = SEQ // 2
NQT = SEQ // P
FF = 4 * D
CHUNKS = FF // D
PLE = 256
HEADS = 8
DIFF_HEADS = 4
GLA_HEADS = 4
DK = 128
DV = 256
LOWRANK = 16
LEVELS = 7
EPS = 1e-6
SIG_MIX1 = 2 * KT
SIG_GATE1 = SIG_MIX1 + 4 * GLA_HEADS
LAM_INIT = 0.8 - 0.6 * 1.0
MASKED = -1.0e30

SUB_LAG = DIFF_HEADS
O_ORDER = [0, 1, 2, 4, 5, 6, 3, 7]
PANELS_MIX = 1 + 3 * HEADS
PANELS_MLP = 2 * KT * CHUNKS
PANELS_LAYER = PANELS_MIX + KT + PANELS_MLP + 4 + KT
PANELS = 2 * PANELS_LAYER
UNITS = 2 * KT
GROUPS = [1 if i < 4 else 2 for i in range(NQT)]
GROUPS_HEAD = sum(GROUPS)


PIECES = 8


class Share:

    def __init__(self, counts, units):
        left = PIECES * units - sum(counts)
        assert left >= 0, left
        self.counts = list(counts[:-1]) + [counts[-1] + left]
        self.units = units

    def complete(self, point):
        return sum(self.counts[:point]) // PIECES

    def fresh(self, point):
        return range(self.complete(point - 1) if point else 0, self.complete(point))

    def rest(self):
        return range(self.complete(len(self.counts) - 1), self.units)


ATT_SHARE = Share([2, 2] + [1, 1, 0, 2] * 4 + [2, 1, 3, 1] * 3 + [1, 0, 3, 3], 6)
NO_SHARE = Share([0] * 34, 0)
GLA_SHARE = {n: Share(c, n) for n, c in {
    8: [4] + [3] * 8 + [4, 4] + [1] * 8 + [10, 10], 12: [8] + [4] * 8 + [6, 6] + [3] * 8 + [10, 10],
    4: [4] + [2] * 8 + [4, 4] + [0] * 8 + [2, 2]}.items()}


class Idx:

    def __init__(self, c, terms=()):
        self.c, self.terms = c, tuple(terms)

    def __add__(self, n):
        if isinstance(n, Idx):
            return Idx(self.c + n.c, self.terms + n.terms)
        return Idx(self.c + n, self.terms)

    def times(self, m):
        return Idx(self.c * m, [(k * m, r) for k, r in self.terms])

    def half(self):
        return Idx(self.c // 2, [(k // 2, r) for k, r in self.terms])

    @property
    def parity(self):
        assert all(k % 2 == 0 for k, _ in self.terms)
        return self.c % 2

    def at(self, add=0):
        v = self.c + add
        for k, r in self.terms:
            v = r * k + v
        return v

    def cols(self, n, scale=None, add=0):
        s = self.times(n if scale is None else scale)
        return ds(s.at(add), n)


class Chain:

    def __init__(self, eng, sem):
        self.eng, self.sem, self.base, self.n = eng, sem, Idx(0), 0

    def link(self, ins):
        self.n += 1
        ins.then_inc(self.sem, 1)
        self.eng.wait_ge(self.sem, self.base.at(self.n))

    def enter(self, reg, steps, start=0):
        self.saved = (self.base, self.n)
        self.base, self.n = self.base + Idx(self.n - steps * start, [(steps, reg)]), 0

    def leave(self, iterations, steps):
        assert self.n == steps, (self.n, steps)
        base, n = self.saved
        self.base, self.n = base, n + iterations * steps


def plan_layer(layer):
    p0 = layer * PANELS_LAYER
    x0 = layer * 128
    s = dict(mix=p0, heads=p0 + 1, wo=p0 + PANELS_MIX)
    s["mlp"] = s["wo"] + KT
    s["gate"] = s["mlp"] + PANELS_MLP
    s["ple"] = s["gate"] + 1
    s["x_mix"] = x0
    s["x_o"] = x0 + 16
    s["x_mlp"] = x0 + 32
    s["x_hid"] = x0 + 48
    s["x_ple"] = x0 + 48 + 16 * CHUNKS
    s["norm"] = 3 * layer
    assert s["x_ple"] + 16 == x0 + 128 and s["heads"] % 2 == s["wo"] % 2
    return s


PLAN = [plan_layer(0), plan_layer(1)]


def build_trunk(nc, x_t, p_t, panels, gains, b_f, lam_vec, g_sub, w_gk, b_gk, g_on, out_t):
    m_dram = nc.dram_tensor("level_masks", [P, 8 * P], F32, kind="Internal").ap()
    h_dram = nc.dram_tensor("h_spill", [KT, P, SEQ], F32, kind="Internal").ap()
    ctx = ExitStack()
    with ctx:
        def overlay(*groups):
            made = {}
            for group in groups[1:]:
                with ExitStack() as inner:
                    for name, shape, dt in group:
                        made[name] = inner.enter_context(nc.sbuf_tensor(name, shape, dt))
            for name, shape, dt in groups[0]:
                made[name] = ctx.enter_context(nc.sbuf_tensor(name, shape, dt))
            return made

        def sb(name, shape, dt=F32):
            return ctx.enter_context(nc.sbuf_tensor(name, shape, dt))

        def sem(name):
            return ctx.enter_context(nc.semaphore(name))

        m = overlay(
            [("a_hi", [P, KT, SEQ], F32R), ("a_lo", [P, KT, SEQ], F32R)],
            [("p_raw", [P, 2, SEQ], F32), ("p_skip", [P, 6, SEQ], F32), ("pp", [P, KT, SEQ], F32)],
        )
        a_hi, a_lo, p_raw, pp = m["a_hi"], m["a_lo"], m["p_raw"], m["pp"]
        m = overlay(
            [("b_hi", [P, KT, SEQ], F32R), ("b_lo", [P, KT, SEQ], F32R)],
            [("o_raw", [P, KT, SEQ], F32),
             ("pt_hi", [P, NQT, 256], F32R), ("pt_lo", [P, NQT, 256], F32R),
             ("v_t", [P, SEQ], F32), ("c_row", [P, SEQ], F32),
             ("q_raw", [P, SEQ], F32), ("k_raw", [P, SEQ], F32)],
            [("o_below", [P, 7, SEQ], F32), ("lmask_built", [P, 8, P], F32)],
            [("o_raw1", [P, KT, SEQ], F32),
             ("dec", [P, SEQ], F32), ("lev", [P, SEQ], F32), ("att", [P, SEQ], F32),
             ("q_dec", [P, SEQ], F32), ("k_dec", [P, SEQ], F32), ("k_tok", [P, SEQ], F32),
             ("gl_t", [P, SEQ], F32), ("resets", [P, SEQ], F32)],
        )
        b_hi, b_lo, o_raw, pt_hi, pt_lo = m["b_hi"], m["b_lo"], m["o_raw"], m["pt_hi"], m["pt_lo"]
        v_t, c_row, q_raw, k_raw, lmask_built = m["v_t"], m["c_row"], m["q_raw"], m["k_raw"], m["lmask_built"]
        o_raw1, dec, lev, att = m["o_raw1"], m["dec"], m["lev"], m["att"]
        q_dec, k_dec, k_tok, gl_t, resets = m["q_dec"], m["k_dec"], m["k_tok"], m["gl_t"], m["resets"]
        m = overlay(
            [("h", [P, KT, SEQ], F32)],
            [("q_hi", [P, SEQ], F32R), ("q_lo", [P, SEQ], F32R), ("k_hi", [P, SEQ], F32R),
             ("k_lo", [P, SEQ], F32R), ("v_hi", [P, NQT, P], F32R), ("v_lo", [P, NQT, P], F32R),
             ("prob", [P, 2, SEQ], F32)],
            [("q_t", [P, SEQ], F32), ("k_t", [P, SEQ], F32), ("vg_t", [P, 2, SEQ], F32),
             ("v_tok", [P, NQT, DV], F32), ("b_cum", [P, SEQ], F32), ("lmask", [P, 8, P], F32)],
        )
        h, prob = m["h"], m["prob"]
        q_hi, q_lo, k_hi, k_lo, v_hi, v_lo = (m[n] for n in ("q_hi", "q_lo", "k_hi", "k_lo", "v_hi", "v_lo"))
        q_t, k_t, vg_t, v_tok, b_cum, lmask = (m[n] for n in ("q_t", "k_t", "vg_t", "v_tok", "b_cum", "lmask"))

        wraw = sb("wraw", [P, 2, KT, P])
        whi = sb("whi", [P, 2, KT, P], F32R)
        wlo = sb("wlo", [P, 2, KT, P], F32R)
        rstd = sb("rstd", [P, SEQ])
        sumsq = sb("sumsq", [P, 2, HALF])
        m = overlay([("zt", [P, 2, HALF], F32), ("zs", [P, 2, HALF], F32)],
                    [("cm_hi", [P, SEQ], F32R), ("cm_lo", [P, SEQ], F32R)])
        zt, zs, cm_hi, cm_lo = m["zt"], m["zs"], m["cm_hi"], m["cm_lo"]
        ones = sb("ones", [P, P])
        ident = sb("ident", [P, P])
        ident_r = sb("ident_r", [P, P], F32R)
        mask_f = zt[:, 0, 0:P]
        mask_r = sb("mask_r", [P, P], F32R)
        negones_r = sb("negones_r", [DIFF_HEADS, P], F32R)
        gcol = sb("gcol", [P, 7 * KT])
        colc = sb("colc", [P, 64])
        state = sb("state", [P, 2, DV])
        wgk_all = sb("wgk_all", [LOWRANK, GLA_HEADS * DK])
        wgk_h = sb("wgk_h", [LOWRANK, DK])
        lam_in = zs[:, 1, 0:256]

        QS = 0
        ONE, NEGLAM = 8, 9
        GSUB, BF, BGK, GON = 10, 11, 12, 16
        LAM1, LAM2 = 18, 19
        NEG, L, RL = 20, 24, 28
        C2 = 32
        EB = 40
        EPSC = 60
        MARK = 50

        gemm_ps = ctx.enter_context(nc.psum_tensor("gemm_ps", [P, 2, HALF], F32))
        s_ps = ctx.enter_context(nc.psum_tensor("s_ps", [P, 2, SEQ], F32))
        to_ps = ctx.enter_context(nc.psum_tensor("to_ps", [P, SEQ], F32))

        w_loaded = [sem("w_loaded0"), sem("w_loaded1")]
        w_hi_ready, w_lo_ready = sem("w_hi_ready"), sem("w_lo_ready")
        unit_ready, unit_free = sem("unit_ready"), sem("unit_free")
        x_hi_ready, x_lo_ready = sem("x_hi_ready"), sem("x_lo_ready")
        sq_ready, sq_added = sem("sq_ready"), sem("sq_added")
        norm_sum, norm_ms, norm_root = sem("norm_sum"), sem("norm_ms"), sem("norm_root")
        x_loaded = [sem(f"x_loaded{o}") for o in range(KT)]
        const_loaded, const_ready = sem("const_loaded"), sem("const_ready")
        gp_const, lam_exp, ph_ready = sem("gp_const"), sem("lam_exp"), sem("ph_ready")
        v_step, a_step, g_step = sem("v_step"), sem("a_step"), sem("g_step")
        qk_hi_ready, qk_lo_ready = sem("qk_hi_ready"), sem("qk_lo_ready")
        vt_ready, v_hi_ready, v_lo_ready = sem("vt_ready"), sem("v_hi_ready"), sem("v_lo_ready")
        scores_ready, negmax_ready, exp_ready, w_ready = (sem("scores_ready"), sem("negmax_ready"),
                                                          sem("exp_ready"), sem("weights_ready"))
        coef_ready, scaled_ready = sem("coef_ready"), sem("scaled_ready")
        masks_stored, masks_loaded = sem("masks_stored"), sem("masks_loaded")
        tr_ready, tr_hi, tr_lo = sem("tr_ready"), sem("tr_hi"), sem("tr_lo")
        pv_ready, o_evacuated = sem("pv_ready"), sem("o_evacuated")
        sub_sq, sub_sum, sub_ms, sub_root, sub_done = (sem("sub_sq"), sem("sub_sum"), sem("sub_ms"),
                                                       sem("sub_root"), sem("sub_done"))
        fl_ready, fl_log = sem("fl_ready"), sem("fl_log")
        cm_hi_ready, cm_lo_ready = sem("cm_hi_ready"), sem("cm_lo_ready")
        h_loaded = [sem("h_loaded0"), sem("h_loaded1")]
        h_spilled, p_loaded, out_stored = sem("h_spilled"), sem("p_loaded"), sem("out_stored")
        p_hi_ready, p_lo_ready = sem("p_hi_ready"), sem("p_lo_ready")
        sig_ready, h_ready, final_ready, o_gated = sem("sig_ready"), sem("h_ready"), sem("final_ready"), sem("o_gated")
        gk_w, gk_sum, gk_in, gk_log = sem("gk_w"), sem("gk_sum"), sem("gk_in"), sem("gk_log")
        vtok_sum, vtok_ready = sem("vtok_sum"), sem("vtok_ready")
        dec_in, dec_exp, lev_ready, lev_sum, lev_done = (sem("dec_in"), sem("dec_exp"), sem("lev_ready"),
                                                         sem("lev_sum"), sem("lev_done"))
        ktok_in, ktok_sum, ktok_ready = sem("ktok_in"), sem("ktok_sum"), sem("ktok_ready")
        gla_o, gla_o_free, st_sum, st_ready = sem("gla_o"), sem("gla_o_free"), sem("st_sum"), sem("st_ready")
        on_sq, on_sum, on_ms, on_root = sem("on_sq"), sem("on_sum"), sem("on_ms"), sem("on_root")

        block = ctx.enter_context(nc.Block())

        def task(hd, i, mp, diff):
            if diff:
                return hd.times(2 * NQT) + (2 * i + mp)
            return hd.times(NQT) + (DIFF_HEADS * NQT + i)

        def state_c(c):
            return state[:, c % 2]

        def half_cols(half):
            return slice(half * HALF, (half + 1) * HALF)

        @block.sync
        def _(sp):
            def load_panel(p):
                if not (isinstance(p.at(), int) and p.at() < 2):
                    sp.wait_ge(w_lo_ready, p.at(-1))
                sp.dma_start(wraw[:, p.parity].rearrange("p k m -> p (k m)"),
                             panels[p.cols(1)].rearrange("a p n -> p (a n)")).then_inc(w_loaded[p.parity], 16)

            def load_panels(first, count):
                if count % 2:
                    load_panel(Idx(first))
                    first, count = first + 1, count - 1
                with sp.Fori(0, count // 2) as i:
                    for s in range(2):
                        load_panel(Idx(first + s, [(2, i)]))

            for layer, st in enumerate(PLAN):
                if layer == 0:
                    load_panel(Idx(0))
                    load_panel(Idx(1))
                    load_panels(2, PANELS_MIX - 2)
                else:
                    load_panels(st["mix"], PANELS_MIX)
                def wo_and_residual(o, first):
                    for s in range(2):
                        load_panel(o + (st["wo"] + s))
                    if first:
                        sp.wait_ge(x_lo_ready, st["x_o"] + 16)
                        if layer == 1:
                            sp.wait_ge(h_spilled, 16 * KT)
                    src = x_t if layer == 0 else h_dram
                    for s in range(2):
                        if not (first and layer == 0):
                            sp.wait_ge(h_loaded[s], (o.half() + 4 * layer).times(16).at())
                        sp.dma_start(h[:, (o + s).cols(1)].rearrange("p a n -> p (a n)"),
                                     src[(o + s).cols(1)].rearrange("a p n -> p (a n)")).then_inc(h_loaded[s], 16)

                wo_and_residual(Idx(0), True)
                with sp.Fori(1, KT // 2) as i:
                    wo_and_residual(Idx(0, [(2, i)]), False)
                load_panels(st["mlp"], PANELS_MLP + 4 + KT)
            for o in range(KT):
                sp.wait_ge(final_ready, o + 1)
                sp.dma_start(out_t[o], h[:, o]).then_inc(out_stored, 16)
            sp.wait_ge(out_stored, 16 * KT)

        @block.tensor
        def _(pe):
            def product(out, hi_w, lo_w, hi_x, lo_x, start, stop):
                nc.tensor.matmul(out, hi_w, hi_x, start=start, stop=False, skip_group_check=True)
                nc.tensor.matmul(out, hi_w, lo_x, start=False, stop=False, skip_group_check=True)
                return nc.tensor.matmul(out, lo_w, hi_x, start=False, stop=stop, skip_group_check=True)

            def norm_sums(n):
                pe.wait_ge(sq_added, 16 * (n + 1))
                for half in range(2):
                    nc.tensor.matmul(s_ps[:, 0, half_cols(half)], ones[:], sumsq[:, half], start=True,
                                     stop=True).then_inc(norm_sum, 1)

            def unit(p, half, hi, lo, x_base=None, k_order=range(KT), part=None):
                s, u = p.parity, p.times(2) + half
                if not part:
                    if half == 0:
                        pe.wait_ge(w_lo_ready, p.at(1))
                    if not (isinstance(u.at(), int) and u.at() < 2):
                        pe.wait_ge(unit_free, u.at(-1))
                for n, k in enumerate(k_order):
                    if part is not None and n * PIECES // KT != part:
                        continue
                    if x_base is not None:
                        pe.wait_ge(x_lo_ready, x_base.at(2 * n + half + 1))
                    last = product(gemm_ps[:, half], whi[:, s, k], wlo[:, s, k],
                                   hi[:, k, half_cols(half)], lo[:, k, half_cols(half)], n == 0, n == KT - 1)
                if part in (None, PIECES - 1):
                    last.then_inc(unit_ready, 1)

            def panel(p, hi, lo, x_base=None, norm=None, k_order=range(KT)):
                for half in range(2):
                    unit(p, half, hi, lo, x_base, k_order)
                    if norm is not None and half == 0:
                        norm_sums(norm)

            def filler(share, first):
                done = [0]

                def fill(point):
                    for _ in range(share.counts[point]):
                        u, part = divmod(done[0], PIECES)
                        unit(first + u // 2, u % 2, a_hi, a_lo, part=part)
                        done[0] += 1
                return fill

            def stage(p, count, hi, lo, x_base=None, norm=None, k_order=range(KT)):
                if x_base is not None:
                    for s in range(2):
                        panel(p + s, hi, lo, x_base if s == 0 else None, norm if s == 0 else None,
                              k_order if s == 0 else range(KT))
                    p, count = p + 2, count - 2
                with pe.Fori(0, count // 2) as i:
                    for s in range(2):
                        panel(p + Idx(s, [(2, i)]), hi, lo)

            def attention(hd, diff, share):
                maps = 2 if diff else 1
                fill = filler(share, hd.times(3) + (PLAN[0]["heads"] + 3))

                def scores(i, mp):
                    keys = (i + 1) * P
                    bank_pair = mp if diff else i % 2
                    r = slice(64 * mp, 64 * mp + 64) if diff else slice(0, P)
                    for c0 in range(0, keys, HALF):
                        c1 = min(keys, c0 + HALF)
                        out = s_ps[:, bank_pair, c0:c1]
                        product(out, q_hi[r, i * P:(i + 1) * P], q_lo[r, i * P:(i + 1) * P],
                                k_hi[r, c0:c1], k_lo[r, c0:c1], True, False)
                        if not diff:
                            for cm in (cm_hi, cm_lo):
                                nc.tensor.matmul(out, negones_r[:], cm[0:DIFF_HEADS, c0:c1], start=False,
                                                 stop=False, skip_group_check=True)
                    nc.tensor.matmul(s_ps[:, bank_pair, i * P:keys], ident_r[:], mask_r[:], start=False,
                                     stop=True, skip_group_check=True).then_inc(scores_ready, 1)

                def transposes(i, done, between):
                    pe.wait_ge(w_ready, hd.times(NQT).at(i + 1))
                    for g in range(GROUPS[i]):
                        if g == 1:
                            between()
                        if i == 0:
                            pe.wait_ge(v_lo_ready, hd.at(1))
                        else:
                            pe.wait_ge(tr_lo, hd.times(GROUPS_HEAD).at(done + g))
                        for j in range(4 * g, min(4 * g + 4, i + 1)):
                            last = nc.tensor.transpose(to_ps[:, (j - 4 * g) * P:(j - 4 * g + 1) * P],
                                                       prob[:, 1 if diff else i % 2, j * P:(j + 1) * P], ident[:])
                        last.then_inc(tr_ready, 1)

                def values(c):
                    pe.wait_ge(tr_lo, hd.times(GROUPS_HEAD).at(sum(GROUPS[:2 * c + 2])))
                    pe.wait_ge(o_evacuated, hd.times(4).at(c + 1))
                    for j in range(2 * c + 2):
                        q0 = P if j == 2 * c + 1 else 0
                        last = product(to_ps[:, HALF + q0:HALF + 256], v_hi[:, j], v_lo[:, j],
                                       pt_hi[:, j, q0:256], pt_lo[:, j, q0:256], j == 0, j == 2 * c + 1)
                    last.then_inc(pv_ready, 1)

                pe.wait_ge(qk_lo_ready, hd.times(2).at(2))
                if not diff:
                    pe.wait_ge(cm_lo_ready, hd.at(1 - DIFF_HEADS))
                for mp in range(maps):
                    scores(0, mp)
                fill(0)
                pe.wait_ge(unit_free, hd.times(6).at(8))
                pe.wait_ge(o_evacuated, hd.times(4).at(1))
                for t in range(NQT):
                    last = nc.tensor.transpose(to_ps[:, t * P:(t + 1) * P], v_t[:, t * P:(t + 1) * P], ident[:])
                last.then_inc(vt_ready, 1)
                fill(1)
                for i in range(NQT):
                    for mp in range(2):
                        if i + 1 < NQT and mp < maps:
                            if diff:
                                pe.wait_ge(exp_ready, task(hd, i, mp, diff).at(1))
                            elif i >= 1:
                                pe.wait_ge(exp_ready, task(hd, i - 1, 0, diff).at(1))
                            if not diff and i == 3:
                                pe.wait_ge(sub_ms, hd.at(1 - SUB_LAG))
                            scores(i + 1, mp)
                        fill(4 * i + mp + 2)
                    if i >= 2 and i % 2 == 0:
                        values(i // 2 - 1)
                    if not diff and i == 1:
                        pe.wait_ge(sub_sq, hd.at(1 - SUB_LAG))
                        for half in range(2):
                            last = nc.tensor.matmul(s_ps[:, half, HALF:SEQ], ones[:], v_t[:, half_cols(half)],
                                                    start=True, stop=True)
                        last.then_inc(sub_sum, 1)
                    transposes(i, sum(GROUPS[:i]), lambda: fill(4 * i + 4))
                    fill(4 * i + 5)
                values(3)

            def gk_sums(hd):
                pe.wait_ge(gk_w, hd.at(1))
                for half in range(2):
                    last = nc.tensor.matmul(to_ps[:, half_cols(half)], wgk_h[:], gl_t[0:LOWRANK, half_cols(half)],
                                            start=True, stop=True)
                last.then_inc(gk_sum, 1)

            def gla_head(hd, share, first, v_panel, following):
                fill = filler(share, first)
                pe.wait_ge(unit_free, v_panel.times(2).at(2))
                if share.units != 8:
                    pe.wait_ge(on_ms, hd.at())
                for t in range(2):
                    for c in range(NQT):
                        last = nc.tensor.transpose(s_ps[:, t, c * P:(c + 1) * P], vg_t[:, t, c * P:(c + 1) * P], ident[:])
                last.then_inc(vtok_sum, 1)
                fill(0)
                pe.wait_ge(vtok_ready, hd.at(1))
                for lv in range(LEVELS + 1):
                    n = hd.times(LEVELS + 1)
                    if lv < LEVELS:
                        pe.wait_ge(lev_ready, hd.times(LEVELS).at(lv + 1))
                    if lv >= 2:
                        pe.wait_ge(lev_done, n.at(lv - 1))
                    for c in range(NQT):
                        cs = slice(c * P, (c + 1) * P)
                        kk, qq = (lev, lev) if lv < LEVELS else (k_t, q_t)
                        last = nc.tensor.matmul(s_ps[:, lv % 2, cs], kk[:, cs], qq[:, cs], start=True, stop=True)
                    last.then_inc(lev_sum, 1)
                    fill(1 + lv)
                fill(9)
                pe.wait_ge(ktok_in, hd.at(1))
                for c in range(NQT):
                    cs = slice(c * P, (c + 1) * P)
                    last = nc.tensor.transpose(to_ps[:, cs], k_dec[:, cs], ident[:])
                last.then_inc(ktok_sum, 1)
                fill(10)
                pe.wait_ge(ktok_ready, hd.at(1))
                pe.wait_ge(lev_done, hd.times(LEVELS + 1).at(LEVELS + 1))
                for c in range(NQT):
                    cs = slice(c * P, (c + 1) * P)
                    if c >= 1:
                        pe.wait_ge(st_ready, hd.times(NQT - 1).at(c))
                    if c < NQT - 1:
                        nc.tensor.matmul(to_ps[:, 0:DV], k_tok[:, cs], v_tok[:, c], start=True,
                                         stop=True).then_inc(st_sum, 1)
                    if c >= 2:
                        pe.wait_ge(gla_o_free, hd.times(NQT).at(c - 1))
                    for t in range(2):
                        out = s_ps[:, c % 2, t * P:(t + 1) * P]
                        last = nc.tensor.matmul(out, v_tok[:, c, t * P:(t + 1) * P], att[:, cs], start=True,
                                                stop=(c == 0))
                        if c >= 1:
                            last = nc.tensor.matmul(out, state_c(c - 1)[:, t * P:(t + 1) * P], q_dec[:, cs],
                                                    start=False, stop=True)
                    last.then_inc(gla_o, 1)
                    fill(11 + c)
                if following:
                    gk_sums(hd + 1)
                fill(19)
                pe.wait_ge(on_sq, hd.at(1))
                for half in range(2):
                    for t, sq in enumerate((dec, lev)):
                        last = nc.tensor.matmul(s_ps[:, 0, half_cols(half)], ones[:], sq[:, half_cols(half)],
                                                start=(t == 0), stop=(t == 1))
                last.then_inc(on_sum, 1)
                fill(20)

            def rest_of_layer(layer):
                st = PLAN[layer]
                stage(Idx(st["wo"]), KT, a_hi, a_lo, Idx(st["x_o"]), k_order=O_ORDER if layer == 0 else range(KT))

                def ff_chunk(c, first):
                    p = c.times(2 * KT) + st["mlp"]
                    if first:
                        stage(p, KT, b_hi, b_lo, Idx(st["x_mlp"]), st["norm"] + 1)
                    else:
                        stage(p, KT, b_hi, b_lo)
                    stage(p + KT, KT, a_hi, a_lo, c.times(16) + st["x_hid"])

                ff_chunk(Idx(0), True)
                with pe.Fori(1, CHUNKS) as c:
                    ff_chunk(Idx(0, [(1, c)]), False)
                panel(Idx(st["gate"]), b_hi, b_lo, Idx(st["x_ple"]), st["norm"] + 2)
                for j in range(4):
                    p = st["ple"] + j
                    s = p % 2
                    pe.wait_ge(w_lo_ready, p + 1)
                    if j == 0:
                        pe.wait_ge(p_lo_ready, layer + 1)
                        pe.wait_ge(norm_ms, 2 * (st["norm"] + 3))
                    half = j // 2
                    wh = whi[:, s].rearrange("p k m -> p (k m)")
                    wl = wlo[:, s].rearrange("p k m -> p (k m)")
                    for e in range(2):
                        pe.wait_ge(unit_free, 2 * p + e - 1)
                        for b in range(2):
                            for k in range(2):
                                o = k * HALF + (2 * e + b) * P
                                last = product(s_ps[:, e, half_cols(b)], wh[:, o:o + P], wl[:, o:o + P],
                                               a_hi[:, 4 + k, half_cols(half)], a_hi[:, 6 + k, half_cols(half)],
                                               k == 0, k == 1)
                        last.then_inc(unit_ready, 1)
                panel(Idx(st["gate"] + 5), b_hi, b_lo)
                stage(Idx(st["gate"] + 6), KT - 2, b_hi, b_lo)

            st = PLAN[0]
            pe.wait_ge(const_ready, 1)
            pe.wait_ge(gp_const, 1)
            panel(Idx(st["mix"]), a_hi, a_lo, Idx(st["x_mix"]), st["norm"])
            pe.wait_ge(ph_ready, 1)
            for j in range(3):
                panel(Idx(st["heads"] + j), a_hi, a_lo)
            with pe.Fori(0, DIFF_HEADS // 2) as i:
                for e in range(2):
                    attention(Idx(e, [(2, i)]), True, ATT_SHARE)
            for hd in range(DIFF_HEADS, HEADS):
                attention(Idx(hd), False, ATT_SHARE if hd < HEADS - 1 else NO_SHARE)
            rest_of_layer(0)
            st = PLAN[1]
            panel(Idx(st["mix"]), a_hi, a_lo, Idx(st["x_mix"]), st["norm"])
            gk_sums(Idx(0))
            p = Idx(st["heads"])
            for j in range(4):
                panel(p + j, a_hi, a_lo)
            gla_head(Idx(0), GLA_SHARE[8], p + 4, p + 1, True)
            with pe.Fori(1, GLA_HEADS - 1) as i:
                hd = Idx(0, [(1, i)])
                gla_head(hd, GLA_SHARE[12], hd.times(6) + (st["heads"] + 2), hd.times(6) + (st["heads"] - 1), True)
            gla_head(Idx(3), GLA_SHARE[4], Idx(st["heads"] + 20), Idx(st["heads"] + 17), False)
            for j in range(2):
                panel(Idx(st["heads"] + 22 + j), a_hi, a_lo)
            rest_of_layer(1)
            norm_sums(6)

        @block.gpsimd
        def _(gp):
            steps = Chain(gp, g_step)
            gp.dma_start(gcol[:], gains).then_inc(const_loaded, 16)
            gp.dma_start(colc[:, GSUB:GSUB + 1], g_sub).then_inc(const_loaded, 16)
            gp.dma_start(colc[0:DIFF_HEADS, BF:BF + 1], b_f).then_inc(const_loaded, 16)
            gp.dma_start(colc[:, BGK:BGK + GLA_HEADS], b_gk).then_inc(const_loaded, 16)
            gp.dma_start(colc[:, GON:GON + 2], g_on).then_inc(const_loaded, 16)
            gp.dma_start(wgk_all[:], w_gk).then_inc(const_loaded, 16)
            gp.dma_start(lam_in, lam_vec.rearrange("a n -> (a n)").partition_broadcast(P)).then_inc(const_loaded, 16)
            steps.link(nc.gpsimd.memset(ident[:], 0.0))
            steps.link(nc.gpsimd.affine_select(out=ident[:], in_=ident[:], compare_op=ALU.not_equal, fill=1.0,
                                               base=0, pattern=[[-1, P]], channel_multiplier=1))
            steps.link(nc.gpsimd.memset(mask_f, 0.0))
            nc.gpsimd.affine_select(out=mask_f, in_=mask_f, compare_op=ALU.is_ge, fill=MASKED,
                                    base=0, pattern=[[-1, P]], channel_multiplier=1).then_inc(gp_const, 1)

            def add_squares(n, o, half):
                a = o.times(2) + (16 * n + half)
                gp.wait_ge(sq_ready, a.at(1))
                return a

            def tile_squares(n, o, first):
                for half in range(2):
                    a = add_squares(n, o, half)
                    if first:
                        if n >= 1:
                            gp.wait_ge(norm_sum, 2 * n)
                        nc.gpsimd.tensor_copy(sumsq[:, half], zs[:, half]).then_inc(sq_added, 1)
                    else:
                        gp.wait_ge(sq_added, a.at(-1))
                        nc.gpsimd.tensor_tensor(sumsq[:, half], sumsq[:, half], zs[:, half],
                                                ALU.add).then_inc(sq_added, 1)

            def all_squares(n, after=None):
                tile_squares(n, Idx(0), True)
                if after:
                    after(Idx(0))
                with gp.Fori(1, KT) as o:
                    tile_squares(n, Idx(0, [(1, o)]), False)
                    if after:
                        after(Idx(0, [(1, o)]))

            all_squares(0)
            for lv in range(LEVELS):
                half_block = 64 >> lv
                v = lmask_built[:, lv].rearrange("p (b n) -> p b n", n=2 * half_block)
                nb = P // (2 * half_block)
                steps.link(nc.gpsimd.memset(v, 1.0))
                steps.link(nc.gpsimd.memset(v[:, :, 0:half_block], 0.0))
                steps.link(nc.gpsimd.affine_select(out=v, in_=v, compare_op=ALU.is_ge, fill=0.0, base=0,
                                                   pattern=[[-2 * half_block, nb], [0, 2 * half_block]],
                                                   channel_multiplier=1))
                steps.link(nc.gpsimd.affine_select(out=v, in_=v, compare_op=ALU.is_ge, fill=0.0,
                                                   base=half_block - 1,
                                                   pattern=[[2 * half_block, nb], [0, 2 * half_block]],
                                                   channel_multiplier=-1))
            steps.link(nc.gpsimd.tensor_copy(lmask_built[:, LEVELS], ident[:]))
            gp.dma_start(m_dram, lmask_built[:].rearrange("p a n -> p (a n)")).then_inc(masks_stored, 16)
            for layer, st in enumerate(PLAN):
                if layer == 1:
                    gp.wait_ge(h_spilled, 16 * KT)
                    gp.wait_ge(x_lo_ready, st["x_mix"] + 16)
                    gp.wait_ge(masks_stored, 16)
                    gp.dma_start(lmask[:].rearrange("p a n -> p (a n)"), m_dram).then_inc(masks_loaded, 16)
                all_squares(st["norm"] + 1)
                all_squares(st["norm"] + 2)
                gp.wait_ge(unit_ready, 2 * st["gate"])
                gp.dma_start(p_raw[:], p_t[layer].rearrange("k p n -> p k n")).then_inc(p_loaded, 16)

                def spill(o):
                    gp.wait_ge(h_ready, o.times(2).at(2))
                    gp.dma_start(h_dram[o.cols(1)].rearrange("a p n -> p (a n)"),
                                 h[:, o.cols(1)].rearrange("p a n -> p (a n)")).then_inc(h_spilled, 16)

                all_squares(st["norm"] + 3, spill if layer == 0 else None)

        @block.scalar
        def _(act):
            steps = Chain(act, a_step)
            A = nc.scalar.activation
            eps = colc[:, EPSC:EPSC + 1]

            def w_hi(p):
                if p.at() is not None and isinstance(p.at(), int) and p.at() >= PANELS:
                    return
                act.wait_ge(w_loaded[p.parity], p.half().times(16).at(16))
                if not (isinstance(p.at(), int) and p.at() < 2):
                    act.wait_ge(unit_ready, p.times(2).at(-2))
                A(whi[:, p.parity], wraw[:, p.parity], ACT.Copy).then_inc(w_hi_ready, 1)

            def finish(n, o, half, next_hi):
                a = o.times(2) + (16 * n + half)
                src = h[:, o.cols(1), half_cols(half)].rearrange("p a n -> p (a n)")
                if not (isinstance(a.at(), int) and a.at() < 2):
                    act.wait_ge(sq_added, a.at(-1))
                A(zs[:, half], src, ACT.Square).then_inc(sq_ready, 1)
                if next_hi is not None:
                    A(next_hi[:, o.cols(1), half_cols(half)].rearrange("p a n -> p (a n)"), src, ACT.Copy,
                      scale=gcol[:, o.cols(1, add=KT * n)]).then_inc(x_hi_ready, 1)

            def norm_root_of(n):
                for half in range(2):
                    act.wait_ge(norm_sum, 2 * n + half + 1)
                    r = rstd[:, half_cols(half)]
                    A(r, s_ps[:, 0, half_cols(half)], ACT.Ln, scale=1.0 / D, bias=eps).then_inc(norm_ms, 1)
                for half in range(2):
                    act.wait_ge(norm_ms, 2 * n + half + 1)
                    r = rstd[:, half_cols(half)]
                    A(r, r, ACT.Exp, scale=-0.5).then_inc(norm_root, 1)

            def taker(share, first, work):
                taken = [0]

                def take(point):
                    for u in range(taken[0], share.complete(point)):
                        work(first + u // 2, u)
                        taken[0] += 1
                return take

            def split_qk(hd):
                act.wait_ge(unit_free, hd.times(6).at(6))
                A(q_hi[:], q_raw[:], ACT.Copy).then_inc(qk_hi_ready, 1)
                A(k_hi[:], k_raw[:], ACT.Copy).then_inc(qk_hi_ready, 1)

            def split_gates(hd):
                A(cm_hi[0:DIFF_HEADS], c_row[0:DIFF_HEADS], ACT.Copy,
                  scale=ident[0:DIFF_HEADS, hd.cols(1, add=-DIFF_HEADS)]).then_inc(cm_hi_ready, 1)

            def split_o(src, o):
                for half in range(2):
                    A(a_hi[:, o.cols(1), half_cols(half)].rearrange("p a n -> p (a n)"),
                      src[:, o.cols(1), half_cols(half)].rearrange("p a n -> p (a n)"),
                      ACT.Copy).then_inc(x_hi_ready, 1)

            def attention(hd, diff, share, following):
                maps = 2 if diff else 1
                last_head = share is NO_SHARE

                def next_weights(p, u):
                    if u % 2:
                        w_hi(p + 2)

                take = taker(share, hd.times(3) + (PLAN[0]["heads"] + 3), next_weights)

                def exps(i, mp):
                    n = (i + 1) * P
                    act.wait_ge(negmax_ready, task(hd, i, mp, diff).at(1))
                    pair = mp if diff else i % 2
                    c = 2 * (i % 2) + mp
                    A(prob[:, pair, 0:n], s_ps[:, pair, 0:n], ACT.Exp, bias=colc[:, NEG + c:NEG + c + 1],
                      accum_out=colc[:, L + c:L + c + 1]).then_inc(exp_ready, 1)

                for mp in range(maps):
                    exps(0, mp)
                act.wait_ge(vt_ready, hd.at(1))
                A(v_hi[:].rearrange("p a n -> p (a n)"), to_ps[:], ACT.Copy).then_inc(v_hi_ready, 1)
                if not diff:
                    A(v_t[:], o_raw[:, hd.cols(1, scale=1, add=-SUB_LAG)].rearrange("p a n -> p (a n)"),
                      ACT.Square).then_inc(sub_sq, 1)
                if last_head:
                    act.wait_ge(unit_ready, 2 * PLAN[0]["wo"])
                done = 0
                for i in range(NQT):
                    if diff:
                        n, c = (i + 1) * P, C2 + 2 * (i % 2) + 1
                        act.wait_ge(coef_ready, hd.times(NQT).at(i + 1))
                        A(prob[:, 1, 0:n], prob[:, 1, 0:n], ACT.Copy, scale=colc[:, c:c + 1]).then_inc(scaled_ready, 1)
                    if i + 1 < NQT:
                        if diff:
                            act.wait_ge(w_ready, hd.times(NQT).at(i + 1))
                        exps(i + 1, 0)
                    take(4 * i + 2)
                    if i == 2 and not diff:
                        act.wait_ge(sub_sum, hd.at(1 - SUB_LAG))
                        A(v_t[:].rearrange("p (t n) -> p t n", t=2), s_ps[:, :, HALF:SEQ], ACT.Ln, scale=1.0 / P,
                          bias=eps).then_inc(sub_ms, 1)
                        act.wait_ge(sub_ms, hd.at(1 - SUB_LAG))
                        A(v_t[:], v_t[:], ACT.Exp, scale=-0.5).then_inc(sub_root, 1)
                    if i + 1 == NQT and following:
                        split_qk(hd + 1)
                        if not diff:
                            split_gates(hd + 1)
                    if i % 2 == 0 and i >= 2:
                        act.wait_ge(pv_ready, hd.times(4).at(i // 2))
                    for g in range(GROUPS[i]):
                        n = min(4, i + 1 - 4 * g)
                        act.wait_ge(tr_ready, hd.times(GROUPS_HEAD).at(done + 1))
                        A(pt_hi[:, 4 * g:4 * g + n, (i % 2) * P:(i % 2 + 1) * P],
                          to_ps[:, 0:n * P].rearrange("p (j q) -> p j q", q=P), ACT.Copy).then_inc(tr_hi, 1)
                        done += 1
                    if diff and i + 1 < NQT:
                        exps(i + 1, 1)
                    if last_head and i < KT - 1:
                        if O_ORDER[i] == DIFF_HEADS - 1:
                            act.wait_ge(sub_done, DIFF_HEADS)
                        split_o(o_raw, Idx(O_ORDER[i]))
                take(len(share.counts))
                if last_head:
                    act.wait_ge(o_evacuated, 4 * HEADS + 1)
                    split_o(o_raw, Idx(O_ORDER[KT - 1]))

            def log_sigmoid_part(x, t):
                steps.link(A(t, x, ACT.Abs))
                steps.link(A(t, t, ACT.Exp, scale=-1.0))
                return A(t, t, ACT.Ln, bias=colc[0:x.shape[0], ONE:ONE + 1])

            def gk_logs(hd):
                act.wait_ge(gk_in, hd.at(1))
                log_sigmoid_part(b_cum[:], q_dec[:]).then_inc(gk_log, 1)

            def output_gate(p):
                for half in range(2):
                    act.wait_ge(unit_free, p.times(2).at(half + 1))
                    A(zs[:, half], zt[:, half], ACT.Sigmoid).then_inc(sig_ready, 1)

            def gla_head(hd, share, first, following):
                def unit_work(p, u):
                    if u % 2:
                        if share.units != 8 and u < 4:
                            output_gate(p)
                        w_hi(p + 2)

                take = taker(share, first, unit_work)
                act.wait_ge(vtok_sum, hd.at(1))
                for t in range(2):
                    last = A(v_tok[:, :, t * P:(t + 1) * P], s_ps[:, t].rearrange("p (c n) -> p c n", n=P), ACT.Copy)
                last.then_inc(vtok_ready, 1)
                for e in range(LEVELS + 2):
                    act.wait_ge(dec_in, hd.times(LEVELS + 2).at(e + 1))
                    if e == LEVELS:
                        A(dec[:], b_cum[:], ACT.Exp)
                        A(colc[:, EB:EB + NQT], b_cum[:, P - 1:SEQ:P], ACT.Exp).then_inc(dec_exp, 1)
                    else:
                        A(dec[:], dec[:], ACT.Exp).then_inc(dec_exp, 1)
                    if e < LEVELS:
                        take(1 + e)
                act.wait_ge(ktok_sum, hd.at(1))
                A(k_tok[:], to_ps[:], ACT.Copy).then_inc(ktok_ready, 1)
                for c in range(NQT):
                    take(11 + c)
                take(19)
                act.wait_ge(gla_o_free, hd.times(NQT).at(NQT))
                for t, dst in enumerate((dec, lev)):
                    last = A(dst[:], o_raw1[:, (hd.times(2) + t).cols(1)].rearrange("p a n -> p (a n)"), ACT.Square)
                last.then_inc(on_sq, 1)
                if following:
                    gk_logs(hd + 1)
                take(20)
                act.wait_ge(on_sum, hd.at(1))
                A(dec[:], s_ps[:, 0], ACT.Ln, scale=1.0 / DV, bias=eps).then_inc(on_ms, 1)
                act.wait_ge(on_ms, hd.at(1))
                A(dec[:], dec[:], ACT.Exp, scale=-0.5).then_inc(on_root, 1)
                take(len(share.counts))

            def pairs(count, body):
                with act.Fori(0, count // 2) as i:
                    for s in range(2):
                        body(Idx(s, [(2, i)]))

            def rest_of_layer(layer):
                st = PLAN[layer]
                if layer == 1:
                    act.wait_ge(unit_ready, 2 * st["wo"])
                    act.wait_ge(o_gated, 1)
                    pairs(KT, lambda o: split_o(o_raw1, o))

                def wo(o):
                    for half in range(2):
                        act.wait_ge(unit_free, (o + st["wo"]).times(2).at(half + 1))
                        finish(st["norm"] + 1, o, half, b_hi)
                    w_hi(o + (st["wo"] + 2))

                pairs(KT, wo)
                norm_root_of(st["norm"] + 1)

                def ff_chunk(c, last_chunk):
                    p = c.times(2 * KT) + st["mlp"]

                    def up(o):
                        for half in range(2):
                            act.wait_ge(unit_free, (p + o).times(2).at(half + 1))
                            A(zs[:, half], zt[:, half], ACT.Square)
                            A(a_hi[:, o.cols(1), half_cols(half)].rearrange("p a n -> p (a n)"), zt[:, half],
                              ACT.Square).then_inc(x_hi_ready, 1)
                        w_hi(p + (o + 2))

                    def down(o):
                        if last_chunk:
                            for half in range(2):
                                act.wait_ge(unit_free, (p + (o + KT)).times(2).at(half + 1))
                                finish(st["norm"] + 2, o, half, b_hi)
                        w_hi(p + (o + KT + 2))

                    pairs(KT, up)
                    pairs(KT, down)

                with act.Fori(0, CHUNKS - 1) as c:
                    ff_chunk(Idx(0, [(1, c)]), False)
                ff_chunk(Idx(CHUNKS - 1), True)
                norm_root_of(st["norm"] + 2)

                def sigmoid(p, o, half):
                    act.wait_ge(unit_free, p.times(2).at(half + 1))
                    act.wait_ge(sq_added, (o.times(2) + (16 * (st["norm"] + 3) + half)).at(-1))
                    A(zs[:, half], zt[:, half], ACT.Sigmoid).then_inc(sig_ready, 1)

                def finish_gated(o, half):
                    act.wait_ge(h_ready, o.times(2).at(16 * layer + half + 1))
                    finish(st["norm"] + 3, o, half, a_hi if layer == 0 else None)

                def gate(o):
                    p = o + (st["gate"] + 4)
                    for half in range(2):
                        sigmoid(p, o, half)
                        finish_gated(o, half)
                    w_hi(p + 2)

                act.wait_ge(p_loaded, 16 * (layer + 1))
                A(a_hi[:, 4:6], p_raw[:], ACT.Copy).then_inc(p_hi_ready, 1)
                for half in range(2):
                    sigmoid(Idx(st["gate"]), Idx(0), half)
                for j in range(5):
                    w_hi(Idx(st["gate"] + 2 + j))
                for half in range(2):
                    finish_gated(Idx(0), half)
                gate(Idx(1))
                with act.Fori(1, KT // 2 - 1) as i:
                    for s in range(2):
                        gate(Idx(s, [(2, i)]))
                for o in (KT - 2, KT - 1):
                    gate(Idx(o))
                norm_root_of(st["norm"] + 3)

            for o in range(KT):
                act.dma_start(h[:, o], x_t[o]).then_inc(x_loaded[o], 16)
            act.wait_ge(const_loaded, 16 * 7)
            act.wait_ge(gp_const, 1)
            A(ident_r[:], ident[:], ACT.Copy)
            A(mask_r[:], mask_f, ACT.Copy)
            act.wait_ge(const_ready, 2)
            A(negones_r[:], ones[0:DIFF_HEADS], ACT.Copy, scale=-1.0).then_inc(ph_ready, 1)
            A(colc[:, LAM1:LAM1 + 2], colc[:, LAM1:LAM1 + 2], ACT.Exp).then_inc(lam_exp, 1)
            w_hi(Idx(0))
            for o in range(KT):
                act.wait_ge(x_loaded[o], 16)
                for half in range(2):
                    finish(0, Idx(o), half, a_hi)
            w_hi(Idx(1))
            norm_root_of(0)
            for p in range(2, 6):
                w_hi(Idx(p))
            split_qk(Idx(0))
            act.wait_ge(fl_ready, 1)
            log_sigmoid_part(prob[0:DIFF_HEADS, 0], prob[0:DIFF_HEADS, 1]).then_inc(fl_log, 1)
            with act.Fori(0, DIFF_HEADS // 2) as i:
                for e in range(2):
                    attention(Idx(e, [(2, i)]), True, ATT_SHARE, True)
            split_gates(Idx(DIFF_HEADS))
            for hd in range(DIFF_HEADS, HEADS):
                attention(Idx(hd), False, ATT_SHARE if hd < HEADS - 1 else NO_SHARE, hd < HEADS - 1)
            rest_of_layer(0)
            st = PLAN[1]
            w_hi(Idx(st["mix"] + 2))
            gk_logs(Idx(0))
            for j in range(4):
                w_hi(Idx(st["heads"] + 2 + j))
            gla_head(Idx(0), GLA_SHARE[8], Idx(st["heads"] + 4), True)
            with act.Fori(1, GLA_HEADS - 1) as i:
                hd = Idx(0, [(1, i)])
                steps.enter(i, 2, 1)
                gla_head(hd, GLA_SHARE[12], hd.times(6) + (st["heads"] + 2), True)
                steps.leave(GLA_HEADS - 2, 2)
            gla_head(Idx(3), GLA_SHARE[4], Idx(st["heads"] + 20), False)
            for j in range(2):
                output_gate(Idx(st["heads"] + 22 + j))
                w_hi(Idx(st["heads"] + 24 + j))
            rest_of_layer(1)

        @block.vector
        def _(dve):
            steps = Chain(dve, v_step)
            V = nc.vector

            def w_lo(p):
                if isinstance(p.at(), int) and p.at() >= PANELS:
                    return
                dve.wait_ge(w_hi_ready, p.at(1))
                V.tensor_tensor(wlo[:, p.parity], wraw[:, p.parity], whi[:, p.parity],
                                ALU.subtract).then_inc(w_lo_ready, 1)

            def tile_of(t, o, half):
                return t[:, o.cols(1), half_cols(half)].rearrange("p a n -> p (a n)")

            def split_lo(n, o, half, x, hi, lo):
                dve.wait_ge(x_hi_ready, x.at(1))
                V.scalar_tensor_tensor(tile_of(lo, o, half), tile_of(h, o, half), gcol[:, o.cols(1, add=KT * n)],
                                       tile_of(hi, o, half), ALU.mult, ALU.subtract).then_inc(x_lo_ready, 1)

            def norm_scale(n):
                dve.wait_ge(norm_root, 2 * n + 2)

            def bank(half, rows=P):
                return gemm_ps[0:rows, half]

            def evacuate_raw(hd, u):
                p = hd.times(3) + (PLAN[0]["heads"] + u // 2)
                half = u % 2
                dve.wait_ge(unit_ready, p.times(2).at(half + 1))
                dst = (q_raw, k_raw, v_t)[u // 2][:, half_cols(half)]
                if u < 2:
                    V.scalar_tensor_tensor(dst, bank(half), colc[:, hd.cols(1, add=QS)],
                                           rstd[:, half_cols(half)], ALU.mult, ALU.mult).then_inc(unit_free, 1)
                else:
                    V.tensor_tensor(dst, bank(half), rstd[:, half_cols(half)], ALU.mult).then_inc(unit_free, 1)
                if half:
                    w_lo(p + 2)

            def split_qk(hd):
                for n, (raw, hi, lo) in enumerate(((q_raw, q_hi, q_lo), (k_raw, k_hi, k_lo))):
                    dve.wait_ge(qk_hi_ready, hd.times(2).at(n + 1))
                    V.tensor_tensor(lo[:], raw[:], hi[:], ALU.subtract).then_inc(qk_lo_ready, 1)

            def split_gates(hd):
                dve.wait_ge(cm_hi_ready, hd.at(1 - DIFF_HEADS))
                V.scalar_tensor_tensor(cm_lo[0:DIFF_HEADS], c_row[0:DIFF_HEADS],
                                       ident[0:DIFF_HEADS, hd.cols(1, add=-DIFF_HEADS)],
                                       cm_hi[0:DIFF_HEADS], ALU.mult, ALU.subtract).then_inc(cm_lo_ready, 1)

            def split_o(src, pos, o):
                for half in range(2):
                    dve.wait_ge(x_hi_ready, pos.times(2).at(half + 1))
                    V.tensor_tensor(tile_of(a_lo, o, half), tile_of(src, o, half), tile_of(a_hi, o, half),
                                    ALU.subtract).then_inc(x_lo_ready, 1)

            def taker(share, work):
                taken = [0]

                def take(point):
                    for u in range(taken[0], share.complete(point)):
                        work(u)
                        taken[0] += 1
                return take

            def attention(hd, diff, share, following):
                maps = 2 if diff else 1
                last_head = share is NO_SHARE
                take = taker(share, lambda u: evacuate_raw(hd + 1, u))
                x_o = Idx(PLAN[0]["x_o"] // 2)

                def negmax(i, mp):
                    n = (i + 1) * P
                    dve.wait_ge(scores_ready, task(hd, i, mp, diff).at(1))
                    c = NEG + 2 * (i % 2) + mp
                    V.tensor_reduce(colc[:, c:c + 1], s_ps[:, mp if diff else i % 2, 0:n], AX, ALU.max,
                                    negate=True).then_inc(negmax_ready, 1)

                def evacuate(c):
                    dve.wait_ge(pv_ready, hd.times(4).at(c + 1))
                    V.tensor_copy(o_raw[:, hd.cols(1), c * 256:(c + 1) * 256].rearrange("p a n -> p (a n)"),
                                  to_ps[:, HALF:HALF + 256]).then_inc(o_evacuated, 1)

                for mp in range(maps):
                    negmax(0, mp)
                dve.wait_ge(v_hi_ready, hd.at(1))
                V.tensor_tensor(v_lo[:].rearrange("p a n -> p (a n)"), to_ps[:], v_hi[:].rearrange("p a n -> p (a n)"),
                                ALU.subtract).then_inc(v_lo_ready, 1)
                done = 0
                for i in range(NQT):
                    n, c = (i + 1) * P, 2 * (i % 2)
                    dve.wait_ge(exp_ready, task(hd, i, maps - 1, diff).at(1))
                    steps.link(V.reciprocal(colc[:, RL + c:RL + c + maps], colc[:, L + c:L + c + maps]))
                    if diff:
                        V.tensor_tensor(colc[:, C2 + c:C2 + c + 2], colc[:, RL + c:RL + c + 2],
                                        colc[:, ONE:ONE + 2], ALU.mult).then_inc(coef_ready, 1)
                    else:
                        V.tensor_scalar(prob[:, i % 2, 0:n], prob[:, i % 2, 0:n], colc[:, RL + c:RL + c + 1], None,
                                        ALU.mult).then_inc(w_ready, 1)
                    if i + 1 < NQT:
                        negmax(i + 1, 0)
                    if diff:
                        dve.wait_ge(coef_ready, hd.times(NQT).at(i + 1))
                        dve.wait_ge(scaled_ready, hd.times(NQT).at(i + 1))
                        V.scalar_tensor_tensor(prob[:, 1, 0:n], prob[:, 0, 0:n], colc[:, C2 + c:C2 + c + 1],
                                               prob[:, 1, 0:n], ALU.mult, ALU.add).then_inc(w_ready, 1)
                        if i + 1 < NQT:
                            negmax(i + 1, 1)
                    take(4 * i + 2)
                    if i + 1 == NQT and following:
                        split_qk(hd + 1)
                        if not diff:
                            split_gates(hd + 1)
                    if i % 2 == 0 and i >= 2:
                        evacuate(i // 2 - 1)
                    for g in range(GROUPS[i]):
                        n = min(4, i + 1 - 4 * g)
                        done += 1
                        dve.wait_ge(tr_hi, hd.times(GROUPS_HEAD).at(done))
                        q = slice((i % 2) * P, (i % 2 + 1) * P)
                        V.tensor_tensor(pt_lo[:, 4 * g:4 * g + n, q],
                                        to_ps[:, 0:n * P].rearrange("p (j q) -> p j q", q=P),
                                        pt_hi[:, 4 * g:4 * g + n, q], ALU.subtract).then_inc(tr_lo, 1)
                    if not diff and i == 3:
                        dve.wait_ge(sub_root, hd.at(1 - SUB_LAG))
                        o = o_raw[:, hd.cols(1, add=-SUB_LAG)].rearrange("p a n -> p (a n)")
                        V.scalar_tensor_tensor(o, o, colc[:, GSUB:GSUB + 1], v_t[:], ALU.mult,
                                               ALU.mult).then_inc(sub_done, 1)
                    if last_head and i < KT - 1:
                        if O_ORDER[i] == DIFF_HEADS - 1:
                            dve.wait_ge(sub_done, DIFF_HEADS)
                        split_o(o_raw, x_o + i, Idx(O_ORDER[i]))
                evacuate(3)
                take(len(share.counts))
                if last_head:
                    dve.wait_ge(o_evacuated, 4 * HEADS + 1)
                    split_o(o_raw, x_o + (KT - 1), Idx(O_ORDER[KT - 1]))

            def log_sigmoid(x, t, scale):
                steps.link(V.scalar_tensor_tensor(t, x, 0.0, t, ALU.min, ALU.subtract))
                if scale != 1.0:
                    steps.link(V.tensor_scalar(t, t, scale, None, ALU.mult))

            def gk_cumulate(hd):
                dve.wait_ge(gk_log, hd.at(1))
                log_sigmoid(b_cum[:], q_dec[:], 1.0 / 16.0)
                steps.link(V.tensor_tensor_scan(b_cum[:], resets[:], q_dec[:], 0.0, ALU.mult, ALU.add))

            def gk_start(hd):
                dve.wait_ge(gk_sum, hd.at(1))
                V.tensor_scalar(b_cum[:], to_ps[:], colc[:, hd.cols(1, add=BGK)], None, ALU.add).then_inc(gk_in, 1)

            def evacuate_vqk(p, u):
                half = u % 2
                dst = (vg_t[:, 0], vg_t[:, 1], q_t[:], k_t[:])[u // 2][:, half_cols(half)]
                dve.wait_ge(unit_ready, p.times(2).at(half + 1))
                if u // 2 == 2:
                    V.scalar_tensor_tensor(dst, bank(half), DK ** -0.5, rstd[:, half_cols(half)], ALU.mult,
                                           ALU.mult).then_inc(unit_free, 1)
                else:
                    V.tensor_tensor(dst, bank(half), rstd[:, half_cols(half)], ALU.mult).then_inc(unit_free, 1)
                if half:
                    w_lo(p + 2)

            def evacuate_gate(hd, p, u):
                t, half = u // 2, u % 2
                dve.wait_ge(unit_ready, p.times(2).at(half + 1))
                V.tensor_tensor(zt[:, half], bank(half), rstd[:, half_cols(half)], ALU.mult).then_inc(unit_free, 1)
                if half:
                    for hf in range(2):
                        o = tile_of(o_raw1, hd.times(2) + t, hf)
                        dve.wait_ge(sig_ready, hd.times(4).at(SIG_MIX1 + 2 * t + hf + 1))
                        steps.link(V.tensor_tensor(zt[:, hf], zt[:, hf], zs[:, hf], ALU.mult))
                        steps.link(V.scalar_tensor_tensor(o, o, colc[:, GON + t:GON + t + 1], zt[:, hf],
                                                          ALU.mult, ALU.mult))
                    w_lo(p + 2)

            def gla_head(hd, share, first, following):
                gates = 0 if share.units == 8 else 4

                def unit_work(u):
                    p = first + u // 2
                    if u < gates:
                        evacuate_gate(hd + (-1), p, u)
                    else:
                        evacuate_vqk(p, u - gates)

                take = taker(share, unit_work)
                if following:
                    V.tensor_copy(wgk_h[:], wgk_all[:, (hd + 1).cols(DK)]).then_inc(gk_w, 1)

                def decays(lv):
                    hb = 64 >> lv
                    b = b_cum[:].rearrange("p (b n) -> p b n", n=2 * hb)
                    d = dec[:].rearrange("p (b n) -> p b n", n=2 * hb)
                    ref = b[:, :, hb - 1:hb].to_broadcast([P, SEQ // (2 * hb), hb])
                    V.tensor_tensor(d[:, :, 0:hb], ref, b[:, :, 0:hb], ALU.subtract)
                    V.tensor_tensor(d[:, :, hb:2 * hb], b[:, :, hb:2 * hb], ref, ALU.subtract).then_inc(dec_in, 1)

                def level(lv):
                    hb = 64 >> lv
                    dve.wait_ge(dec_exp, hd.times(LEVELS + 2).at(lv + 1))
                    if lv >= 1:
                        dve.wait_ge(lev_sum, hd.times(LEVELS + 1).at(lv))
                    d, t, kk, qq = (a[:].rearrange("p (b n) -> p b n", n=2 * hb) for a in (dec, lev, k_t, q_t))
                    V.tensor_tensor(t[:, :, 0:hb], d[:, :, 0:hb], kk[:, :, 0:hb], ALU.mult)
                    V.tensor_tensor(t[:, :, hb:2 * hb], d[:, :, hb:2 * hb], qq[:, :, hb:2 * hb],
                                    ALU.mult).then_inc(lev_ready, 1)
                    dve.wait_ge(lev_ready, hd.times(LEVELS).at(lv + 1))

                def place(lv):
                    dve.wait_ge(lev_sum, hd.times(LEVELS + 1).at(lv + 1))
                    if lv >= 1:
                        dve.wait_ge(lev_done, hd.times(LEVELS + 1).at(lv))
                    V.memset(colc[:, MARK + 2 + lv:MARK + 3 + lv], 0.0)
                    mask = lmask[:, lv:lv + 1].bitcast(I32).to_broadcast([P, NQT, P])
                    V.copy_predicated(att[:].rearrange("p (c n) -> p c n", n=P), mask,
                                      s_ps[:, lv % 2].rearrange("p (c n) -> p c n", n=P)).then_inc(lev_done, 1)

                decays(0)
                for lv in range(LEVELS):
                    level(lv)
                    if lv + 1 < LEVELS:
                        decays(lv + 1)
                    else:
                        V.memset(colc[:, MARK + 1:MARK + 2], 0.0).then_inc(dec_in, 1)
                    if lv >= 1:
                        place(lv - 1)
                    take(1 + lv)
                place(LEVELS - 1)
                dve.wait_ge(dec_exp, hd.times(LEVELS + 2).at(LEVELS + 1))
                steps.link(V.tensor_tensor(q_dec[:], q_t[:], dec[:], ALU.mult))
                b = b_cum[:].rearrange("p (c n) -> p c n", n=P)
                V.tensor_tensor(dec[:].rearrange("p (c n) -> p c n", n=P),
                                b[:, :, P - 1:P].to_broadcast([P, NQT, P]), b, ALU.subtract).then_inc(dec_in, 1)
                dve.wait_ge(dec_exp, hd.times(LEVELS + 2).at(LEVELS + 2))
                V.tensor_tensor(k_dec[:], k_t[:], dec[:], ALU.mult).then_inc(ktok_in, 1)
                place(LEVELS)
                for c in range(NQT):
                    take(11 + c)
                    if c < NQT - 1:
                        dve.wait_ge(st_sum, hd.times(NQT - 1).at(c + 1))
                        if c == 0:
                            V.tensor_copy(state_c(0), to_ps[:, 0:DV]).then_inc(st_ready, 1)
                        else:
                            V.scalar_tensor_tensor(state_c(c), state_c(c - 1), colc[:, EB + c:EB + c + 1],
                                                   to_ps[:, 0:DV], ALU.mult, ALU.add).then_inc(st_ready, 1)
                        dve.wait_ge(st_ready, hd.times(NQT - 1).at(c + 1))
                    dve.wait_ge(gla_o, hd.times(NQT).at(c + 1))
                    V.tensor_copy(o_raw1[:, hd.times(2).cols(2, scale=1), c * P:(c + 1) * P],
                                  s_ps[:, c % 2, 0:DV].rearrange("p (t n) -> p t n", n=P)).then_inc(gla_o_free, 1)
                take(19)
                if following:
                    gk_start(hd + 1)
                take(20)
                if following:
                    gk_cumulate(hd + 1)
                dve.wait_ge(on_root, hd.at(1))
                for t in range(2):
                    o = o_raw1[:, (hd.times(2) + t).cols(1)].rearrange("p a n -> p (a n)")
                    last = V.tensor_tensor(o, o, dec[:], ALU.mult)
                steps.link(last)
                take(len(share.counts))

            def pairs(count, body, links=0):
                with dve.Fori(0, count // 2) as i:
                    steps.enter(i, links)
                    for s in range(2):
                        body(Idx(s, [(2, i)]))
                    steps.leave(count // 2, links)

            def rest_of_layer(layer):
                st = PLAN[layer]
                if layer == 1:
                    V.memset(colc[:, MARK:MARK + 1], 0.0).then_inc(o_gated, 1)
                    pairs(KT, lambda o: split_o(o_raw1, o + st["x_o"] // 2, o))

                def wo(o):
                    for half in range(2):
                        u = (o + st["wo"]).times(2) + half
                        if half == 0:
                            dve.wait_ge(h_loaded[o.parity], (o.half() + 4 * layer).times(16).at(16))
                        dve.wait_ge(unit_ready, u.at(1))
                        V.tensor_tensor(tile_of(h, o, half), bank(half), tile_of(h, o, half),
                                        ALU.add).then_inc(unit_free, 1)
                        split_lo(st["norm"] + 1, o, half, o.times(2) + (st["x_mlp"] + half), b_hi, b_lo)
                    w_lo(o + (st["wo"] + 2))

                pairs(KT, wo)
                norm_scale(st["norm"] + 1)

                def ff_chunk(c, last_chunk):
                    p = c.times(2 * KT) + st["mlp"]
                    x = c.times(16) + st["x_hid"]

                    def up(o):
                        for half in range(2):
                            dve.wait_ge(unit_ready, (p + o).times(2).at(half + 1))
                            V.scalar_tensor_tensor(zt[:, half], bank(half), 0.0, rstd[:, half_cols(half)], ALU.max,
                                                   ALU.mult).then_inc(unit_free, 1)
                            dve.wait_ge(x_hi_ready, (x + o.times(2)).at(half + 1))
                            V.tensor_tensor(tile_of(a_lo, o, half), zs[:, half], tile_of(a_hi, o, half),
                                            ALU.subtract).then_inc(x_lo_ready, 1)
                        w_lo(p + (o + 2))

                    def down(o):
                        for half in range(2):
                            dve.wait_ge(unit_ready, (p + (o + KT)).times(2).at(half + 1))
                            V.tensor_tensor(tile_of(h, o, half), bank(half), tile_of(h, o, half),
                                            ALU.add).then_inc(unit_free, 1)
                            if last_chunk:
                                split_lo(st["norm"] + 2, o, half, o.times(2) + (st["x_ple"] + half), b_hi, b_lo)
                        w_lo(p + (o + KT + 2))

                    pairs(KT, up)
                    pairs(KT, down)

                with dve.Fori(0, CHUNKS - 1) as c:
                    ff_chunk(Idx(0, [(1, c)]), False)
                ff_chunk(Idx(CHUNKS - 1), True)
                n = st["norm"] + 3
                norm_scale(n - 1)

                def gate_in(p, half):
                    dve.wait_ge(unit_ready, p.times(2).at(half + 1))
                    V.tensor_tensor(zt[:, half], bank(half), rstd[:, half_cols(half)], ALU.mult).then_inc(unit_free, 1)

                def gate_out(o, half):
                    g = o.times(2) + half
                    dve.wait_ge(sig_ready, g.at((0 if layer == 0 else SIG_GATE1) + 1))
                    steps.link(V.tensor_tensor(zt[:, half], zs[:, half], tile_of(pp, o, half), ALU.mult))
                    V.tensor_tensor(tile_of(h, o, half), tile_of(h, o, half), zt[:, half], ALU.add).then_inc(h_ready, 1)

                def next_lo(o, half):
                    if layer == 0:
                        split_lo(n, o, half, o.times(2) + (PLAN[1]["x_mix"] + half), a_hi, a_lo)

                def gate(o):
                    p = o + (st["gate"] + 4)
                    for half in range(2):
                        gate_in(p, half)
                        if half == 0:
                            next_lo(o + (-1), 1)
                        else:
                            next_lo(o, 0)
                        gate_out(o, half)
                    w_lo(p + 2)

                dve.wait_ge(p_hi_ready, layer + 1)
                V.tensor_tensor(a_hi[:, 6:8], p_raw[:], a_hi[:, 4:6], ALU.subtract).then_inc(p_lo_ready, 1)
                for half in range(2):
                    gate_in(Idx(st["gate"]), half)
                w_lo(Idx(st["gate"] + 2))
                for j in range(4):
                    for e in range(2):
                        o = 4 * (j % 2) + 2 * e
                        dve.wait_ge(unit_ready, 2 * (st["ple"] + j) + e + 1)
                        V.tensor_copy(pp[:, o:o + 2, half_cols(j // 2)],
                                      s_ps[:, e].rearrange("p (a n) -> p a n", n=HALF)).then_inc(unit_free, 1)
                    w_lo(Idx(st["ple"] + j + 2))
                for half in range(2):
                    gate_out(Idx(0), half)
                    if half == 1:
                        next_lo(Idx(0), 0)
                gate(Idx(1))
                with dve.Fori(1, KT // 2 - 1) as i:
                    steps.enter(i, 4, 1)
                    for s in range(2):
                        gate(Idx(s, [(2, i)]))
                    steps.leave(KT // 2 - 2, 4)
                for o in (KT - 2, KT - 1):
                    gate(Idx(o))
                next_lo(Idx(KT - 1), 1)

            V.memset(ones[:], 1.0).then_inc(const_ready, 1)
            V.memset(colc[:, QS:QS + DIFF_HEADS], 64 ** -0.5).then_inc(o_evacuated, 1)
            V.memset(colc[:, QS + DIFF_HEADS:QS + HEADS], 128 ** -0.5)
            V.memset(colc[:, EPSC:EPSC + 1], EPS)
            steps.link(V.memset(colc[:, ONE:ONE + 1], 1.0))
            dve.wait_ge(const_loaded, 16 * 7)
            for t in range(2):
                steps.link(V.tensor_tensor(zt[:, 1, t * 64:(t + 1) * 64], lam_in[:, 2 * t * 64:(2 * t + 1) * 64],
                                           lam_in[:, (2 * t + 1) * 64:(2 * t + 2) * 64], ALU.mult))
            V.tensor_reduce(colc[:, LAM1:LAM1 + 2], zt[:, 1, 0:128].rearrange("p (t n) -> p t n", t=2), AX,
                            ALU.add).then_inc(const_ready, 1)
            w_lo(Idx(0))
            for o in range(KT):
                for half in range(2):
                    split_lo(0, Idx(o), half, Idx(2 * o + half), a_hi, a_lo)
            dve.wait_ge(lam_exp, 1)
            steps.link(V.tensor_tensor(colc[:, NEGLAM:NEGLAM + 1], colc[:, LAM2:LAM2 + 1], colc[:, LAM1:LAM1 + 1],
                                       ALU.subtract))
            steps.link(V.tensor_scalar(colc[:, NEGLAM:NEGLAM + 1], colc[:, NEGLAM:NEGLAM + 1], LAM_INIT, None,
                                       ALU.subtract))
            steps.link(V.tensor_scalar(colc[:, GSUB:GSUB + 1], colc[:, GSUB:GSUB + 1], 1.0 - LAM_INIT, None, ALU.mult))
            w_lo(Idx(1))
            norm_scale(0)
            F = DIFF_HEADS
            for half in range(2):
                dve.wait_ge(unit_ready, half + 1)
                V.tensor_tensor(prob[0:F, 0, half_cols(half)], bank(half, F), rstd[0:F, half_cols(half)],
                                ALU.mult).then_inc(unit_free, 1)
            w_lo(Idx(2))
            for u in range(6):
                evacuate_raw(Idx(0), u)
            split_qk(Idx(0))
            V.tensor_scalar(prob[0:F, 0], prob[0:F, 0], colc[0:F, BF:BF + 1], None, ALU.add).then_inc(fl_ready, 1)
            V.memset(c_row[:], 0.0)
            dve.wait_ge(fl_log, 1)
            log_sigmoid(prob[0:F, 0], prob[0:F, 1], 1.0)
            steps.link(V.memset(prob[0:F, 0], 1.0))
            steps.link(V.tensor_tensor_scan(c_row[0:F], prob[0:F, 0], prob[0:F, 1], 0.0, ALU.mult, ALU.add))
            with dve.Fori(0, DIFF_HEADS // 2) as i:
                links = 2 * NQT
                steps.enter(i, links)
                for e in range(2):
                    attention(Idx(e, [(2, i)]), True, ATT_SHARE, True)
                steps.leave(DIFF_HEADS // 2, links)
            split_gates(Idx(DIFF_HEADS))
            dve.wait_ge(masks_stored, 16)
            for hd in range(DIFF_HEADS, HEADS):
                attention(Idx(hd), False, ATT_SHARE if hd < HEADS - 1 else NO_SHARE, hd < HEADS - 1)
            rest_of_layer(0)
            st = PLAN[1]
            norm_scale(st["norm"])
            for half in range(2):
                dve.wait_ge(unit_ready, 2 * st["mix"] + half + 1)
                V.tensor_tensor(gl_t[0:LOWRANK, half_cols(half)], bank(half, LOWRANK), rstd[0:LOWRANK, half_cols(half)],
                                ALU.mult).then_inc(unit_free, 1)
            V.tensor_copy(wgk_h[:], wgk_all[:, 0:DK]).then_inc(gk_w, 1)
            w_lo(Idx(st["mix"] + 2))
            V.memset(att[:], 0.0)
            steps.link(V.memset(resets[:], 1.0))
            steps.link(V.memset(resets[:, 0:SEQ:P], 0.0))
            dve.wait_ge(h_spilled, 16 * KT)
            gk_start(Idx(0))
            gk_cumulate(Idx(0))
            p = Idx(st["heads"])
            for u in range(8):
                evacuate_vqk(p + u // 2, u)
            dve.wait_ge(masks_loaded, 16)
            gla_head(Idx(0), GLA_SHARE[8], p + 4, True)
            with dve.Fori(1, GLA_HEADS - 1) as i:
                hd = Idx(0, [(1, i)])
                links = 2 + 1 + 1 + 1 + 8
                steps.enter(i, links, 1)
                gla_head(hd, GLA_SHARE[12], hd.times(6) + (st["heads"] + 2), True)
                steps.leave(GLA_HEADS - 2, links)
            gla_head(Idx(3), GLA_SHARE[4], p + 20, False)
            for u in range(4):
                evacuate_gate(Idx(3), p + (22 + u // 2), u)
            rest_of_layer(1)
            norm_scale(6)
            for o in range(KT):
                V.scalar_tensor_tensor(h[:, o], h[:, o], gcol[:, 6 * KT + o:6 * KT + o + 1], rstd[:], ALU.mult,
                                       ALU.mult).then_inc(final_ready, 1)


def kernel(**inputs):
    import numpy as np
    import concourse.bacc as bacc
    from concourse.bass_utils import run_bass_kernel_spmd

    a = {k: np.asarray(v) for k, v in inputs.items()}

    def panel(w):
        k, n = w.shape
        return w.reshape(k // P, P, n // P, P).transpose(2, 1, 0, 3).reshape(n // P, P, -1)

    def padded(w):
        return np.concatenate([w, np.zeros((w.shape[0], P - w.shape[1]), w.dtype)], axis=1)

    def layer_tail(w_o, i):
        up, down = a["w_up"][i], a["w_down"][i]
        parts = [panel(w_o)]
        for c in range(CHUNKS):
            parts += [panel(up[:, c * D:(c + 1) * D]), panel(down[c * D:(c + 1) * D])]
        proj = a["w_ple_proj"][i].reshape(2, P, 2, HALF).transpose(2, 1, 0, 3).reshape(2, P, -1)
        gate = panel(a["w_ple_gate"][i])
        return parts + [gate[:1], proj, proj, gate[1:]]

    even, odd = a["even_w_in"][0], a["odd_w_in"][0]
    W = DIFF_HEADS * P
    cols = lambda w, c: panel(w[:, c:c + P])
    stream = [panel(padded(even[:, 6 * W:]))]
    for hd in range(HEADS):
        base = (hd // DIFF_HEADS) * 3 * W + (hd % DIFF_HEADS) * P
        stream += [cols(even, base), cols(even, base + W), cols(even, base + 2 * W)]
    stream += layer_tail(a["even_w_o"][0], 0)
    stream += [panel(padded(odd[:, 6 * W:]))]

    def vqk(hd):
        v = 2 * W + hd * DV
        return [cols(odd, v), cols(odd, v + P), cols(odd, hd * DK), cols(odd, W + hd * DK)]

    def gate(hd):
        g = 4 * W + hd * DV
        return [cols(odd, g), cols(odd, g + P)]

    stream += vqk(0) + vqk(1) + gate(0) + vqk(2) + gate(1) + vqk(3) + gate(2) + gate(3)
    stream += layer_tail(a["odd_w_o"][0], 1)
    gains = [g for i in range(2) for g in (a["norm_mix"][i], a["norm_mlp"][i], a["norm_ple"][i])]
    arrays = {
        "x_t": a["x"][0].T.reshape(KT, P, SEQ),
        "p_t": a["p"][:, 0].transpose(0, 2, 1).reshape(2, 2, P, SEQ),
        "panels": np.concatenate(stream),
        "gains": np.stack(gains + [a["norm_final"]]).reshape(7 * KT, P).T,
        "b_f": a["even_b_f"].reshape(DIFF_HEADS, 1),
        "lam_vec": np.concatenate([a["lam_q1"], a["lam_k1"], a["lam_q2"], a["lam_k2"]]),
        "g_sub": a["diff_subln"].reshape(P, 1),
        "w_gk": a["odd_w_gk"][0],
        "b_gk": a["odd_b_gk"].reshape(GLA_HEADS, DK).T,
        "g_on": a["gla_onorm"].reshape(2, P).T,
    }
    arrays = {k: np.ascontiguousarray(v) for k, v in arrays.items()}
    assert arrays["panels"].shape == (PANELS, P, D)
    nc = bacc.Bacc("TRN2", target_bir_lowering=False, num_devices=1)
    args = [nc.dram_tensor(k, v.shape, mybir.dt.from_np(v.dtype), kind="ExternalInput").ap()
            for k, v in arrays.items()]
    args.append(nc.dram_tensor("out_t", [KT, P, SEQ], F32, kind="ExternalOutput").ap())
    build_trunk(nc, *args)
    r = run_bass_kernel_spmd(nc, [arrays], core_ids=[0])
    got = r.results[0]["out_t"]
    return np.ascontiguousarray(got.reshape(D, SEQ).T).reshape(1, SEQ, D)
```

```python
from contextlib import ExitStack

import concourse.bass as bass
from concourse import mybir
from concourse.alu_op_type import AluOpType as ALU

F32 = mybir.dt.float32
F32R = mybir.dt.float32r
I32 = mybir.dt.int32
ACT = mybir.ActivationFunctionType
AX = mybir.AxisListType.X
ds = bass.ds

P = 128
D = 1024
SEQ = 1024
KT = D // P
HALF = SEQ // 2
NQT = SEQ // P
FF = 4 * D
CHUNKS = FF // D
HEADS = 8
DIFF_HEADS = 4
GLA_HEADS = 4
DK = 128
DV = 256
LOWRANK = 16
LEVELS = 7
EPS = 1e-6
SIG_MIX1 = 2 * KT
SIG_GATE1 = SIG_MIX1 + 4 * GLA_HEADS
LAM_INIT = 0.8 - 0.6 * 1.0
MASKED = -1.0e30

LOW_ROW = 32
GATE_ROWS = LOW_ROW + DIFF_HEADS
SUB_LAG = DIFF_HEADS
O_ORDER = [0, 1, 2, 4, 5, 6, 3, 7]
PANELS_MIX = 1 + 3 * HEADS
PANELS_MLP = 2 * KT * CHUNKS
PANELS_LAYER = PANELS_MIX + KT + PANELS_MLP + 4 + KT
PANELS = 2 * PANELS_LAYER
FINAL_GP = 1
GROUPS = [1 if i < 4 else 2 for i in range(NQT)]
GROUPS_HEAD = sum(GROUPS)


class Share:

    def __init__(self, counts, units):
        left = KT * units - sum(counts)
        assert left >= 0, left
        self.counts = list(counts[:-1]) + [counts[-1] + left]
        self.units = units

    def complete(self, point):
        return sum(self.counts[:point]) // KT


DIFF_SHARE = Share([1, 3] + [1, 1, 0, 1] * 4 + [1, 1, 3, 1] * 2 + [2, 1, 2, 1] + [7, 1, 3, 3], 6)
FOX_SHARE = Share([2, 1] + [1, 1, 0, 1] + [1, 1, 0, 2] * 2 + [1, 1, 0, 2] + [2, 1, 3, 1] * 3 + [2, 0, 3, 4], 6)
NO_SHARE = Share([0] * 34, 0)
WO_PLACES = {4 * i + 3: [i - 2] for i in range(2, NQT)}
WO_PLACES[4 * (NQT - 1) + 4] = [KT - 2]
GLA_SHARE = {n: Share(c, n) for n, c in {
    8: [8] + [4, 3, 4, 3, 3, 3, 2, 1] + [2, 4] + [1] * 8 + [10, 9],
    12: [8] + [4, 4, 8, 3, 3, 2, 7, 1] + [6, 6] + [3] * 8 + [10, 10],
    6: [6] + [3, 3, 4, 8, 3, 5, 5, 0] + [3, 2] + [0] * 8 + [6, 0]}.items()}
GATES = {8: 0, 12: 4, 6: 6}


class Idx:

    def __init__(self, c, terms=()):
        self.c, self.terms = c, tuple(terms)

    def __add__(self, n):
        if isinstance(n, Idx):
            return Idx(self.c + n.c, self.terms + n.terms)
        return Idx(self.c + n, self.terms)

    def times(self, m):
        return Idx(self.c * m, [(k * m, r) for k, r in self.terms])

    def half(self):
        return Idx(self.c // 2, [(k // 2, r) for k, r in self.terms])

    @property
    def parity(self):
        assert all(k % 2 == 0 for k, _ in self.terms)
        return self.c % 2

    def at(self, add=0):
        v = self.c + add
        for k, r in self.terms:
            v = r * k + v
        return v

    def cols(self, n, scale=None, add=0):
        s = self.times(n if scale is None else scale)
        return ds(s.at(add), n)


class Chain:

    def __init__(self, eng, sem):
        self.eng, self.sem, self.base, self.n = eng, sem, Idx(0), 0

    def link(self, ins):
        self.n += 1
        ins.then_inc(self.sem, 1)
        self.eng.wait_ge(self.sem, self.base.at(self.n))

    def enter(self, reg, steps, start=0):
        self.saved = (self.base, self.n)
        self.base, self.n = self.base + Idx(self.n - steps * start, [(steps, reg)]), 0

    def leave(self, iterations, steps):
        assert self.n == steps, (self.n, steps)
        base, n = self.saved
        self.base, self.n = base, n + iterations * steps


def plan_layer(layer):
    p0 = layer * PANELS_LAYER
    x0 = layer * 128
    s = dict(mix=p0, heads=p0 + 1, wo=p0 + PANELS_MIX)
    s["mlp"] = s["wo"] + KT
    s["gate"] = s["mlp"] + PANELS_MLP
    s["ple"] = s["gate"] + 1
    s["x_mix"] = x0
    s["x_o"] = x0 + 16
    s["x_mlp"] = x0 + 32
    s["x_hid"] = x0 + 48
    s["x_ple"] = x0 + 48 + 16 * CHUNKS
    s["norm"] = 3 * layer
    assert s["x_ple"] + 16 == x0 + 128 and s["heads"] % 2 == s["wo"] % 2
    return s


PLAN = [plan_layer(0), plan_layer(1)]


def build_trunk(nc, x_t, p_t, panels, gains, b_f, lam_vec, g_sub, w_gk, b_gk, g_on, out_t):
    m_dram = nc.dram_tensor("level_masks", [P, 8 * P], F32, kind="Internal").ap()
    h_dram = nc.dram_tensor("h_spill", [KT, P, SEQ], F32, kind="Internal").ap()
    ctx = ExitStack()
    with ctx:
        def overlay(*groups):
            made = {}
            for group in groups[1:]:
                with ExitStack() as inner:
                    for name, shape, dt in group:
                        made[name] = inner.enter_context(nc.sbuf_tensor(name, shape, dt))
            for name, shape, dt in groups[0]:
                made[name] = ctx.enter_context(nc.sbuf_tensor(name, shape, dt))
            return made

        def sb(name, shape, dt=F32):
            return ctx.enter_context(nc.sbuf_tensor(name, shape, dt))

        def sem(name):
            return ctx.enter_context(nc.semaphore(name))

        m = overlay(
            [("a_hi", [P, KT, SEQ], F32R), ("a_lo", [P, KT, SEQ], F32R)],
            [("p_raw", [P, 2, SEQ], F32), ("p_skip", [P, 6, SEQ], F32), ("pp", [P, KT, SEQ], F32)],
        )
        a_hi, a_lo, p_raw, pp = m["a_hi"], m["a_lo"], m["p_raw"], m["pp"]
        m = overlay(
            [("b_hi", [P, KT, SEQ], F32R), ("b_lo", [P, KT, SEQ], F32R)],
            [("o_raw", [P, KT, SEQ], F32),
             ("pt_hi", [P, NQT, 256], F32R), ("pt_lo", [P, NQT, 256], F32R),
             ("v_t", [P, SEQ], F32), ("c_row", [P, SEQ], F32),
             ("q_raw", [P, SEQ], F32), ("k_raw", [P, SEQ], F32)],
            [("o_below", [P, 7, SEQ], F32), ("lmask_built", [P, 8, P], F32)],
            [("o_raw1", [P, KT, SEQ], F32),
             ("dec", [P, SEQ], F32), ("lev", [P, SEQ], F32), ("att", [P, SEQ], F32),
             ("q_dec", [P, SEQ], F32), ("k_dec", [P, SEQ], F32), ("k_tok", [P, SEQ], F32),
             ("gl_t", [P, SEQ], F32), ("resets", [P, SEQ], F32)],
        )
        b_hi, b_lo, o_raw, pt_hi, pt_lo = m["b_hi"], m["b_lo"], m["o_raw"], m["pt_hi"], m["pt_lo"]
        v_t, c_row, q_raw, k_raw, lmask_built = m["v_t"], m["c_row"], m["q_raw"], m["k_raw"], m["lmask_built"]
        o_raw1, dec, lev, att = m["o_raw1"], m["dec"], m["lev"], m["att"]
        q_dec, k_dec, k_tok, gl_t, resets = m["q_dec"], m["k_dec"], m["k_tok"], m["gl_t"], m["resets"]
        m = overlay(
            [("h", [P, KT, SEQ], F32)],
            [("q_hi", [P, SEQ], F32R), ("q_lo", [P, SEQ], F32R), ("k_hi", [P, SEQ], F32R),
             ("k_lo", [P, SEQ], F32R), ("v_hi", [P, NQT, P], F32R), ("v_lo", [P, NQT, P], F32R),
             ("prob", [P, 2, SEQ], F32)],
            [("q_t", [P, SEQ], F32), ("k_t", [P, SEQ], F32), ("vg_t", [P, 2, SEQ], F32),
             ("v_tok", [P, NQT, DV], F32), ("b_cum", [P, SEQ], F32), ("lmask", [P, 8, P], F32)],
        )
        h, prob = m["h"], m["prob"]
        q_hi, q_lo, k_hi, k_lo, v_hi, v_lo = (m[n] for n in ("q_hi", "q_lo", "k_hi", "k_lo", "v_hi", "v_lo"))
        q_t, k_t, vg_t, v_tok, b_cum, lmask = (m[n] for n in ("q_t", "k_t", "vg_t", "v_tok", "b_cum", "lmask"))

        wraw = sb("wraw", [P, 2, KT, P])
        whi = sb("whi", [P, 2, KT, P], F32R)
        wlo = sb("wlo", [P, 2, KT, P], F32R)
        rstd = sb("rstd", [P, SEQ])
        sumsq = sb("sumsq", [P, 2, HALF])
        m = overlay([("zt", [P, 2, HALF], F32), ("zs", [P, 2, HALF], F32)],
                    [("cm", [P, SEQ], F32R)])
        zt, zs, cm = m["zt"], m["zs"], m["cm"]
        ones = sb("ones", [P, P])
        ident = sb("ident", [P, P])
        ident_r = sb("ident_r", [P, P], F32R)
        mask_f = zt[:, 0, 0:P]
        mask_r = sb("mask_r", [P, P], F32R)
        negones_r = sb("negones_r", [GATE_ROWS, P], F32R)
        gcol = sb("gcol", [P, 7 * KT])
        colc = sb("colc", [P, 64])
        state = sb("state", [P, 2, DV])
        wgk_all = sb("wgk_all", [LOWRANK, GLA_HEADS * DK])
        wgk_h = sb("wgk_h", [LOWRANK, DK])
        lam_in = k_raw[:, 0:256]

        QS = 0
        ONE, NEGLAM = 8, 9
        GSUB, BF, BGK, GON = 10, 11, 12, 16
        LAM1, LAM2 = 18, 19
        NEG, L, RL = 20, 24, 28
        C2 = 32
        SEL = 36
        EB = 40
        EPSC = 60
        MARK = 50

        gemm_ps = ctx.enter_context(nc.psum_tensor("gemm_ps", [P, 2, HALF], F32))
        s_ps = ctx.enter_context(nc.psum_tensor("s_ps", [P, 2, SEQ], F32))
        to_ps = ctx.enter_context(nc.psum_tensor("to_ps", [P, SEQ], F32))

        w_loaded = [sem("w_loaded0"), sem("w_loaded1")]
        w_hi_ready, w_lo_ready = sem("w_hi_ready"), sem("w_lo_ready")
        unit_ready, unit_free = sem("unit_ready"), sem("unit_free")
        x_hi_ready, x_lo_ready = sem("x_hi_ready"), sem("x_lo_ready")
        sq_ready, sq_added = sem("sq_ready"), sem("sq_added")
        norm_sum, norm_ms, norm_root = sem("norm_sum"), sem("norm_ms"), sem("norm_root")
        x_loaded = [sem(f"x_loaded{o}") for o in range(KT)]
        gains_loaded, const_loaded, const_ready = sem("gains_loaded"), sem("const_loaded"), sem("const_ready")
        gp_const, lam_exp, ph_ready = sem("gp_const"), sem("lam_exp"), sem("ph_ready")
        v_step, a_step, g_step = sem("v_step"), sem("a_step"), sem("g_step")
        qk_hi_ready, qk_lo_ready = sem("qk_hi_ready"), sem("qk_lo_ready")
        vt_ready, v_hi_ready, v_lo_ready = sem("vt_ready"), sem("v_hi_ready"), sem("v_lo_ready")
        scores_ready, negmax_ready, exp_ready, w_ready = (sem("scores_ready"), sem("negmax_ready"),
                                                          sem("exp_ready"), sem("weights_ready"))
        coef_ready, scaled_ready = sem("coef_ready"), sem("scaled_ready")
        masks_stored, masks_loaded = sem("masks_stored"), sem("masks_loaded")
        tr_ready, tr_hi, tr_lo = sem("tr_ready"), sem("tr_hi"), sem("tr_lo")
        pv_ready, o_evacuated = sem("pv_ready"), sem("o_evacuated")
        sub_sq, sub_sum, sub_ms, sub_root, sub_done = (sem("sub_sq"), sem("sub_sum"), sem("sub_ms"),
                                                       sem("sub_root"), sem("sub_done"))
        fl_ready, fl_log, fl_done = sem("fl_ready"), sem("fl_log"), sem("fl_done")
        cm_hi_ready, cm_lo_ready = sem("cm_hi_ready"), sem("cm_lo_ready")
        h_loaded = [sem("h_loaded0"), sem("h_loaded1")]
        h_spilled, p_loaded, out_stored = sem("h_spilled"), sem("p_loaded"), sem("out_stored")
        p_hi_ready, p_lo_ready = sem("p_hi_ready"), sem("p_lo_ready")
        sig_ready, h_ready, o_gated = sem("sig_ready"), sem("h_ready"), sem("o_gated")
        final_ready, final_gp = sem("final_ready"), sem("final_gp")
        gk_w, gk_sum, gk_in, gk_log = sem("gk_w"), sem("gk_sum"), sem("gk_in"), sem("gk_log")
        vtok_sum, vtok_ready = sem("vtok_sum"), sem("vtok_ready")
        dec_in, dec_exp, lev_ready, lev_sum, lev_done = (sem("dec_in"), sem("dec_exp"), sem("lev_ready"),
                                                         sem("lev_sum"), sem("lev_done"))
        ktok_in, ktok_sum, ktok_ready = sem("ktok_in"), sem("ktok_sum"), sem("ktok_ready")
        gla_o, gla_o_free, st_sum, st_ready = sem("gla_o"), sem("gla_o_free"), sem("st_sum"), sem("st_ready")
        on_sq, on_added, on_sum = sem("on_sq"), sem("on_added"), sem("on_sum")
        on_ms, on_root = sem("on_ms"), sem("on_root")

        block = ctx.enter_context(nc.Block())

        def task(hd, i, mp, diff):
            if diff:
                return hd.times(2 * NQT) + (2 * i + mp)
            return hd.times(NQT) + (DIFF_HEADS * NQT + i)

        def second_halves(a, lv):
            hb = 64 >> lv
            return a.rearrange("p (b n) -> p b n", n=2 * hb)[:, :, hb:2 * hb]

        def state_c(c):
            return state[:, c % 2]

        def half_cols(half):
            return slice(half * HALF, (half + 1) * HALF)

        @block.sync
        def _(sp):
            def load_panel(p):
                if not (isinstance(p.at(), int) and p.at() < 2):
                    sp.wait_ge(w_lo_ready, p.at(-1))
                sp.dma_start(wraw[:, p.parity].rearrange("p k m -> p (k m)"),
                             panels[p.cols(1)].rearrange("a p n -> p (a n)")).then_inc(w_loaded[p.parity], 16)

            def load_panels(first, count):
                if count % 2:
                    load_panel(Idx(first))
                    first, count = first + 1, count - 1
                with sp.Fori(0, count // 2) as i:
                    for s in range(2):
                        load_panel(Idx(first + s, [(2, i)]))

            for layer, st in enumerate(PLAN):
                if layer == 0:
                    load_panel(Idx(0))
                    sp.dma_start(h[:, 0], x_t[0]).then_inc(x_loaded[0], 16)
                    load_panel(Idx(1))
                    for o in range(2, KT, 2):
                        sp.dma_start(h[:, o], x_t[o]).then_inc(x_loaded[o], 16)
                    load_panels(2, PANELS_MIX - 2)
                else:
                    load_panels(st["mix"], PANELS_MIX)
                def wo_and_residual(o, first):
                    if first and layer == 1:
                        sp.wait_ge(gla_o, GLA_HEADS * NQT)
                        sp.wait_ge(h_spilled, 16 * KT)
                        residual(o, first)
                    for s in range(2):
                        load_panel(o + (st["wo"] + s))
                    if first and layer == 0:
                        sp.wait_ge(o_evacuated, 4 * HEADS + 1)
                    if not (first and layer == 1):
                        residual(o, first)

                def residual(o, first):
                    src = x_t if layer == 0 else h_dram
                    for s in range(2):
                        if not (first and layer == 0):
                            sp.wait_ge(h_loaded[s], (o.half() + 4 * layer).times(16).at())
                        sp.dma_start(h[:, (o + s).cols(1)].rearrange("p a n -> p (a n)"),
                                     src[(o + s).cols(1)].rearrange("a p n -> p (a n)")).then_inc(h_loaded[s], 16)

                wo_and_residual(Idx(0), True)
                with sp.Fori(1, KT // 2) as i:
                    wo_and_residual(Idx(0, [(2, i)]), False)
                load_panels(st["mlp"], PANELS_MLP + 4 + KT)
            for o in range(KT):
                if o < KT - FINAL_GP:
                    sp.wait_ge(final_ready, o + 1)
                else:
                    sp.wait_ge(final_gp, o - (KT - FINAL_GP) + 1)
                sp.dma_start(out_t[o], h[:, o]).then_inc(out_stored, 16)
            sp.wait_ge(out_stored, 16 * KT)

        @block.tensor
        def _(pe):
            def product(out, hi_w, lo_w, hi_x, lo_x, start, stop):
                nc.tensor.matmul(out, hi_w, hi_x, start=start, stop=False, skip_group_check=True)
                nc.tensor.matmul(out, hi_w, lo_x, start=False, stop=False, skip_group_check=True)
                return nc.tensor.matmul(out, lo_w, hi_x, start=False, stop=stop, skip_group_check=True)

            def norm_sums(n):
                pe.wait_ge(sq_added, 16 * (n + 1))
                for half in range(2):
                    nc.tensor.matmul(s_ps[:, 0, half_cols(half)], ones[:], sumsq[:, half], start=True,
                                     stop=True).then_inc(norm_sum, 1)

            def unit(p, half, hi, lo, x_base=None, k_order=range(KT), places=range(KT), half_major=False):
                s, u = p.parity, p.times(2) + half
                if 0 in places:
                    if half == 0:
                        pe.wait_ge(w_lo_ready, p.at(1))
                    if not (isinstance(u.at(), int) and u.at() < 2):
                        pe.wait_ge(unit_free, u.at(-1))
                for n in places:
                    k = k_order[n]
                    if x_base is not None:
                        pe.wait_ge(x_lo_ready, x_base.at((KT * half + n if half_major else 2 * n + half) + 1))
                    last = product(gemm_ps[:, half], whi[:, s, k], wlo[:, s, k],
                                   hi[:, k, half_cols(half)], lo[:, k, half_cols(half)], n == 0, n == KT - 1)
                if KT - 1 in places:
                    last.then_inc(unit_ready, 1)

            def panel(p, hi, lo, x_base=None, norm=None, k_order=range(KT), begun=0, half_major=False):
                for half in range(2):
                    unit(p, half, hi, lo, x_base, k_order, range(begun, KT), half_major)
                    if norm is not None and half == 0:
                        norm_sums(norm)

            def filler(share, first):
                done = [0]

                def fill(point):
                    for _ in range(share.counts[point]):
                        u, place = divmod(done[0], KT)
                        unit(first + u // 2, u % 2, a_hi, a_lo, places=[place])
                        done[0] += 1
                return fill

            def stage(p, count, hi, lo, x_base=None, norm=None, k_order=range(KT), begun=0, half_major=False):
                if x_base is not None:
                    for s in range(2):
                        first = s == 0
                        panel(p + s, hi, lo, x_base if first else None, norm if first else None,
                              k_order if first else range(KT), begun if first else 0, half_major)
                    p, count = p + 2, count - 2
                with pe.Fori(0, count // 2) as i:
                    for s in range(2):
                        panel(p + Idx(s, [(2, i)]), hi, lo)

            def attention(hd, diff, share):
                maps = 2 if diff else 1
                if share is NO_SHARE:
                    def fill(point):
                        for place in WO_PLACES.get(point, ()):
                            for half in range(2):
                                unit(Idx(PLAN[0]["wo"]), half, a_hi, a_lo, Idx(PLAN[0]["x_o"]), O_ORDER, [place])
                else:
                    fill = filler(share, hd.times(3) + (PLAN[0]["heads"] + 3))

                def scores(i, mp):
                    keys = (i + 1) * P
                    bank_pair = mp if diff else i % 2
                    r = slice(64 * mp, 64 * mp + 64) if diff else slice(0, P)
                    for c0 in range(0, keys, HALF):
                        c1 = min(keys, c0 + HALF)
                        out = s_ps[:, bank_pair, c0:c1]
                        product(out, q_hi[r, i * P:(i + 1) * P], q_lo[r, i * P:(i + 1) * P],
                                k_hi[r, c0:c1], k_lo[r, c0:c1], True, False)
                        if not diff:
                            nc.tensor.matmul(out, negones_r[:], cm[0:GATE_ROWS, c0:c1], start=False,
                                             stop=False, skip_group_check=True)
                    nc.tensor.matmul(s_ps[:, bank_pair, i * P:keys], ident_r[:], mask_r[:], start=False,
                                     stop=True, skip_group_check=True).then_inc(scores_ready, 1)

                def transposes(i, done, between):
                    pe.wait_ge(w_ready, hd.times(NQT).at(i + 1))
                    for g in range(GROUPS[i]):
                        if g == 1:
                            between()
                        if i == 0:
                            pe.wait_ge(v_lo_ready, hd.at(1))
                        else:
                            pe.wait_ge(tr_lo, hd.times(GROUPS_HEAD).at(done + g))
                        for j in range(4 * g, min(4 * g + 4, i + 1)):
                            last = nc.tensor.transpose(to_ps[:, (j - 4 * g) * P:(j - 4 * g + 1) * P],
                                                       prob[:, 1 if diff else i % 2, j * P:(j + 1) * P], ident[:])
                        last.then_inc(tr_ready, 1)

                def values(c):
                    pe.wait_ge(tr_lo, hd.times(GROUPS_HEAD).at(sum(GROUPS[:2 * c + 2])))
                    pe.wait_ge(o_evacuated, hd.times(4).at(c + 1))
                    for j in range(2 * c + 2):
                        q0 = P if j == 2 * c + 1 else 0
                        last = product(to_ps[:, HALF + q0:HALF + 256], v_hi[:, j], v_lo[:, j],
                                       pt_hi[:, j, q0:256], pt_lo[:, j, q0:256], j == 0, j == 2 * c + 1)
                    last.then_inc(pv_ready, 1)

                pe.wait_ge(qk_lo_ready, hd.times(2).at(2))
                if not diff:
                    pe.wait_ge(cm_lo_ready, hd.at(1 - DIFF_HEADS))
                for mp in range(maps):
                    scores(0, mp)
                fill(0)
                pe.wait_ge(unit_free, hd.times(6).at(8))
                pe.wait_ge(o_evacuated, hd.times(4).at(1))
                for t in range(NQT):
                    last = nc.tensor.transpose(to_ps[:, t * P:(t + 1) * P], v_t[:, t * P:(t + 1) * P], ident[:])
                last.then_inc(vt_ready, 1)
                fill(1)
                for i in range(NQT):
                    for mp in range(2):
                        if i + 1 < NQT and mp < maps:
                            if diff:
                                pe.wait_ge(exp_ready, task(hd, i, mp, diff).at(1))
                            elif i >= 1:
                                pe.wait_ge(exp_ready, task(hd, i - 1, 0, diff).at(1))
                            if not diff and i == 3:
                                pe.wait_ge(sub_ms, hd.at(1 - SUB_LAG))
                            scores(i + 1, mp)
                        fill(4 * i + mp + 2)
                    if i >= 2 and i % 2 == 0:
                        values(i // 2 - 1)
                    if not diff and i == 1:
                        pe.wait_ge(sub_sq, hd.at(1 - SUB_LAG))
                        for half in range(2):
                            last = nc.tensor.matmul(s_ps[:, half, HALF:SEQ], ones[:], v_t[:, half_cols(half)],
                                                    start=True, stop=True)
                        last.then_inc(sub_sum, 1)
                    transposes(i, sum(GROUPS[:i]), lambda: fill(4 * i + 4))
                    fill(4 * i + 5)
                values(3)

            def gk_sums(hd):
                pe.wait_ge(gk_w, hd.at(1))
                for half in range(2):
                    last = nc.tensor.matmul(to_ps[:, half_cols(half)], wgk_h[:], gl_t[0:LOWRANK, half_cols(half)],
                                            start=True, stop=True)
                last.then_inc(gk_sum, 1)

            def gla_head(hd, share, first, v_panel, following):
                fill = filler(share, first)
                pe.wait_ge(unit_free, v_panel.times(2).at(2))
                if share.units != 8:
                    pe.wait_ge(on_ms, hd.at())
                for t in range(2):
                    for c in range(NQT):
                        last = nc.tensor.transpose(s_ps[:, t, c * P:(c + 1) * P], vg_t[:, t, c * P:(c + 1) * P], ident[:])
                last.then_inc(vtok_sum, 1)
                fill(0)
                pe.wait_ge(vtok_ready, hd.at(1))
                for lv in range(LEVELS + 1):
                    n = hd.times(LEVELS + 1)
                    if lv < LEVELS:
                        pe.wait_ge(lev_ready, hd.times(LEVELS).at(lv + 1))
                    if lv >= 2:
                        pe.wait_ge(lev_done, n.at(lv - 1))
                    for c in range(NQT):
                        cs = slice(c * P, (c + 1) * P)
                        if lv < LEVELS:
                            last = nc.tensor.matmul(second_halves(s_ps[:, lv % 2, cs], lv), lev[:, cs],
                                                    second_halves(lev[:, cs], lv), start=True, stop=True)
                        else:
                            last = nc.tensor.matmul(s_ps[:, lv % 2, cs], k_t[:, cs], q_t[:, cs], start=True, stop=True)
                    last.then_inc(lev_sum, 1)
                    fill(1 + lv)
                fill(9)
                pe.wait_ge(ktok_in, hd.at(1))
                for c in range(NQT):
                    cs = slice(c * P, (c + 1) * P)
                    last = nc.tensor.transpose(to_ps[:, cs], k_dec[:, cs], ident[:])
                last.then_inc(ktok_sum, 1)
                fill(10)
                pe.wait_ge(ktok_ready, hd.at(1))
                pe.wait_ge(lev_done, hd.times(LEVELS + 1).at(LEVELS + 1))
                for c in range(NQT):
                    cs = slice(c * P, (c + 1) * P)
                    if c >= 1:
                        pe.wait_ge(st_ready, hd.times(NQT - 1).at(c))
                    if c < NQT - 1:
                        nc.tensor.matmul(to_ps[:, 0:DV], k_tok[:, cs], v_tok[:, c], start=True,
                                         stop=True).then_inc(st_sum, 1)
                    if c >= 2:
                        pe.wait_ge(gla_o_free, hd.times(NQT).at(c - 1))
                    for t in range(2):
                        out = s_ps[:, c % 2, t * P:(t + 1) * P]
                        last = nc.tensor.matmul(out, v_tok[:, c, t * P:(t + 1) * P], att[:, cs], start=True,
                                                stop=(c == 0))
                        if c >= 1:
                            last = nc.tensor.matmul(out, state_c(c - 1)[:, t * P:(t + 1) * P], q_dec[:, cs],
                                                    start=False, stop=True)
                    last.then_inc(gla_o, 1)
                    fill(11 + c)
                if following:
                    gk_sums(hd + 1)
                fill(19)
                pe.wait_ge(on_added, hd.at(1))
                for half in range(2):
                    last = nc.tensor.matmul(s_ps[:, 0, half_cols(half)], ones[:], dec[:, half_cols(half)],
                                            start=True, stop=True)
                last.then_inc(on_sum, 1)
                fill(20)

            def rest_of_layer(layer):
                st = PLAN[layer]
                stage(Idx(st["wo"]), KT, a_hi, a_lo, Idx(st["x_o"]), k_order=O_ORDER if layer == 0 else range(KT), begun=KT - 1 if layer == 0 else 0,
                      half_major=layer == 1)

                def ff_chunk(c, first):
                    p = c.times(2 * KT) + st["mlp"]
                    if first:
                        stage(p, KT, b_hi, b_lo, Idx(st["x_mlp"]), st["norm"] + 1)
                    else:
                        stage(p, KT, b_hi, b_lo)
                    stage(p + KT, KT, a_hi, a_lo, c.times(16) + st["x_hid"])

                ff_chunk(Idx(0), True)
                with pe.Fori(1, CHUNKS) as c:
                    ff_chunk(Idx(0, [(1, c)]), False)
                panel(Idx(st["gate"]), b_hi, b_lo, Idx(st["x_ple"]), st["norm"] + 2)
                for j in range(4):
                    p = st["ple"] + j
                    s = p % 2
                    pe.wait_ge(w_lo_ready, p + 1)
                    if j == 0:
                        pe.wait_ge(p_lo_ready, layer + 1)
                    half = j // 2
                    wh = whi[:, s].rearrange("p k m -> p (k m)")
                    wl = wlo[:, s].rearrange("p k m -> p (k m)")
                    for e in range(2):
                        if j:
                            pe.wait_ge(unit_free, 2 * p + e - 1)
                        elif e == 1:
                            pe.wait_ge(norm_ms, 2 * (st["norm"] + 3))
                        for b in range(2):
                            for k in range(2):
                                o = k * HALF + (2 * e + b) * P
                                last = product(s_ps[:, 1 - e, half_cols(b)], wh[:, o:o + P], wl[:, o:o + P],
                                               a_hi[:, 4 + k, half_cols(half)], a_hi[:, 6 + k, half_cols(half)],
                                               k == 0, k == 1)
                        last.then_inc(unit_ready, 1)
                panel(Idx(st["gate"] + 5), b_hi, b_lo)
                stage(Idx(st["gate"] + 6), KT - 2, b_hi, b_lo)

            st = PLAN[0]
            pe.wait_ge(const_ready, 1)
            for k in range(KT):
                if k == KT - 1:
                    norm_sums(st["norm"])
                for p in range(2):
                    if k == 0:
                        pe.wait_ge(w_lo_ready, p + 1)
                    for half in range(2):
                        pe.wait_ge(x_lo_ready, 2 * k + half + 1)
                        out = gemm_ps[:, half] if p == 0 else to_ps[:, half_cols(half)]
                        last = product(out, whi[:, p, k], wlo[:, p, k], a_hi[:, k, half_cols(half)],
                                       a_lo[:, k, half_cols(half)], k == 0, k == KT - 1)
                        if k == KT - 1:
                            last.then_inc(unit_ready, 1)
            pe.wait_ge(ph_ready, 1)
            for n, out in enumerate((s_ps[:, 1], gemm_ps[:].rearrange("p h n -> p (h n)"))):
                p = st["heads"] + 1 + n
                pe.wait_ge(w_lo_ready, p + 1)
                if n:
                    pe.wait_ge(unit_free, 2)
                for half in range(2):
                    for k in range(KT):
                        last = product(out[:, half_cols(half)], whi[:, p % 2, k], wlo[:, p % 2, k],
                                       a_hi[:, k, half_cols(half)], a_lo[:, k, half_cols(half)], k == 0, k == KT - 1)
                    last.then_inc(unit_ready, 1)
            with pe.Fori(0, DIFF_HEADS // 2) as i:
                for e in range(2):
                    attention(Idx(e, [(2, i)]), True, DIFF_SHARE)
            for hd in range(DIFF_HEADS, HEADS):
                attention(Idx(hd), False, FOX_SHARE if hd < HEADS - 1 else NO_SHARE)
            rest_of_layer(0)
            st = PLAN[1]
            panel(Idx(st["mix"]), a_hi, a_lo, Idx(st["x_mix"]), st["norm"])
            gk_sums(Idx(0))
            p = Idx(st["heads"])
            for j in range(4):
                panel(p + j, a_hi, a_lo)
            gla_head(Idx(0), GLA_SHARE[8], p + 4, p + 1, True)
            with pe.Fori(1, GLA_HEADS - 1) as i:
                hd = Idx(0, [(1, i)])
                gla_head(hd, GLA_SHARE[12], hd.times(6) + (st["heads"] + 2), hd.times(6) + (st["heads"] - 1), True)
            gla_head(Idx(3), GLA_SHARE[6], Idx(st["heads"] + 20), Idx(st["heads"] + 17), False)
            panel(Idx(st["heads"] + 23), a_hi, a_lo)
            rest_of_layer(1)
            norm_sums(6)

        @block.gpsimd
        def _(gp):
            steps = Chain(gp, g_step)
            gp.dma_start(gcol[:], gains).then_inc(gains_loaded, 16)
            gp.dma_start(colc[:, GSUB:GSUB + 1], g_sub).then_inc(const_loaded, 16)
            gp.dma_start(colc[0:GATE_ROWS, BF:BF + 1], b_f).then_inc(const_loaded, 16)
            gp.dma_start(colc[:, BGK:BGK + GLA_HEADS], b_gk).then_inc(const_loaded, 16)
            gp.dma_start(colc[:, GON:GON + 2], g_on).then_inc(const_loaded, 16)
            gp.dma_start(wgk_all[:], w_gk).then_inc(const_loaded, 16)
            gp.dma_start(lam_in, lam_vec.rearrange("a n -> (a n)").partition_broadcast(P)).then_inc(const_loaded, 16)
            steps.link(nc.gpsimd.memset(ident[:], 0.0))
            steps.link(nc.gpsimd.affine_select(out=ident[:], in_=ident[:], compare_op=ALU.not_equal, fill=1.0,
                                               base=0, pattern=[[-1, P]], channel_multiplier=1))
            steps.link(nc.gpsimd.memset(colc[:, SEL:SEL + DIFF_HEADS], 0.0))
            for row in (0, LOW_ROW):
                sel = colc[:, SEL:SEL + DIFF_HEADS]
                steps.link(nc.gpsimd.affine_select(out=sel, in_=sel, compare_op=ALU.not_equal, fill=1.0, base=-row,
                                                   pattern=[[-1, DIFF_HEADS]], channel_multiplier=1))
            steps.link(nc.gpsimd.memset(mask_f, 0.0))
            nc.gpsimd.affine_select(out=mask_f, in_=mask_f, compare_op=ALU.is_ge, fill=MASKED,
                                    base=0, pattern=[[-1, P]], channel_multiplier=1).then_inc(gp_const, 1)

            def add_squares(n, o, half):
                a = o.times(2) + (16 * n + half)
                gp.wait_ge(sq_ready, a.at(1))
                return a

            def tile_squares(n, o, first):
                for half in range(2):
                    a = add_squares(n, o, half)
                    if first:
                        if n >= 1:
                            gp.wait_ge(norm_sum, 2 * n)
                        nc.gpsimd.tensor_copy(sumsq[:, half], zs[:, half]).then_inc(sq_added, 1)
                    else:
                        gp.wait_ge(sq_added, a.at(-1))
                        nc.gpsimd.tensor_tensor(sumsq[:, half], sumsq[:, half], zs[:, half],
                                                ALU.add).then_inc(sq_added, 1)

            def all_squares(n, after=None):
                tile_squares(n, Idx(0), True)
                if after:
                    after(Idx(0))
                with gp.Fori(1, KT) as o:
                    tile_squares(n, Idx(0, [(1, o)]), False)
                    if after:
                        after(Idx(0, [(1, o)]))

            all_squares(0)
            for lv in range(LEVELS):
                half_block = 64 >> lv
                v = lmask_built[:, lv].rearrange("p (b n) -> p b n", n=2 * half_block)
                nb = P // (2 * half_block)
                steps.link(nc.gpsimd.memset(v, 1.0))
                steps.link(nc.gpsimd.memset(v[:, :, 0:half_block], 0.0))
                steps.link(nc.gpsimd.affine_select(out=v, in_=v, compare_op=ALU.is_ge, fill=0.0, base=0,
                                                   pattern=[[-2 * half_block, nb], [0, 2 * half_block]],
                                                   channel_multiplier=1))
                steps.link(nc.gpsimd.affine_select(out=v, in_=v, compare_op=ALU.is_ge, fill=0.0,
                                                   base=half_block - 1,
                                                   pattern=[[2 * half_block, nb], [0, 2 * half_block]],
                                                   channel_multiplier=-1))
            steps.link(nc.gpsimd.tensor_copy(lmask_built[:, LEVELS], ident[:]))
            gp.dma_start(m_dram, lmask_built[:].rearrange("p a n -> p (a n)")).then_inc(masks_stored, 16)
            for layer, st in enumerate(PLAN):
                if layer == 1:
                    gp.wait_ge(h_spilled, 16 * KT)
                    gp.wait_ge(x_lo_ready, st["x_mix"] + 16)
                    gp.wait_ge(masks_stored, 16)
                    gp.dma_start(lmask[:].rearrange("p a n -> p (a n)"), m_dram).then_inc(masks_loaded, 16)
                    with gp.Fori(0, GLA_HEADS) as hd:
                        gp.wait_ge(on_sq, hd + 1)
                        nc.gpsimd.tensor_tensor(dec[:], dec[:], lev[:], ALU.add).then_inc(on_added, 1)
                all_squares(st["norm"] + 1)
                all_squares(st["norm"] + 2)
                gp.wait_ge(unit_ready, 2 * st["gate"])
                gp.dma_start(p_raw[:], p_t[layer].rearrange("k p n -> p k n")).then_inc(p_loaded, 16)

                def spill(o):
                    gp.wait_ge(h_ready, o.times(2).at(2))
                    gp.dma_start(h_dram[o.cols(1)].rearrange("a p n -> p (a n)"),
                                 h[:, o.cols(1)].rearrange("p a n -> p (a n)")).then_inc(h_spilled, 16)

                all_squares(st["norm"] + 3, spill if layer == 0 else None)
            gp.wait_ge(norm_root, 2 * 7)
            for o in range(KT - FINAL_GP, KT):
                steps.link(nc.gpsimd.tensor_tensor(h[:, o], h[:, o], rstd[:], ALU.mult))
                nc.gpsimd.tensor_scalar(h[:, o], h[:, o], gcol[:, 6 * KT + o:6 * KT + o + 1], None,
                                        ALU.mult).then_inc(final_gp, 1)

        @block.scalar
        def _(act):
            steps = Chain(act, a_step)
            A = nc.scalar.activation
            eps = colc[:, EPSC:EPSC + 1]

            def w_hi(p):
                if p.at() is not None and isinstance(p.at(), int) and p.at() >= PANELS:
                    return
                act.wait_ge(w_loaded[p.parity], p.half().times(16).at(16))
                if not (isinstance(p.at(), int) and p.at() < 2):
                    act.wait_ge(unit_ready, p.times(2).at(-2))
                A(whi[:, p.parity], wraw[:, p.parity], ACT.Copy).then_inc(w_hi_ready, 1)

            def finish(n, o, half, next_hi):
                a = o.times(2) + (16 * n + half)
                src = h[:, o.cols(1), half_cols(half)].rearrange("p a n -> p (a n)")
                if not (isinstance(a.at(), int) and a.at() < 2):
                    act.wait_ge(sq_added, a.at(-1))
                A(zs[:, half], src, ACT.Square).then_inc(sq_ready, 1)
                if next_hi is not None:
                    A(next_hi[:, o.cols(1), half_cols(half)].rearrange("p a n -> p (a n)"), src, ACT.Copy,
                      scale=gcol[:, o.cols(1, add=KT * n)]).then_inc(x_hi_ready, 1)

            def norm_root_of(n):
                for half in range(2):
                    act.wait_ge(norm_sum, 2 * n + half + 1)
                    r = rstd[:, half_cols(half)]
                    A(r, s_ps[:, 0, half_cols(half)], ACT.Ln, scale=1.0 / D, bias=eps).then_inc(norm_ms, 1)
                for half in range(2):
                    act.wait_ge(norm_ms, 2 * n + half + 1)
                    r = rstd[:, half_cols(half)]
                    A(r, r, ACT.Exp, scale=-0.5).then_inc(norm_root, 1)

            def taker(share, first, work):
                taken = [0]

                def take(point):
                    for u in range(taken[0], share.complete(point)):
                        work(first + u // 2, u)
                        taken[0] += 1
                return take

            def split_qk(hd):
                act.wait_ge(unit_free, hd.times(6).at(6))
                A(q_hi[:], q_raw[:], ACT.Copy).then_inc(qk_hi_ready, 1)
                A(k_hi[:], k_raw[:], ACT.Copy).then_inc(qk_hi_ready, 1)

            def split_gates(hd):
                A(cm[0:GATE_ROWS], c_row[0:GATE_ROWS], ACT.Copy,
                  scale=colc[0:GATE_ROWS, hd.cols(1, add=SEL - DIFF_HEADS)]).then_inc(cm_hi_ready, 1)

            def split_o(src, o, halves=(0, 1)):
                for half in halves:
                    A(a_hi[:, o.cols(1), half_cols(half)].rearrange("p a n -> p (a n)"),
                      src[:, o.cols(1), half_cols(half)].rearrange("p a n -> p (a n)"),
                      ACT.Copy).then_inc(x_hi_ready, 1)

            def attention(hd, diff, share, following):
                maps = 2 if diff else 1
                last_head = share is NO_SHARE

                def next_weights(p, u):
                    if u % 2:
                        w_hi(p + 2)

                take = taker(share, hd.times(3) + (PLAN[0]["heads"] + 3), next_weights)

                def exps(i, mp):
                    n = (i + 1) * P
                    act.wait_ge(negmax_ready, task(hd, i, mp, diff).at(1))
                    pair = mp if diff else i % 2
                    c = 2 * (i % 2) + mp
                    A(prob[:, pair, 0:n], s_ps[:, pair, 0:n], ACT.Exp, bias=colc[:, NEG + c:NEG + c + 1],
                      accum_out=colc[:, L + c:L + c + 1]).then_inc(exp_ready, 1)

                for mp in range(maps):
                    exps(0, mp)
                act.wait_ge(vt_ready, hd.at(1))
                A(v_hi[:].rearrange("p a n -> p (a n)"), to_ps[:], ACT.Copy).then_inc(v_hi_ready, 1)
                if not diff:
                    A(v_t[:], o_raw[:, hd.cols(1, scale=1, add=-SUB_LAG)].rearrange("p a n -> p (a n)"),
                      ACT.Square).then_inc(sub_sq, 1)
                if last_head:
                    act.wait_ge(unit_ready, 2 * PLAN[0]["wo"])
                done = 0
                for i in range(NQT):
                    if diff:
                        n, c = (i + 1) * P, C2 + 2 * (i % 2) + 1
                        act.wait_ge(coef_ready, hd.times(NQT).at(i + 1))
                        A(prob[:, 1, 0:n], prob[:, 1, 0:n], ACT.Copy, scale=colc[:, c:c + 1]).then_inc(scaled_ready, 1)
                    if i + 1 < NQT:
                        if diff:
                            act.wait_ge(w_ready, hd.times(NQT).at(i + 1))
                        exps(i + 1, 0)
                    take(4 * i + 2)
                    if i % 2 == 0 and i >= 2:
                        act.wait_ge(pv_ready, hd.times(4).at(i // 2))
                    for g in range(GROUPS[i]):
                        n = min(4, i + 1 - 4 * g)
                        act.wait_ge(tr_ready, hd.times(GROUPS_HEAD).at(done + 1))
                        A(pt_hi[:, 4 * g:4 * g + n, (i % 2) * P:(i % 2 + 1) * P],
                          to_ps[:, 0:n * P].rearrange("p (j q) -> p j q", q=P), ACT.Copy).then_inc(tr_hi, 1)
                        done += 1
                    if diff and i + 1 < NQT:
                        exps(i + 1, 1)
                    if i == 1 and not diff:
                        act.wait_ge(sub_sum, hd.at(1 - SUB_LAG))
                        for half in range(2):
                            last = A(v_t[:, half_cols(half)], s_ps[:, half, HALF:SEQ], ACT.Ln, scale=1.0 / P, bias=eps)
                        last.then_inc(sub_ms, 1)
                        act.wait_ge(sub_ms, hd.at(1 - SUB_LAG))
                        A(v_t[:], v_t[:], ACT.Exp, scale=-0.5).then_inc(sub_root, 1)
                    take(4 * i + 5)
                    if i + 1 == NQT and following:
                        split_qk(hd + 1)
                        if not diff:
                            split_gates(hd + 1)
                    if last_head and i < KT - 1:
                        if O_ORDER[i] == DIFF_HEADS - 1:
                            act.wait_ge(sub_done, DIFF_HEADS)
                        split_o(o_raw, Idx(O_ORDER[i]))
                take(len(share.counts))
                if last_head:
                    act.wait_ge(o_evacuated, 4 * HEADS + 1)
                    split_o(o_raw, Idx(O_ORDER[KT - 1]))

            def log_sigmoid_part(x, t):
                steps.link(A(t, x, ACT.Abs))
                steps.link(A(t, t, ACT.Exp, scale=-1.0))
                return A(t, t, ACT.Ln, bias=colc[0:x.shape[0], ONE:ONE + 1])

            def gk_logs(hd):
                act.wait_ge(gk_in, hd.at(1))
                log_sigmoid_part(b_cum[:], q_dec[:]).then_inc(gk_log, 1)

            def output_gate(p, halves=(0, 1)):
                for half in halves:
                    act.wait_ge(unit_free, p.times(2).at(half + 1))
                    A(zs[:, half], zt[:, half], ACT.Sigmoid).then_inc(sig_ready, 1)

            def gla_head(hd, share, first, following):
                def unit_work(p, u):
                    if u % 2:
                        if u < GATES[share.units]:
                            output_gate(p)
                        w_hi(p + 2)

                take = taker(share, first, unit_work)
                act.wait_ge(vtok_sum, hd.at(1))
                for t in range(2):
                    last = A(v_tok[:, :, t * P:(t + 1) * P], s_ps[:, t].rearrange("p (c n) -> p c n", n=P), ACT.Copy)
                last.then_inc(vtok_ready, 1)
                for e in range(LEVELS + 2):
                    act.wait_ge(dec_in, hd.times(LEVELS + 2).at(e + 1))
                    if e == LEVELS:
                        A(dec[:], b_cum[:], ACT.Exp)
                        A(colc[:, EB:EB + NQT], b_cum[:, P - 1:SEQ:P], ACT.Exp).then_inc(dec_exp, 1)
                    else:
                        A(dec[:], dec[:], ACT.Exp).then_inc(dec_exp, 1)
                    if e < LEVELS:
                        take(1 + e)
                act.wait_ge(ktok_sum, hd.at(1))
                A(k_tok[:], to_ps[:], ACT.Copy).then_inc(ktok_ready, 1)
                for c in range(NQT):
                    take(11 + c)
                take(19)
                act.wait_ge(gla_o_free, hd.times(NQT).at(NQT))
                for t, dst in enumerate((dec, lev)):
                    last = A(dst[:], o_raw1[:, (hd.times(2) + t).cols(1)].rearrange("p a n -> p (a n)"), ACT.Square)
                last.then_inc(on_sq, 1)
                if following:
                    gk_logs(hd + 1)
                take(20)
                act.wait_ge(on_sum, hd.at(1))
                A(dec[:], s_ps[:, 0], ACT.Ln, scale=1.0 / DV, bias=eps).then_inc(on_ms, 1)
                act.wait_ge(on_ms, hd.at(1))
                A(dec[:], dec[:], ACT.Exp, scale=-0.5).then_inc(on_root, 1)
                take(len(share.counts))

            def pairs(count, body):
                with act.Fori(0, count // 2) as i:
                    for s in range(2):
                        body(Idx(s, [(2, i)]))

            def rest_of_layer(layer):
                st = PLAN[layer]
                def wo(o):
                    for half in range(2):
                        act.wait_ge(unit_free, (o + st["wo"]).times(2).at(half + 1))
                        finish(st["norm"] + 1, o, half, b_hi)
                    w_hi(o + (st["wo"] + 2))

                pairs(KT, wo)
                norm_root_of(st["norm"] + 1)

                def ff_chunk(c, last_chunk):
                    p = c.times(2 * KT) + st["mlp"]

                    def up(o):
                        for half in range(2):
                            act.wait_ge(unit_free, (p + o).times(2).at(half + 1))
                            A(zs[:, half], zt[:, half], ACT.Square)
                            A(a_hi[:, o.cols(1), half_cols(half)].rearrange("p a n -> p (a n)"), zt[:, half],
                              ACT.Square).then_inc(x_hi_ready, 1)
                        w_hi(p + (o + 2))

                    def down(o):
                        if last_chunk:
                            for half in range(2):
                                act.wait_ge(unit_free, (p + (o + KT)).times(2).at(half + 1))
                                finish(st["norm"] + 2, o, half, b_hi)
                        w_hi(p + (o + KT + 2))

                    pairs(KT, up)
                    pairs(KT, down)

                with act.Fori(0, CHUNKS - 1) as c:
                    ff_chunk(Idx(0, [(1, c)]), False)
                ff_chunk(Idx(CHUNKS - 1), True)
                act.wait_ge(p_loaded, 16 * (layer + 1))
                A(a_hi[:, 4:6], p_raw[:], ACT.Copy).then_inc(p_hi_ready, 1)
                norm_root_of(st["norm"] + 2)

                def sigmoid(p, o, half):
                    act.wait_ge(unit_free, p.times(2).at(half + 1))
                    act.wait_ge(sq_added, (o.times(2) + (16 * (st["norm"] + 3) + half)).at(-1))
                    A(zs[:, half], zt[:, half], ACT.Sigmoid).then_inc(sig_ready, 1)

                def finish_gated(o, half):
                    act.wait_ge(h_ready, o.times(2).at(16 * layer + half + 1))
                    finish(st["norm"] + 3, o, half, a_hi if layer == 0 else None)

                def gate(o):
                    p = o + (st["gate"] + 4)
                    for half in range(2):
                        sigmoid(p, o, half)
                        finish_gated(o, half)
                    w_hi(p + 2)

                w_hi(Idx(st["gate"] + 2))
                for half in range(2):
                    sigmoid(Idx(st["gate"]), Idx(0), half)
                for j in range(1, 5):
                    w_hi(Idx(st["gate"] + 2 + j))
                for half in range(2):
                    finish_gated(Idx(0), half)
                gate(Idx(1))
                with act.Fori(1, KT // 2 - 1) as i:
                    for s in range(2):
                        gate(Idx(s, [(2, i)]))
                for o in (KT - 2, KT - 1):
                    gate(Idx(o))
                norm_root_of(st["norm"] + 3)

            for o in range(1, KT, 2):
                act.dma_start(h[:, o], x_t[o]).then_inc(x_loaded[o], 16)
            w_hi(Idx(0))
            act.wait_ge(gains_loaded, 16)
            for o in range(KT):
                act.wait_ge(x_loaded[o], 16)
                for half in range(2):
                    finish(0, Idx(o), half, a_hi)
                if o == 0:
                    w_hi(Idx(1))
            act.wait_ge(gp_const, 1)
            A(ident_r[:], ident[:], ACT.Copy)
            A(mask_r[:], mask_f, ACT.Copy)
            act.wait_ge(const_ready, 1)
            A(negones_r[:], ones[0:GATE_ROWS], ACT.Copy, scale=-1.0).then_inc(ph_ready, 1)
            w_hi(Idx(2))
            norm_root_of(0)
            act.wait_ge(const_ready, 2)
            A(colc[:, LAM1:LAM1 + 2], colc[:, LAM1:LAM1 + 2], ACT.Exp).then_inc(lam_exp, 1)
            w_hi(Idx(3))
            act.wait_ge(fl_ready, 1)
            log_sigmoid_part(prob[0:GATE_ROWS, 0], prob[0:GATE_ROWS, 1]).then_inc(fl_log, 1)
            w_hi(Idx(4))
            split_qk(Idx(0))
            w_hi(Idx(5))
            act.wait_ge(fl_done, 1)
            split_gates(Idx(DIFF_HEADS))
            with act.Fori(0, DIFF_HEADS // 2) as i:
                for e in range(2):
                    attention(Idx(e, [(2, i)]), True, DIFF_SHARE, True)
            for hd in range(DIFF_HEADS, HEADS):
                attention(Idx(hd), False, FOX_SHARE if hd < HEADS - 1 else NO_SHARE, hd < HEADS - 1)
            rest_of_layer(0)
            st = PLAN[1]
            w_hi(Idx(st["mix"] + 2))
            gk_logs(Idx(0))
            for j in range(4):
                w_hi(Idx(st["heads"] + 2 + j))
            gla_head(Idx(0), GLA_SHARE[8], Idx(st["heads"] + 4), True)
            with act.Fori(1, GLA_HEADS - 1) as i:
                hd = Idx(0, [(1, i)])
                steps.enter(i, 2, 1)
                gla_head(hd, GLA_SHARE[12], hd.times(6) + (st["heads"] + 2), True)
                steps.leave(GLA_HEADS - 2, 2)
            gla_head(Idx(3), GLA_SHARE[6], Idx(st["heads"] + 20), False)
            output_gate(Idx(st["heads"] + 23), (0,))
            act.wait_ge(unit_ready, 2 * st["wo"])
            for half in range(2):
                for o in range(KT):
                    if half == 0 and o == KT - 2:
                        output_gate(Idx(st["heads"] + 23), (1,))
                    if o == KT - 1:
                        act.wait_ge(o_gated, half + 1)
                    split_o(o_raw1, Idx(o), (half,))
                if half == 0:
                    w_hi(Idx(st["heads"] + 25))
            rest_of_layer(1)

        @block.vector
        def _(dve):
            steps = Chain(dve, v_step)
            V = nc.vector

            def w_lo(p):
                if isinstance(p.at(), int) and p.at() >= PANELS:
                    return
                dve.wait_ge(w_hi_ready, p.at(1))
                V.tensor_tensor(wlo[:, p.parity], wraw[:, p.parity], whi[:, p.parity],
                                ALU.subtract).then_inc(w_lo_ready, 1)

            def tile_of(t, o, half):
                return t[:, o.cols(1), half_cols(half)].rearrange("p a n -> p (a n)")

            def split_lo(n, o, half, x, hi, lo):
                dve.wait_ge(x_hi_ready, x.at(1))
                V.scalar_tensor_tensor(tile_of(lo, o, half), tile_of(h, o, half), gcol[:, o.cols(1, add=KT * n)],
                                       tile_of(hi, o, half), ALU.mult, ALU.subtract).then_inc(x_lo_ready, 1)

            def norm_scale(n):
                dve.wait_ge(norm_root, 2 * n + 2)

            def bank(half, rows=P):
                return gemm_ps[0:rows, half]

            def evacuate_raw(hd, u, src=None):
                p = hd.times(3) + (PLAN[0]["heads"] + u // 2)
                half = u % 2
                src = bank(half) if src is None else src
                dve.wait_ge(unit_ready, p.times(2).at(half + 1))
                dst = (q_raw, k_raw, v_t)[u // 2][:, half_cols(half)]
                if u < 2:
                    V.scalar_tensor_tensor(dst, src, colc[:, hd.cols(1, add=QS)],
                                           rstd[:, half_cols(half)], ALU.mult, ALU.mult).then_inc(unit_free, 1)
                else:
                    V.tensor_tensor(dst, src, rstd[:, half_cols(half)], ALU.mult).then_inc(unit_free, 1)
                if half:
                    w_lo(p + 2)

            def split_qk(hd):
                for n, (raw, hi, lo) in enumerate(((q_raw, q_hi, q_lo), (k_raw, k_hi, k_lo))):
                    dve.wait_ge(qk_hi_ready, hd.times(2).at(n + 1))
                    V.tensor_tensor(lo[:], raw[:], hi[:], ALU.subtract).then_inc(qk_lo_ready, 1)

            def split_gates(hd):
                dve.wait_ge(cm_hi_ready, hd.at(1 - DIFF_HEADS))
                low = slice(LOW_ROW, GATE_ROWS)
                V.scalar_tensor_tensor(cm[low], c_row[low], colc[low, hd.cols(1, add=SEL - DIFF_HEADS)],
                                       cm[low], ALU.mult, ALU.subtract).then_inc(cm_lo_ready, 1)

            def split_o(src, x, o, halves=(0, 1)):
                for n, half in enumerate(halves):
                    dve.wait_ge(x_hi_ready, x.at(n + 1))
                    V.tensor_tensor(tile_of(a_lo, o, half), tile_of(src, o, half), tile_of(a_hi, o, half),
                                    ALU.subtract).then_inc(x_lo_ready, 1)

            def taker(share, work):
                taken = [0]

                def take(point):
                    for u in range(taken[0], share.complete(point)):
                        work(u)
                        taken[0] += 1
                return take

            def attention(hd, diff, share, following):
                maps = 2 if diff else 1
                last_head = share is NO_SHARE
                take = taker(share, lambda u: evacuate_raw(hd + 1, u))
                x_o = PLAN[0]["x_o"]

                def negmax(i, mp):
                    n = (i + 1) * P
                    dve.wait_ge(scores_ready, task(hd, i, mp, diff).at(1))
                    c = NEG + 2 * (i % 2) + mp
                    V.tensor_reduce(colc[:, c:c + 1], s_ps[:, mp if diff else i % 2, 0:n], AX, ALU.max,
                                    negate=True).then_inc(negmax_ready, 1)

                def evacuate(c):
                    dve.wait_ge(pv_ready, hd.times(4).at(c + 1))
                    V.tensor_copy(o_raw[:, hd.cols(1), c * 256:(c + 1) * 256].rearrange("p a n -> p (a n)"),
                                  to_ps[:, HALF:HALF + 256]).then_inc(o_evacuated, 1)

                for mp in range(maps):
                    negmax(0, mp)
                dve.wait_ge(v_hi_ready, hd.at(1))
                V.tensor_tensor(v_lo[:].rearrange("p a n -> p (a n)"), to_ps[:], v_hi[:].rearrange("p a n -> p (a n)"),
                                ALU.subtract).then_inc(v_lo_ready, 1)
                done = 0
                for i in range(NQT):
                    n, c = (i + 1) * P, 2 * (i % 2)
                    dve.wait_ge(exp_ready, task(hd, i, maps - 1, diff).at(1))
                    steps.link(V.reciprocal(colc[:, RL + c:RL + c + maps], colc[:, L + c:L + c + maps]))
                    if diff:
                        V.tensor_tensor(colc[:, C2 + c:C2 + c + 2], colc[:, RL + c:RL + c + 2],
                                        colc[:, ONE:ONE + 2], ALU.mult).then_inc(coef_ready, 1)
                    else:
                        V.tensor_scalar(prob[:, i % 2, 0:n], prob[:, i % 2, 0:n], colc[:, RL + c:RL + c + 1], None,
                                        ALU.mult).then_inc(w_ready, 1)
                    if i + 1 < NQT:
                        negmax(i + 1, 0)
                    if diff:
                        dve.wait_ge(coef_ready, hd.times(NQT).at(i + 1))
                        dve.wait_ge(scaled_ready, hd.times(NQT).at(i + 1))
                        V.scalar_tensor_tensor(prob[:, 1, 0:n], prob[:, 0, 0:n], colc[:, C2 + c:C2 + c + 1],
                                               prob[:, 1, 0:n], ALU.mult, ALU.add).then_inc(w_ready, 1)
                        if i + 1 < NQT:
                            negmax(i + 1, 1)
                    take(4 * i + 2)
                    if i % 2 == 0 and i >= 2:
                        evacuate(i // 2 - 1)
                    for g in range(GROUPS[i]):
                        n = min(4, i + 1 - 4 * g)
                        done += 1
                        dve.wait_ge(tr_hi, hd.times(GROUPS_HEAD).at(done))
                        q = slice((i % 2) * P, (i % 2 + 1) * P)
                        V.tensor_tensor(pt_lo[:, 4 * g:4 * g + n, q],
                                        to_ps[:, 0:n * P].rearrange("p (j q) -> p j q", q=P),
                                        pt_hi[:, 4 * g:4 * g + n, q], ALU.subtract).then_inc(tr_lo, 1)
                    take(4 * i + 5)
                    if i + 1 == NQT and following:
                        split_qk(hd + 1)
                        if not diff:
                            split_gates(hd + 1)
                    if not diff and i == 3:
                        dve.wait_ge(sub_root, hd.at(1 - SUB_LAG))
                        o = o_raw[:, hd.cols(1, add=-SUB_LAG)].rearrange("p a n -> p (a n)")
                        V.scalar_tensor_tensor(o, o, colc[:, GSUB:GSUB + 1], v_t[:], ALU.mult,
                                               ALU.mult).then_inc(sub_done, 1)
                    if last_head and i < KT - 1:
                        if O_ORDER[i] == DIFF_HEADS - 1:
                            dve.wait_ge(sub_done, DIFF_HEADS)
                        split_o(o_raw, Idx(x_o + 2 * i), Idx(O_ORDER[i]))
                evacuate(3)
                take(len(share.counts))
                if last_head:
                    dve.wait_ge(o_evacuated, 4 * HEADS + 1)
                    split_o(o_raw, Idx(x_o + 2 * (KT - 1)), Idx(O_ORDER[KT - 1]))

            def log_sigmoid(x, t, scale):
                steps.link(V.scalar_tensor_tensor(t, x, 0.0, t, ALU.min, ALU.subtract))
                if scale != 1.0:
                    steps.link(V.tensor_scalar(t, t, scale, None, ALU.mult))

            def gk_cumulate(hd):
                dve.wait_ge(gk_log, hd.at(1))
                log_sigmoid(b_cum[:], q_dec[:], 1.0 / 16.0)
                steps.link(V.tensor_tensor_scan(b_cum[:], resets[:], q_dec[:], 0.0, ALU.mult, ALU.add))

            def gk_start(hd):
                dve.wait_ge(gk_sum, hd.at(1))
                V.tensor_scalar(b_cum[:], to_ps[:], colc[:, hd.cols(1, add=BGK)], None, ALU.add).then_inc(gk_in, 1)

            def evacuate_vqk(p, u):
                half = u % 2
                dst = (vg_t[:, 0], vg_t[:, 1], q_t[:], k_t[:])[u // 2][:, half_cols(half)]
                dve.wait_ge(unit_ready, p.times(2).at(half + 1))
                if u // 2 == 2:
                    V.scalar_tensor_tensor(dst, bank(half), DK ** -0.5, rstd[:, half_cols(half)], ALU.mult,
                                           ALU.mult).then_inc(unit_free, 1)
                else:
                    V.tensor_tensor(dst, bank(half), rstd[:, half_cols(half)], ALU.mult).then_inc(unit_free, 1)
                if half:
                    w_lo(p + 2)

            def evacuate_gate(hd, p, u):
                t, half = u // 2, u % 2
                dve.wait_ge(unit_ready, p.times(2).at(half + 1))
                V.tensor_tensor(zt[:, half], bank(half), rstd[:, half_cols(half)], ALU.mult).then_inc(unit_free, 1)
                if half:
                    for hf in range(2):
                        o = tile_of(o_raw1, hd.times(2) + t, hf)
                        dve.wait_ge(sig_ready, hd.times(4).at(SIG_MIX1 + 2 * t + hf + 1))
                        steps.link(V.tensor_tensor(zt[:, hf], zt[:, hf], zs[:, hf], ALU.mult))
                        steps.link(V.scalar_tensor_tensor(o, o, colc[:, GON + t:GON + t + 1], zt[:, hf],
                                                          ALU.mult, ALU.mult))
                    w_lo(p + 2)

            def keep_gate(p, u):
                half = u % 2
                dve.wait_ge(unit_ready, p.times(2).at(half + 1))
                V.tensor_tensor(zt[:, half], bank(half), rstd[:, half_cols(half)], ALU.mult).then_inc(unit_free, 1)
                if half:
                    for hf in range(2):
                        dve.wait_ge(sig_ready, SIG_MIX1 + 4 * (GLA_HEADS - 1) + hf + 1)
                        last = V.tensor_tensor(gl_t[:, half_cols(hf)], zt[:, hf], zs[:, hf], ALU.mult)
                    steps.link(last)
                    w_lo(p + 2)

            def last_gates(p):
                x_o = PLAN[1]["x_o"]
                tile, gain = KT - 2, colc[:, GON:GON + 1]
                o = o_raw1[:, tile]
                steps.link(V.scalar_tensor_tensor(o, o, gain, gl_t[:], ALU.mult, ALU.mult))

                def evacuate(half):
                    dve.wait_ge(unit_ready, p.times(2).at(half + 1))
                    V.tensor_tensor(zt[:, half], bank(half), rstd[:, half_cols(half)], ALU.mult).then_inc(unit_free, 1)

                def gate(half):
                    dve.wait_ge(sig_ready, SIG_GATE1 - 2 + half + 1)
                    steps.link(V.tensor_tensor(zt[:, half], zt[:, half], zs[:, half], ALU.mult))
                    o = o_raw1[:, KT - 1, half_cols(half)]
                    V.scalar_tensor_tensor(o, o, colc[:, GON + 1:GON + 2], zt[:, half], ALU.mult,
                                           ALU.mult).then_inc(o_gated, 1)
                    dve.wait_ge(o_gated, half + 1)

                evacuate(0)
                gate(0)
                for o in range(KT):
                    if o == 4:
                        evacuate(1)
                    split_o(o_raw1, Idx(x_o + o), Idx(o), (0,))
                for o in range(KT):
                    if o == 2:
                        gate(1)
                    if o == KT - 2:
                        w_lo(p + 2)
                    split_o(o_raw1, Idx(x_o + KT + o), Idx(o), (1,))

            def gla_head(hd, share, first, following):
                gates = GATES[share.units]

                def unit_work(u):
                    p = first + u // 2
                    if u < min(gates, 4):
                        evacuate_gate(hd + (-1), p, u)
                    elif u < gates:
                        keep_gate(p, u)
                    else:
                        evacuate_vqk(p, u - gates)

                take = taker(share, unit_work)
                if following:
                    V.tensor_copy(wgk_h[:], wgk_all[:, (hd + 1).cols(DK)]).then_inc(gk_w, 1)

                def decays(lv):
                    hb = 64 >> lv
                    b = b_cum[:].rearrange("p (b n) -> p b n", n=2 * hb)
                    d = dec[:].rearrange("p (b n) -> p b n", n=2 * hb)
                    ref = b[:, :, hb - 1:hb].to_broadcast([P, SEQ // (2 * hb), hb])
                    V.tensor_tensor(d[:, :, 0:hb], ref, b[:, :, 0:hb], ALU.subtract)
                    V.tensor_tensor(d[:, :, hb:2 * hb], b[:, :, hb:2 * hb], ref, ALU.subtract).then_inc(dec_in, 1)

                def level(lv):
                    hb = 64 >> lv
                    dve.wait_ge(dec_exp, hd.times(LEVELS + 2).at(lv + 1))
                    if lv >= 1:
                        dve.wait_ge(lev_sum, hd.times(LEVELS + 1).at(lv))
                    d, t, kk, qq = (a[:].rearrange("p (b n) -> p b n", n=2 * hb) for a in (dec, lev, k_t, q_t))
                    V.tensor_tensor(t[:, :, 0:hb], d[:, :, 0:hb], kk[:, :, 0:hb], ALU.mult)
                    V.tensor_tensor(t[:, :, hb:2 * hb], d[:, :, hb:2 * hb], qq[:, :, hb:2 * hb],
                                    ALU.mult).then_inc(lev_ready, 1)
                    dve.wait_ge(lev_ready, hd.times(LEVELS).at(lv + 1))

                def place(lv):
                    dve.wait_ge(lev_sum, hd.times(LEVELS + 1).at(lv + 1))
                    if lv >= 1:
                        dve.wait_ge(lev_done, hd.times(LEVELS + 1).at(lv))
                    V.memset(colc[:, MARK + 2 + lv:MARK + 3 + lv], 0.0)
                    hb, lo = (64 >> lv, 64 >> lv) if lv < LEVELS else (P, 0)
                    shape = [P, NQT, P // (lo + hb), lo + hb]
                    split = dict(c=NQT, n=lo + hb)
                    mask = lmask[:, lv:lv + 1].bitcast(I32).to_broadcast([P, NQT, P])
                    mask = mask.rearrange("p c (b n) -> p c b n", n=lo + hb)[:, :, :, lo:]
                    V.copy_predicated(att[:].rearrange("p (c b n) -> p c b n", **split)[:, :, :, lo:], mask,
                                      s_ps[:, lv % 2].rearrange("p (c b n) -> p c b n", **split)[:, :, :, lo:]
                                      ).then_inc(lev_done, 1)

                decays(0)
                for lv in range(LEVELS):
                    level(lv)
                    if lv + 1 < LEVELS:
                        decays(lv + 1)
                    else:
                        V.memset(colc[:, MARK + 1:MARK + 2], 0.0).then_inc(dec_in, 1)
                    if lv >= 1:
                        place(lv - 1)
                    take(1 + lv)
                place(LEVELS - 1)
                dve.wait_ge(dec_exp, hd.times(LEVELS + 2).at(LEVELS + 1))
                steps.link(V.tensor_tensor(q_dec[:], q_t[:], dec[:], ALU.mult))
                b = b_cum[:].rearrange("p (c n) -> p c n", n=P)
                V.tensor_tensor(dec[:].rearrange("p (c n) -> p c n", n=P),
                                b[:, :, P - 1:P].to_broadcast([P, NQT, P]), b, ALU.subtract).then_inc(dec_in, 1)
                dve.wait_ge(dec_exp, hd.times(LEVELS + 2).at(LEVELS + 2))
                V.tensor_tensor(k_dec[:], k_t[:], dec[:], ALU.mult).then_inc(ktok_in, 1)
                place(LEVELS)
                for c in range(NQT):
                    take(11 + c)
                    if c < NQT - 1:
                        dve.wait_ge(st_sum, hd.times(NQT - 1).at(c + 1))
                        if c == 0:
                            V.tensor_copy(state_c(0), to_ps[:, 0:DV]).then_inc(st_ready, 1)
                        else:
                            V.scalar_tensor_tensor(state_c(c), state_c(c - 1), colc[:, EB + c:EB + c + 1],
                                                   to_ps[:, 0:DV], ALU.mult, ALU.add).then_inc(st_ready, 1)
                        dve.wait_ge(st_ready, hd.times(NQT - 1).at(c + 1))
                    dve.wait_ge(gla_o, hd.times(NQT).at(c + 1))
                    V.tensor_copy(o_raw1[:, hd.times(2).cols(2, scale=1), c * P:(c + 1) * P],
                                  s_ps[:, c % 2, 0:DV].rearrange("p (t n) -> p t n", n=P)).then_inc(gla_o_free, 1)
                take(19)
                if following:
                    gk_start(hd + 1)
                take(20)
                if following:
                    gk_cumulate(hd + 1)
                dve.wait_ge(on_root, hd.at(1))
                for t in range(2):
                    o = o_raw1[:, (hd.times(2) + t).cols(1)].rearrange("p a n -> p (a n)")
                    last = V.tensor_tensor(o, o, dec[:], ALU.mult)
                steps.link(last)
                take(len(share.counts))

            def pairs(count, body, links=0):
                with dve.Fori(0, count // 2) as i:
                    steps.enter(i, links)
                    for s in range(2):
                        body(Idx(s, [(2, i)]))
                    steps.leave(count // 2, links)

            def rest_of_layer(layer):
                st = PLAN[layer]
                def wo(o):
                    for half in range(2):
                        u = (o + st["wo"]).times(2) + half
                        if half == 0:
                            dve.wait_ge(h_loaded[o.parity], (o.half() + 4 * layer).times(16).at(16))
                        dve.wait_ge(unit_ready, u.at(1))
                        V.tensor_tensor(tile_of(h, o, half), bank(half), tile_of(h, o, half),
                                        ALU.add).then_inc(unit_free, 1)
                        split_lo(st["norm"] + 1, o, half, o.times(2) + (st["x_mlp"] + half), b_hi, b_lo)
                    w_lo(o + (st["wo"] + 2))

                pairs(KT, wo)
                norm_scale(st["norm"] + 1)

                def ff_chunk(c, last_chunk):
                    p = c.times(2 * KT) + st["mlp"]
                    x = c.times(16) + st["x_hid"]

                    def up(o):
                        for half in range(2):
                            dve.wait_ge(unit_ready, (p + o).times(2).at(half + 1))
                            V.scalar_tensor_tensor(zt[:, half], bank(half), 0.0, rstd[:, half_cols(half)], ALU.max,
                                                   ALU.mult).then_inc(unit_free, 1)
                            dve.wait_ge(x_hi_ready, (x + o.times(2)).at(half + 1))
                            V.tensor_tensor(tile_of(a_lo, o, half), zs[:, half], tile_of(a_hi, o, half),
                                            ALU.subtract).then_inc(x_lo_ready, 1)
                        w_lo(p + (o + 2))

                    def down(o):
                        for half in range(2):
                            dve.wait_ge(unit_ready, (p + (o + KT)).times(2).at(half + 1))
                            V.tensor_tensor(tile_of(h, o, half), bank(half), tile_of(h, o, half),
                                            ALU.add).then_inc(unit_free, 1)
                            if last_chunk:
                                split_lo(st["norm"] + 2, o, half, o.times(2) + (st["x_ple"] + half), b_hi, b_lo)
                        w_lo(p + (o + KT + 2))

                    pairs(KT, up)
                    pairs(KT, down)

                with dve.Fori(0, CHUNKS - 1) as c:
                    ff_chunk(Idx(0, [(1, c)]), False)
                ff_chunk(Idx(CHUNKS - 1), True)
                n = st["norm"] + 3
                dve.wait_ge(p_hi_ready, layer + 1)
                V.tensor_tensor(a_hi[:, 6:8], p_raw[:], a_hi[:, 4:6], ALU.subtract).then_inc(p_lo_ready, 1)
                norm_scale(n - 1)

                def gate_in(p, half):
                    dve.wait_ge(unit_ready, p.times(2).at(half + 1))
                    V.tensor_tensor(zt[:, half], bank(half), rstd[:, half_cols(half)], ALU.mult).then_inc(unit_free, 1)

                def gate_out(o, half):
                    g = o.times(2) + half
                    dve.wait_ge(sig_ready, g.at((0 if layer == 0 else SIG_GATE1) + 1))
                    steps.link(V.tensor_tensor(zt[:, half], zs[:, half], tile_of(pp, o, half), ALU.mult))
                    V.tensor_tensor(tile_of(h, o, half), tile_of(h, o, half), zt[:, half], ALU.add).then_inc(h_ready, 1)

                def next_lo(o, half):
                    if layer == 0:
                        split_lo(n, o, half, o.times(2) + (PLAN[1]["x_mix"] + half), a_hi, a_lo)

                def gate(o):
                    p = o + (st["gate"] + 4)
                    for half in range(2):
                        gate_in(p, half)
                        if half == 0:
                            next_lo(o + (-1), 1)
                        else:
                            next_lo(o, 0)
                        gate_out(o, half)
                    w_lo(p + 2)

                for half in range(2):
                    gate_in(Idx(st["gate"]), half)
                w_lo(Idx(st["gate"] + 2))
                for j in range(4):
                    for e in range(2):
                        o = 4 * (j % 2) + 2 * e
                        dve.wait_ge(unit_ready, 2 * (st["ple"] + j) + e + 1)
                        V.tensor_copy(pp[:, o:o + 2, half_cols(j // 2)],
                                      s_ps[:, 1 - e].rearrange("p (a n) -> p a n", n=HALF)).then_inc(unit_free, 1)
                    w_lo(Idx(st["ple"] + j + 2))
                for half in range(2):
                    gate_out(Idx(0), half)
                    if half == 1:
                        next_lo(Idx(0), 0)
                gate(Idx(1))
                with dve.Fori(1, KT // 2 - 1) as i:
                    steps.enter(i, 4, 1)
                    for s in range(2):
                        gate(Idx(s, [(2, i)]))
                    steps.leave(KT // 2 - 2, 4)
                for o in (KT - 2, KT - 1):
                    gate(Idx(o))
                next_lo(Idx(KT - 1), 1)

            V.memset(ones[:], 1.0).then_inc(const_ready, 1)
            V.memset(colc[:, QS:QS + DIFF_HEADS], 64 ** -0.5).then_inc(o_evacuated, 1)
            V.memset(colc[:, QS + DIFF_HEADS:QS + HEADS], 128 ** -0.5)
            V.memset(colc[:, EPSC:EPSC + 1], EPS)
            steps.link(V.memset(colc[:, ONE:ONE + 1], 1.0))
            dve.wait_ge(gains_loaded, 16)
            w_lo(Idx(0))
            for o in range(KT):
                for half in range(2):
                    split_lo(0, Idx(o), half, Idx(2 * o + half), a_hi, a_lo)
                if o == 0:
                    w_lo(Idx(1))
            dve.wait_ge(const_loaded, 16 * 6)
            for t in range(2):
                steps.link(V.tensor_tensor(k_raw[:, 256 + t * 64:256 + (t + 1) * 64], lam_in[:, 2 * t * 64:(2 * t + 1) * 64],
                                           lam_in[:, (2 * t + 1) * 64:(2 * t + 2) * 64], ALU.mult))
            V.tensor_reduce(colc[:, LAM1:LAM1 + 2], k_raw[:, 256:384].rearrange("p (t n) -> p t n", t=2), AX,
                            ALU.add).then_inc(const_ready, 1)
            w_lo(Idx(2))
            norm_scale(0)
            F = GATE_ROWS
            for half in range(2):
                dve.wait_ge(unit_ready, half + 1)
                V.tensor_tensor(prob[0:F, 0, half_cols(half)], bank(half, F), rstd[0:F, half_cols(half)],
                                ALU.mult).then_inc(unit_free, 1)
            for u in range(2):
                evacuate_raw(Idx(0), u, to_ps[:, half_cols(u)])
            dve.wait_ge(unit_free, 2)
            V.tensor_scalar(prob[0:F, 0], prob[0:F, 0], colc[0:F, BF:BF + 1], None, ALU.add).then_inc(fl_ready, 1)
            dve.wait_ge(lam_exp, 1)
            steps.link(V.tensor_tensor(colc[:, NEGLAM:NEGLAM + 1], colc[:, LAM2:LAM2 + 1], colc[:, LAM1:LAM1 + 1],
                                       ALU.subtract))
            steps.link(V.tensor_scalar(colc[:, NEGLAM:NEGLAM + 1], colc[:, NEGLAM:NEGLAM + 1], LAM_INIT, None,
                                       ALU.subtract))
            steps.link(V.tensor_scalar(colc[:, GSUB:GSUB + 1], colc[:, GSUB:GSUB + 1], 1.0 - LAM_INIT, None, ALU.mult))
            dve.wait_ge(fl_log, 1)
            log_sigmoid(prob[0:F, 0], prob[0:F, 1], 1.0)
            steps.link(V.memset(prob[0:F, 0], 1.0))
            V.tensor_tensor_scan(c_row[0:F], prob[0:F, 0], prob[0:F, 1], 0.0, ALU.mult,
                                 ALU.add).then_inc(fl_done, 1)
            for u in range(2, 4):
                evacuate_raw(Idx(0), u, s_ps[:, 1, half_cols(u % 2)])
            split_qk(Idx(0))
            for u in range(4, 6):
                evacuate_raw(Idx(0), u)
            split_gates(Idx(DIFF_HEADS))
            with dve.Fori(0, DIFF_HEADS // 2) as i:
                links = 2 * NQT
                steps.enter(i, links)
                for e in range(2):
                    attention(Idx(e, [(2, i)]), True, DIFF_SHARE, True)
                steps.leave(DIFF_HEADS // 2, links)
            dve.wait_ge(masks_stored, 16)
            for hd in range(DIFF_HEADS, HEADS):
                attention(Idx(hd), False, FOX_SHARE if hd < HEADS - 1 else NO_SHARE, hd < HEADS - 1)
            rest_of_layer(0)
            st = PLAN[1]
            norm_scale(st["norm"])
            for half in range(2):
                dve.wait_ge(unit_ready, 2 * st["mix"] + half + 1)
                V.tensor_tensor(gl_t[0:LOWRANK, half_cols(half)], bank(half, LOWRANK), rstd[0:LOWRANK, half_cols(half)],
                                ALU.mult).then_inc(unit_free, 1)
            V.tensor_copy(wgk_h[:], wgk_all[:, 0:DK]).then_inc(gk_w, 1)
            w_lo(Idx(st["mix"] + 2))
            V.memset(att[:], 0.0)
            steps.link(V.memset(resets[:], 1.0))
            steps.link(V.memset(resets[:, 0:SEQ:P], 0.0))
            dve.wait_ge(h_spilled, 16 * KT)
            gk_start(Idx(0))
            gk_cumulate(Idx(0))
            p = Idx(st["heads"])
            for u in range(8):
                evacuate_vqk(p + u // 2, u)
            dve.wait_ge(masks_loaded, 16)
            gla_head(Idx(0), GLA_SHARE[8], p + 4, True)
            with dve.Fori(1, GLA_HEADS - 1) as i:
                hd = Idx(0, [(1, i)])
                links = 2 + 1 + 1 + 1 + 8
                steps.enter(i, links, 1)
                gla_head(hd, GLA_SHARE[12], hd.times(6) + (st["heads"] + 2), True)
                steps.leave(GLA_HEADS - 2, links)
            gla_head(Idx(3), GLA_SHARE[6], p + 20, False)
            last_gates(p + 23)
            rest_of_layer(1)
            norm_scale(6)
            for o in range(KT - FINAL_GP):
                V.scalar_tensor_tensor(h[:, o], h[:, o], gcol[:, 6 * KT + o:6 * KT + o + 1], rstd[:], ALU.mult,
                                       ALU.mult).then_inc(final_ready, 1)


def kernel(**inputs):
    import numpy as np
    import concourse.bacc as bacc
    from concourse.bass_utils import run_bass_kernel_spmd

    a = {k: np.asarray(v) for k, v in inputs.items()}

    def panel(w):
        k, n = w.shape
        return w.reshape(k // P, P, n // P, P).transpose(2, 1, 0, 3).reshape(n // P, P, -1)

    def padded(w):
        return np.concatenate([w, np.zeros((w.shape[0], P - w.shape[1]), w.dtype)], axis=1)

    def twice(w):
        return np.concatenate([w, np.zeros((w.shape[0], LOW_ROW - w.shape[1]), w.dtype), w], axis=1)

    def layer_tail(w_o, i):
        up, down = a["w_up"][i], a["w_down"][i]
        parts = [panel(w_o)]
        for c in range(CHUNKS):
            parts += [panel(up[:, c * D:(c + 1) * D]), panel(down[c * D:(c + 1) * D])]
        proj = a["w_ple_proj"][i].reshape(2, P, 2, HALF).transpose(2, 1, 0, 3).reshape(2, P, -1)
        gate = panel(a["w_ple_gate"][i])
        return parts + [gate[:1], proj, proj, gate[1:]]

    even, odd = a["even_w_in"][0], a["odd_w_in"][0]
    W = DIFF_HEADS * P
    cols = lambda w, c: panel(w[:, c:c + P])
    stream = [panel(padded(twice(even[:, 6 * W:])))]
    for hd in range(HEADS):
        base = (hd // DIFF_HEADS) * 3 * W + (hd % DIFF_HEADS) * P
        stream += [cols(even, base), cols(even, base + W), cols(even, base + 2 * W)]
    stream += layer_tail(a["even_w_o"][0], 0)
    stream += [panel(padded(odd[:, 6 * W:]))]

    def vqk(hd):
        v = 2 * W + hd * DV
        return [cols(odd, v), cols(odd, v + P), cols(odd, hd * DK), cols(odd, W + hd * DK)]

    def gate(hd):
        g = 4 * W + hd * DV
        return [cols(odd, g), cols(odd, g + P)]

    stream += vqk(0) + vqk(1) + gate(0) + vqk(2) + gate(1) + vqk(3) + gate(2) + gate(3)
    stream += layer_tail(a["odd_w_o"][0], 1)
    gains = [g for i in range(2) for g in (a["norm_mix"][i], a["norm_mlp"][i], a["norm_ple"][i])]
    arrays = {
        "x_t": a["x"][0].T.reshape(KT, P, SEQ),
        "p_t": a["p"][:, 0].transpose(0, 2, 1).reshape(2, 2, P, SEQ),
        "panels": np.concatenate(stream),
        "gains": np.stack(gains + [a["norm_final"]]).reshape(7 * KT, P).T,
        "b_f": twice(a["even_b_f"].reshape(1, DIFF_HEADS)).T,
        "lam_vec": np.concatenate([a["lam_q1"], a["lam_k1"], a["lam_q2"], a["lam_k2"]]),
        "g_sub": a["diff_subln"].reshape(P, 1),
        "w_gk": a["odd_w_gk"][0],
        "b_gk": a["odd_b_gk"].reshape(GLA_HEADS, DK).T,
        "g_on": a["gla_onorm"].reshape(2, P).T,
    }
    arrays = {k: np.ascontiguousarray(v) for k, v in arrays.items()}
    assert arrays["panels"].shape == (PANELS, P, D)
    nc = bacc.Bacc("TRN2", target_bir_lowering=False, num_devices=1)
    args = [nc.dram_tensor(k, v.shape, mybir.dt.from_np(v.dtype), kind="ExternalInput").ap()
            for k, v in arrays.items()]
    args.append(nc.dram_tensor("out_t", [KT, P, SEQ], F32, kind="ExternalOutput").ap())
    build_trunk(nc, *args)
    r = run_bass_kernel_spmd(nc, [arrays], core_ids=[0])
    got = r.results[0]["out_t"]
    return np.ascontiguousarray(got.reshape(D, SEQ).T).reshape(1, SEQ, D)
```
